# Optimizing a Trainium2 kernel written in Bass

```python
import jax, jax.numpy as jnp
from jax import lax
import numpy as np
import math
import jax
import jax.numpy as jnp

D_MODEL = 1024
BATCH = 1
SEQ = 512
DEPTH = 1

N_META = 16
BLOCK = 128
LEAD = BLOCK
FOX_HD = 64
FOX_HEADS = D_MODEL // FOX_HD
FOX_W = FOX_HEADS * FOX_HD
RET_HEADS = 4
RET_DK = D_MODEL // (2 * RET_HEADS)
RET_DV = 2 * RET_DK
RET_QK = RET_HEADS * RET_DK
RET_V = RET_HEADS * RET_DV
D_FF = ((8 * D_MODEL // 3 + 127) // 128) * 128
IN_SIZES = (FOX_W, FOX_W, FOX_W, FOX_HEADS, RET_QK, RET_QK, RET_V, RET_V, D_MODEL, D_MODEL)
N_IN = sum(IN_SIZES)
IN_SPLITS = [int(s) for s in np.cumsum(IN_SIZES)[:-1]]
EPS = 1e-6
GN_EPS = 1e-5
ROPE_BASE = 10000.0
FORGET_BIAS_INIT = 3.0
NEG = -1e30


def rmsnorm(x, g):
    xf = x.astype(jnp.float32)
    y = xf * lax.rsqrt(jnp.mean(xf * xf, axis=-1, keepdims=True) + EPS)
    return (y * g.astype(jnp.float32)).astype(x.dtype)

def swiglu(x, w_in, w_out):
    a, b = jnp.split(x @ w_in, 2, axis=-1)
    return (jax.nn.silu(a) * b) @ w_out

def rotary(x, pos):
    half = x.shape[-1] // 2
    inv = ROPE_BASE ** (-jnp.arange(half, dtype=jnp.float32) / half)
    ang = pos[:, None] * inv[None, :]
    cos, sin = jnp.cos(ang)[None, :, None, :], jnp.sin(ang)[None, :, None, :]
    xf = x.astype(jnp.float32)
    x1, x2 = xf[..., :half], xf[..., half:]
    return jnp.concatenate([x1 * cos - x2 * sin, x2 * cos + x1 * sin], axis=-1)

def forgetting_attention(q, k, v, logf, valid):
    B, H, P, hd = q.shape
    nb = P // BLOCK
    c = jnp.cumsum(logf, axis=-1)
    kpos = jnp.arange(P)
    scale = hd ** -0.5

    def block(i):
        s0 = i * BLOCK
        qb = lax.dynamic_slice_in_dim(q, s0, BLOCK, axis=2)
        cb = lax.dynamic_slice_in_dim(c, s0, BLOCK, axis=2)
        logits = jnp.einsum('bhqd,bhkd->bhqk', qb, k) * scale + cb[..., None] - c[:, :, None, :]
        qpos = s0 + jnp.arange(BLOCK)
        allowed = (kpos[None, :] <= qpos[:, None]) & (valid[None, :] | (kpos[None, :] == qpos[:, None]))
        p = jax.nn.softmax(jnp.where(allowed[None, None], logits, NEG), axis=-1)
        return jnp.einsum('bhqk,bhkd->bhqd', p, v)

    out = lax.map(block, jnp.arange(nb))
    return out.transpose(1, 2, 0, 3, 4).reshape(B, H, P, hd)

def retention(q, k, v, log_gamma):
    B, H, P, dk = q.shape
    dv = v.shape[-1]
    nc = P // BLOCK
    qc = q.reshape(B, H, nc, BLOCK, dk)
    kc = k.reshape(B, H, nc, BLOCK, dk)
    vc = v.reshape(B, H, nc, BLOCK, dv)
    n = jnp.arange(BLOCK, dtype=jnp.float32)
    diff = n[:, None] - n[None, :]
    lg = log_gamma[:, None, None]
    decay = jnp.where(diff >= 0, jnp.exp(lg * jnp.maximum(diff, 0.0)), 0.0)
    scores = jnp.einsum('bhcnd,bhcmd->bhcnm', qc, kc) * decay[None, :, None]
    out = jnp.einsum('bhcnm,bhcme->bhcne', scores, vc)
    zeta = jnp.exp(log_gamma[:, None] * (BLOCK - 1 - n)[None, :])
    kv = jnp.einsum('bhcmd,bhcme->cbhde', kc * zeta[None, :, None, :, None], vc)
    chunk_decay = jnp.exp(log_gamma * BLOCK)[None, :, None, None]

    def step(R, kv_c):
        return chunk_decay * R + kv_c, R

    _, r_prev = lax.scan(step, jnp.zeros((B, H, dk, dv), jnp.float32), kv)
    xi = jnp.exp(log_gamma[:, None] * (n + 1.0)[None, :])
    out = out + jnp.einsum('bhcnd,cbhde->bhcne', qc * xi[None, :, None, :, None], r_prev)
    return out.reshape(B, H, P, dv)

def head_groupnorm(y, g):
    mu = jnp.mean(y, axis=-1, keepdims=True)
    var = jnp.mean(jnp.square(y - mu), axis=-1, keepdims=True)
    yn = (y - mu) * lax.rsqrt(var + GN_EPS)
    B, H, P, dv = y.shape
    return yn.transpose(0, 2, 1, 3).reshape(B, P, H * dv) * g.astype(jnp.float32)

def hybrid_layer(h, valid, pos, log_gamma, norm_ffn1, w_ffn1_in, w_ffn1_out, norm_mix, w_in,
                 b_forget, b_gate, fox_q_norm, fox_k_norm, w_o_fox, ret_gn, w_o_ret, w_out,
                 norm_ffn2, w_ffn2_in, w_ffn2_out):
    dt = h.dtype
    B, P, _ = h.shape
    h = h + 0.5 * swiglu(rmsnorm(h, norm_ffn1), w_ffn1_in, w_ffn1_out)
    u = rmsnorm(h, norm_mix)
    fq, fk, fv, ff, rq, rk, rv, rg, ga, gb = jnp.split(u @ w_in, IN_SPLITS, axis=-1)
    vmask = valid[None, :, None, None].astype(jnp.float32)

    def fox_heads(t):
        return t.reshape(B, P, FOX_HEADS, FOX_HD)
    q_a = rmsnorm(fox_heads(fq), fox_q_norm).astype(jnp.float32).transpose(0, 2, 1, 3)
    k_a = rmsnorm(fox_heads(fk), fox_k_norm).astype(jnp.float32).transpose(0, 2, 1, 3)
    v_a = fox_heads(fv).astype(jnp.float32).transpose(0, 2, 1, 3)
    logf = jax.nn.log_sigmoid(ff.astype(jnp.float32) + b_forget.astype(jnp.float32))
    logf = jnp.where(valid[None, :, None], logf, 0.0).transpose(0, 2, 1)
    y_a = forgetting_attention(q_a, k_a, v_a, logf, valid)
    y_a = y_a.transpose(0, 2, 1, 3).reshape(B, P, FOX_W).astype(dt)

    q_b = rotary(rq.reshape(B, P, RET_HEADS, RET_DK), pos).transpose(0, 2, 1, 3)
    k_b = (rotary(rk.reshape(B, P, RET_HEADS, RET_DK), pos) * (RET_DK ** -0.5) * vmask).transpose(0, 2, 1, 3)
    v_b = (rv.reshape(B, P, RET_HEADS, RET_DV).astype(jnp.float32) * vmask).transpose(0, 2, 1, 3)
    y_b = head_groupnorm(retention(q_b, k_b, v_b, log_gamma), ret_gn)
    y_b = (jax.nn.silu(rg.astype(jnp.float32)) * y_b).astype(dt)

    g_a = jax.nn.sigmoid(ga + b_gate[:D_MODEL])
    g_b = jax.nn.sigmoid(gb + b_gate[D_MODEL:])
    mixed = g_a * (y_a @ w_o_fox) + g_b * (y_b @ w_o_ret)
    h = h + mixed @ w_out

    h = h + 0.5 * swiglu(rmsnorm(h, norm_ffn2), w_ffn2_in, w_ffn2_out)
    return h

def first_inputs(seed: int = 0) -> dict:
    key = jax.random.key(seed)
    ks = jax.random.split(key, 20)
    f32 = jnp.float32

    def w(k, shape, fan_in):
        return jax.random.normal(k, shape, f32) * fan_in ** -0.5

    def gain(k, shape):
        return 1.0 + 0.01 * jax.random.normal(k, shape, f32)

    L = DEPTH
    return {
        "x": jax.random.normal(ks[0], (BATCH, SEQ, D_MODEL), f32),
        "meta_tokens": jax.random.normal(ks[1], (N_META, D_MODEL), f32),
        "norm_ffn1": gain(ks[2], (L, D_MODEL)),
        "w_ffn1_in": w(ks[3], (L, D_MODEL, 2 * D_FF), D_MODEL),
        "w_ffn1_out": w(ks[4], (L, D_FF, D_MODEL), D_FF),
        "norm_mix": gain(ks[5], (L, D_MODEL)),
        "w_in": w(ks[6], (L, D_MODEL, N_IN), D_MODEL),
        "b_forget": FORGET_BIAS_INIT + 0.1 * jax.random.normal(ks[7], (L, FOX_HEADS), f32),
        "b_gate": 0.01 * jax.random.normal(ks[8], (L, 2 * D_MODEL), f32),
        "fox_q_norm": gain(ks[9], (L, FOX_HD)),
        "fox_k_norm": gain(ks[10], (L, FOX_HD)),
        "w_o_fox": w(ks[11], (L, FOX_W, D_MODEL), FOX_W),
        "ret_gn": gain(ks[12], (L, RET_V)),
        "w_o_ret": w(ks[13], (L, RET_V, D_MODEL), RET_V),
        "w_out": w(ks[14], (L, D_MODEL, D_MODEL), D_MODEL),
        "norm_ffn2": gain(ks[15], (L, D_MODEL)),
        "w_ffn2_in": w(ks[16], (L, D_MODEL, 2 * D_FF), D_MODEL),
        "w_ffn2_out": w(ks[17], (L, D_FF, D_MODEL), D_FF),
    }

def first_block(x, meta_tokens, norm_ffn1, w_ffn1_in, w_ffn1_out, norm_mix, w_in, b_forget, b_gate,
              fox_q_norm, fox_k_norm, w_o_fox, ret_gn, w_o_ret, w_out, norm_ffn2, w_ffn2_in,
              w_ffn2_out):
    B, S, D = x.shape
    n_empty = LEAD - N_META
    h = jnp.concatenate([
        jnp.zeros((B, n_empty, D), x.dtype),
        jnp.broadcast_to(meta_tokens.astype(x.dtype)[None], (B, N_META, D)),
        x], axis=1)
    P = h.shape[1]
    idx = jnp.arange(P)
    valid = idx >= n_empty
    pos = (idx - n_empty).astype(jnp.float32)
    log_gamma = jnp.log1p(-jnp.exp2(-5.0 - jnp.arange(RET_HEADS, dtype=jnp.float32)))
    for l in range(DEPTH):
        h = hybrid_layer(h, valid, pos, log_gamma, norm_ffn1[l], w_ffn1_in[l], w_ffn1_out[l],
                         norm_mix[l], w_in[l], b_forget[l], b_gate[l], fox_q_norm[l], fox_k_norm[l],
                         w_o_fox[l], ret_gn[l], w_o_ret[l], w_out[l], norm_ffn2[l], w_ffn2_in[l],
                         w_ffn2_out[l])
    return h[:, LEAD:]


_first_inputs = first_inputs


def first_inputs(seed=0):
    import zlib

    import numpy as np

    out = dict(_first_inputs(seed))
    spreads = {}
    factors = {'norm_ffn1': 8.0,
     'norm_mix': 7.94,
     'b_forget': 7.146,
     'b_gate': 8.0,
     'fox_q_norm': 8.0,
     'fox_k_norm': 8.0,
     'ret_gn': 8.0,
     'norm_ffn2': 8.0}
    for name, (base, spread) in spreads.items():
        noise = np.random.default_rng([zlib.crc32(name.encode()), seed]).standard_normal(out[name].shape)
        drawn = base * np.exp(spread * noise) if base else spread * noise
        out[name] = __import__('jax').numpy.asarray(drawn.astype(out[name].dtype))
    for name, factor in factors.items():
        out[name] = (out[name] * factor).astype(out[name].dtype)
    return out


_narrow_inputs = first_inputs


def first_inputs(seed=0):

    out = dict(_narrow_inputs(seed))
    wider = {'b_forget': 8.53,
     'b_gate': 6.56,
     'fox_q_norm': 5.1,
     'fox_k_norm': 5.23,
     'ret_gn': 7.32,
     'norm_ffn2': 8.86}
    for name, times in wider.items():
        mean = out[name].mean()
        out[name] = (mean + times * (out[name] - mean)).astype(out[name].dtype)
    return out


DEPTH_2 = 2

GRID_W = 64
CTX_LEN = 256
HEAD_DIM = 64
NA_HEADS = 6
NA_WIN_R = 8
NA_WIN_C = 16
SG_GROUPS = 4
SG_CHUNK = 128
GQA_Q_HEADS = 6
GQA_KV_HEADS = 2
Q_BLOCK = 128
ROPE_THETA = 10000.0

D_A = NA_HEADS * HEAD_DIM
D_B = SG_GROUPS * HEAD_DIM
D_C = GQA_Q_HEADS * HEAD_DIM
D_MIX = D_A + D_B + D_C
D_KV_C = GQA_KV_HEADS * HEAD_DIM
IN_SIZES_2 = (D_A, D_A, D_A, 2 * D_B, D_C, D_KV_C, D_KV_C)
D_IN = 3 * D_A + 2 * D_B + D_C + 2 * D_KV_C
D_FF_2 = int(math.ceil(8 * D_MODEL / 3 / 256)) * 256
N_MOD = 6
ALPHA = (2 * DEPTH_2) ** 0.25
BETA = (8 * DEPTH_2) ** -0.25
LN_EPS = 1e-6


def layer_norm(x):
    xf = x.astype(jnp.float32)
    mu = jnp.mean(xf, -1, keepdims=True)
    var = jnp.mean(jnp.square(xf - mu), -1, keepdims=True)
    return ((xf - mu) * lax.rsqrt(var + LN_EPS)).astype(x.dtype)

def rms_norm(x, g):
    xf = x.astype(jnp.float32)
    y = xf * lax.rsqrt(jnp.mean(xf * xf, -1, keepdims=True) + LN_EPS)
    return y.astype(x.dtype) * g

def modulate(x, shift, scale):
    return layer_norm(x) * (1 + scale) + shift

def split_cols(p, sizes):
    out, off = [], 0
    for s in sizes:
        out.append(p[..., off:off + s])
        off += s
    return out

def heads(t, n):
    return t.reshape(t.shape[0], t.shape[1], n, HEAD_DIM)

def axial_rope_tables(n_tokens, dtype):
    t = jnp.arange(n_tokens, dtype=jnp.int32)
    row = (t // GRID_W).astype(jnp.float32)
    col = (t % GRID_W).astype(jnp.float32)
    n_freq = HEAD_DIM // 4
    inv = 1.0 / (ROPE_THETA ** (jnp.arange(n_freq, dtype=jnp.float32) / n_freq))
    ang = jnp.stack([row[:, None] * inv, col[:, None] * inv], axis=1)
    return jnp.cos(ang).astype(dtype), jnp.sin(ang).astype(dtype)

def apply_axial_rope(x, cos, sin):
    n_freq = HEAD_DIM // 4
    xr = x.reshape(*x.shape[:-1], 2, 2, n_freq)
    x1, x2 = xr[..., 0, :], xr[..., 1, :]
    c, s = cos[:, None], sin[:, None]
    out = jnp.stack([x1 * c - x2 * s, x2 * c + x1 * s], axis=-2)
    return out.reshape(x.shape)

def attend(q, k, v):
    scale = q.shape[-1] ** -0.5
    s = jnp.einsum('bqkgd,bskd->bkgqs', q, k) * scale
    p = jax.nn.softmax(s.astype(jnp.float32), axis=-1).astype(v.dtype)
    return jnp.einsum('bkgqs,bskd->bqkgd', p, v)

def neighbourhood_attention(q, k, v, k_ctx, v_ctx, rpb):
    B, S, H, Dh = q.shape
    rows = S // GRID_W
    kr = min(NA_WIN_R, rows)
    kcw = NA_WIN_C
    scale = Dh ** -0.5
    qg = q.reshape(B, rows, GRID_W, H, Dh)
    kg = k.reshape(B, rows, GRID_W, H, Dh)
    vg = v.reshape(B, rows, GRID_W, H, Dh)
    r_idx = jnp.arange(rows, dtype=jnp.int32)
    row_start = jnp.clip(r_idx - kr // 2, 0, rows - kr)
    c_idx = jnp.arange(GRID_W, dtype=jnp.int32)
    col_start = jnp.clip(c_idx - kcw // 2, 0, GRID_W - kcw)
    col_win = col_start[:, None] + jnp.arange(kcw, dtype=jnp.int32)[None, :]
    dc = col_win - c_idx[:, None] + (NA_WIN_C - 1)
    n_loc = kr * kcw

    def one_row(args):
        q_row, rs, r = args
        k_rows = lax.dynamic_slice_in_dim(kg, rs, kr, axis=1)
        v_rows = lax.dynamic_slice_in_dim(vg, rs, kr, axis=1)
        k_win = k_rows[:, :, col_win]
        v_win = v_rows[:, :, col_win]
        s_loc = jnp.einsum('bqhd,brqchd->bhqrc', q_row, k_win) * scale
        dr = rs + jnp.arange(kr, dtype=jnp.int32) - r + (NA_WIN_R - 1)
        bias = rpb[:, dr][:, :, dc]
        s_loc = s_loc + jnp.transpose(bias, (0, 2, 1, 3))[None]
        s_ctx = jnp.einsum('bqhd,blhd->bhql', q_row, k_ctx) * scale
        s = jnp.concatenate([s_loc.reshape(B, H, GRID_W, n_loc), s_ctx], axis=-1)
        p = jax.nn.softmax(s.astype(jnp.float32), axis=-1).astype(v.dtype)
        p_loc = p[..., :n_loc].reshape(B, H, GRID_W, kr, kcw)
        p_ctx = p[..., n_loc:]
        return (jnp.einsum('bhqrc,brqchd->bqhd', p_loc, v_win)
                + jnp.einsum('bhql,blhd->bqhd', p_ctx, v_ctx))

    out = lax.map(one_row, (jnp.transpose(qg, (1, 0, 2, 3, 4)), row_start, r_idx))
    return jnp.transpose(out, (1, 0, 2, 3, 4)).reshape(B, S, H, Dh)

def gqa_latent(q, k, v, k_ctx, v_ctx):
    B, S, Hq, Dh = q.shape
    G = Hq // GQA_KV_HEADS
    nb = S // Q_BLOCK
    qb = jnp.transpose(q.reshape(B, nb, Q_BLOCK, GQA_KV_HEADS, G, Dh), (1, 0, 2, 3, 4, 5))
    k_all = jnp.concatenate([k, k_ctx], axis=1)
    v_all = jnp.concatenate([v, v_ctx], axis=1)
    out = lax.map(lambda qblk: attend(qblk, k_all, v_all), qb)
    return jnp.transpose(out, (1, 0, 2, 3, 4, 5)).reshape(B, S, Hq, Dh)

def spatial_gating(z, w_s, b_s, g_sgu):
    B, N, _ = z.shape
    u, v = z[..., :D_B], z[..., D_B:]
    v = layer_norm(v) * g_sgu
    vc = v.reshape(B, N // SG_CHUNK, SG_CHUNK, SG_GROUPS, HEAD_DIM)
    mixed = jnp.einsum('gpq,bnqgc->bnpgc', w_s, vc) + jnp.transpose(b_s)[None, None, :, :, None]
    return u * mixed.reshape(B, N, D_B)

def merge_groups(o_a, o_b, o_c, g_out):
    B, N = o_b.shape[0], o_b.shape[1]
    return jnp.concatenate([
        rms_norm(o_a.reshape(B, N, D_A), g_out[:D_A]),
        rms_norm(o_b, g_out[D_A:D_A + D_B]),
        rms_norm(o_c.reshape(B, N, D_C), g_out[D_A + D_B:]),
    ], axis=-1)

def mixing_sublayer(h, hc, w_in, rpb, w_s, b_s, g_sgu, g_q, g_k, g_out, w_o, need_ctx_out):
    B, S, _ = h.shape
    qa, ka, va, zb, qc, kc, vc = split_cols(h @ w_in, IN_SIZES_2)
    qa_x, ka_x, va_x, zb_x, qc_x, kc_x, vc_x = split_cols(hc @ w_in, IN_SIZES_2)
    cos, sin = axial_rope_tables(S, h.dtype)
    ka_x, va_x = heads(ka_x, NA_HEADS), heads(va_x, NA_HEADS)
    kc_x = rms_norm(heads(kc_x, GQA_KV_HEADS), g_k)
    vc_x = heads(vc_x, GQA_KV_HEADS)
    o_a = neighbourhood_attention(heads(qa, NA_HEADS), heads(ka, NA_HEADS), heads(va, NA_HEADS),
                                  ka_x, va_x, rpb)
    o_b = spatial_gating(jax.nn.gelu(zb), w_s, b_s, g_sgu)
    q_c = apply_axial_rope(rms_norm(heads(qc, GQA_Q_HEADS), g_q), cos, sin)
    k_c = apply_axial_rope(rms_norm(heads(kc, GQA_KV_HEADS), g_k), cos, sin)
    o_c = gqa_latent(q_c, k_c, heads(vc, GQA_KV_HEADS), kc_x, vc_x)
    y = merge_groups(o_a, o_b, o_c, g_out) @ w_o
    if not need_ctx_out:
        return y, None
    L = hc.shape[1]
    o_ax = attend(heads(qa_x, NA_HEADS)[:, :, :, None], ka_x, va_x)
    o_bx = spatial_gating(jax.nn.gelu(zb_x), w_s, b_s, g_sgu)
    q_cx = rms_norm(heads(qc_x, GQA_Q_HEADS), g_q).reshape(
        B, L, GQA_KV_HEADS, GQA_Q_HEADS // GQA_KV_HEADS, HEAD_DIM)
    o_cx = attend(q_cx, kc_x, vc_x)
    yc = merge_groups(o_ax, o_bx, o_cx, g_out) @ w_o
    return y, yc

def swiglu_2(h, w_in, w_out):
    a, b = h @ w_in[:, :D_FF_2], h @ w_in[:, D_FF_2:]
    return (jax.nn.silu(a) * b) @ w_out

def second_inputs(seed: int = 0) -> dict:
    key = jax.random.key(seed)
    ks = jax.random.split(key, 24)
    n = jax.random.normal
    f = jnp.float32
    return {
        "x": n(ks[0], (BATCH, SEQ, D_MODEL), f),
        "c": n(ks[1], (BATCH, D_MODEL), f),
        "ctx": n(ks[2], (BATCH, CTX_LEN, D_MODEL), f),
        "c_ctx": n(ks[3], (D_MODEL,), f),
        "w_mod": n(ks[4], (DEPTH_2, D_MODEL, N_MOD * D_MODEL), f) * (0.5 * D_MODEL ** -0.5),
        "b_mod": n(ks[5], (DEPTH_2, N_MOD * D_MODEL), f) * 0.02,
        "w_in": n(ks[6], (DEPTH_2, D_MODEL, D_IN), f) * D_MODEL ** -0.5,
        "rpb": n(ks[7], (DEPTH_2, NA_HEADS, 2 * NA_WIN_R - 1, 2 * NA_WIN_C - 1), f) * 0.02,
        "w_s": n(ks[8], (DEPTH_2, SG_GROUPS, SG_CHUNK, SG_CHUNK), f) * SG_CHUNK ** -0.5,
        "b_s": n(ks[9], (DEPTH_2, SG_GROUPS, SG_CHUNK), f) * 0.02,
        "g_sgu": 1.0 + 0.02 * n(ks[10], (DEPTH_2, D_B), f),
        "g_q": 1.0 + 0.02 * n(ks[11], (DEPTH_2, HEAD_DIM), f),
        "g_k": 1.0 + 0.02 * n(ks[12], (DEPTH_2, HEAD_DIM), f),
        "g_out": 1.0 + 0.02 * n(ks[13], (DEPTH_2, D_MIX), f),
        "w_o": n(ks[14], (DEPTH_2, D_MIX, D_MODEL), f) * (D_MIX ** -0.5 * BETA),
        "ln1_g": 1.0 + 0.02 * n(ks[15], (DEPTH_2, D_MODEL), f),
        "ln1_b": 0.02 * n(ks[16], (DEPTH_2, D_MODEL), f),
        "w_ffn_in": n(ks[17], (DEPTH_2, D_MODEL, 2 * D_FF_2), f) * D_MODEL ** -0.5,
        "w_ffn_out": n(ks[18], (DEPTH_2, D_FF_2, D_MODEL), f) * (D_FF_2 ** -0.5 * BETA),
        "ln2_g": 1.0 + 0.02 * n(ks[19], (DEPTH_2, D_MODEL), f),
        "ln2_b": 0.02 * n(ks[20], (DEPTH_2, D_MODEL), f),
    }

def second_block(x, c, ctx, c_ctx, w_mod, b_mod, w_in, rpb, w_s, b_s, g_sgu, g_q, g_k, g_out, w_o,
              ln1_g, ln1_b, w_ffn_in, w_ffn_out, ln2_g, ln2_b):
    sc = jax.nn.silu(c)
    sc_ctx = jax.nn.silu(c_ctx)
    for l in range(DEPTH_2):
        need_ctx_out = l < DEPTH_2 - 1
        mod = split_cols((sc @ w_mod[l] + b_mod[l])[:, None, :], (D_MODEL,) * N_MOD)
        mod_x = split_cols(sc_ctx @ w_mod[l] + b_mod[l], (D_MODEL,) * N_MOD)
        sh1, sc1, g1, sh2, sc2, g2 = mod
        sh1x, sc1x, g1x, sh2x, sc2x, g2x = mod_x
        h = modulate(x, sh1, sc1)
        hc = modulate(ctx, sh1x, sc1x)
        y, yc = mixing_sublayer(h, hc, w_in[l], rpb[l], w_s[l], b_s[l], g_sgu[l], g_q[l], g_k[l],
                                g_out[l], w_o[l], need_ctx_out)
        x = layer_norm(ALPHA * x + g1 * y) * ln1_g[l] + ln1_b[l]
        x = layer_norm(ALPHA * x + g2 * swiglu_2(modulate(x, sh2, sc2), w_ffn_in[l], w_ffn_out[l])) \
            * ln2_g[l] + ln2_b[l]
        if need_ctx_out:
            ctx = layer_norm(ALPHA * ctx + g1x * yc) * ln1_g[l] + ln1_b[l]
            ctx = layer_norm(ALPHA * ctx + g2x * swiglu_2(modulate(ctx, sh2x, sc2x), w_ffn_in[l],
                                                         w_ffn_out[l])) * ln2_g[l] + ln2_b[l]
    return x


def setup_inputs(seed=0):
    out = dict(first_inputs(seed))
    for name, value in second_inputs(seed + 1).items():
        if name != "x":
            out[name + "_2"] = value
    return out


def reference(
    x, meta_tokens, norm_ffn1, w_ffn1_in, w_ffn1_out, norm_mix, w_in, b_forget, b_gate,
    fox_q_norm, fox_k_norm, w_o_fox, ret_gn, w_o_ret, w_out, norm_ffn2, w_ffn2_in, w_ffn2_out,
    c_2, ctx_2, c_ctx_2, w_mod_2, b_mod_2, w_in_2, rpb_2, w_s_2, b_s_2, g_sgu_2, g_q_2, g_k_2,
    g_out_2, w_o_2, ln1_g_2, ln1_b_2, w_ffn_in_2, w_ffn_out_2, ln2_g_2, ln2_b_2,
):
    x = first_block(
        x, meta_tokens, norm_ffn1, w_ffn1_in, w_ffn1_out, norm_mix, w_in, b_forget, b_gate,
        fox_q_norm, fox_k_norm, w_o_fox, ret_gn, w_o_ret, w_out, norm_ffn2, w_ffn2_in,
        w_ffn2_out,
    )
    return second_block(
        x, c_2, ctx_2, c_ctx_2, w_mod_2, b_mod_2, w_in_2, rpb_2, w_s_2, b_s_2, g_sgu_2, g_q_2,
        g_k_2, g_out_2, w_o_2, ln1_g_2, ln1_b_2, w_ffn_in_2, w_ffn_out_2, ln2_g_2, ln2_b_2,
    )


_drawn_inputs = setup_inputs


def setup_inputs(seed=0):
    import zlib

    import numpy as np

    out = dict(_drawn_inputs(seed))
    spreads = {}
    factors = {'b_mod_2': 4.01,
     'rpb_2': 34.637,
     'b_s_2': 35.327,
     'g_sgu_2': 39.426,
     'g_q_2': 8.0,
     'g_k_2': 8.0,
     'g_out_2': 8.0}
    for name, (base, spread) in spreads.items():
        noise = np.random.default_rng([zlib.crc32(name.encode()), seed]).standard_normal(out[name].shape)
        drawn = base * np.exp(spread * noise) if base else spread * noise
        out[name] = jnp.asarray(drawn.astype(out[name].dtype))
    for name, factor in factors.items():
        out[name] = (out[name] * factor).astype(out[name].dtype)
    return out
```

```python
import concourse.bass as bass
from concourse import mybir
import numpy as np

F32 = mybir.dt.float32
F32R = mybir.dt.float32r
BF16 = mybir.dt.bfloat16
U16 = mybir.dt.uint16
ACT = mybir.ActivationFunctionType
ALU = mybir.AluOpType
AX = mybir.AxisListType.X

D = 1024
KT = 8
NMETA = 16
TX = 512
TC = 256
T1 = NMETA + TX
NFF = 22
CH = [(0, 8), (8, 7), (15, 7)]
ALPHA = (2 * 2) ** 0.25
GAMMA = [1.0 - 2.0 ** (-5 - h) for h in range(4)]
BASE = 16512

VEC = {}
_n = 0
for _name, _w in [("ffn1", 8), ("mix", 8), ("ffn2", 8), ("bgate", 16), ("retgn", 8), ("fq", 1), ("fk", 1),
                  ("bf", 1), ("c", 16), ("bmod0", 48), ("bmod1", 48), ("gq0", 1), ("gk0", 1), ("gq1", 1),
                  ("gk1", 1), ("gout0", 8), ("gout1", 8), ("ln1g0", 8), ("ln1g1", 8), ("ln1b0", 8),
                  ("ln1b1", 8), ("ln2g0", 8), ("ln2g1", 8), ("ln2b0", 8), ("ln2b1", 8), ("bs0", 4), ("bs1", 4)]:
    VEC[_name] = (_n, _w)
    _n += _w
NVEC = _n


class Tok:

    def __init__(self, eng, idx):
        self.eng, self.idx = eng, idx


class Call:

    def matmul(self, *a, **k):
        self.make = lambda e: e.matmul(*a, **k)

    def transpose(self, *a, **k):
        self.make = lambda e: e.transpose(*a, **k)

    def activation(self, *a, **k):
        self.make = lambda e: e.activation(*a, **k)

    def tensor_tensor(self, *a, **k):
        self.make = lambda e: e.tensor_tensor(*a, **k)

    def tensor_scalar(self, *a, **k):
        self.make = lambda e: e.tensor_scalar(*a, **k)

    def scalar_tensor_tensor(self, *a, **k):
        self.make = lambda e: e.scalar_tensor_tensor(*a, **k)

    def tensor_tensor_scan(self, *a, **k):
        self.make = lambda e: e.tensor_tensor_scan(*a, **k)

    def tensor_reduce(self, *a, **k):
        self.make = lambda e: e.tensor_reduce(*a, **k)

    def tensor_copy(self, *a, **k):
        self.make = lambda e: e.tensor_copy(*a, **k)

    def reciprocal(self, *a, **k):
        self.make = lambda e: e.reciprocal(*a, **k)

    def bn_stats(self, *a, **k):
        self.make = lambda e: e.bn_stats(*a, **k)

    def bn_aggr(self, *a, **k):
        self.make = lambda e: e.bn_aggr(*a, **k)

    def memset(self, *a, **k):
        self.make = lambda e: e.memset(*a, **k)

    def dma_start(self, *a, **k):
        self.make = lambda e: e.dma_start(*a, **k)

    def wait_ge(self, *a, **k):
        self.make = lambda e: e.wait_ge(*a, **k)


class Queue:

    def __init__(self, name, sem):
        self.name, self.sem, self.items, self.marked = name, sem, [], set()

    def op(self, fn, *waits, dma=None):
        ws = []
        call = Call()
        fn(call)

        def flat(w):
            if w is None:
                return
            if isinstance(w, (list, tuple)) and not (len(w) == 2 and isinstance(w[1], int)):
                for x in w:
                    flat(x)
            else:
                ws.append(w)
        flat(list(waits))
        for w in ws:
            if isinstance(w, Tok):
                w.eng.marked.add(w.idx)
        self.items.append((ws, call.make, dma))
        return Tok(self, len(self.items) - 1)

    def last(self):
        n = len(self.items) - 1
        while n >= 0 and self.items[n][2] is not None:
            n -= 1
        return Tok(self, n) if n >= 0 else None

    def count(self):
        self.value, n = {}, 0
        for i in sorted(self.marked):
            n += 1
            self.value[i] = n

    def emit(self, e):
        seen = {}
        for i, (ws, make, dma) in enumerate(self.items):
            need = {}
            for w in ws:
                sem, v = (w.eng.sem, w.eng.value[w.idx]) if isinstance(w, Tok) else w
                k = id(sem)
                if v > seen.get(k, 0) and v > need.get(k, (None, 0))[1]:
                    need[k] = (sem, v)
            for k, (sem, v) in need.items():
                e.wait_ge(sem, v)
                seen[k] = v
            inst = make(e)
            if dma is not None:
                inst.then_inc(dma, 16)
            if i in self.marked:
                inst.then_inc(self.sem, 1)


class DmaSem:

    def __init__(self, sem):
        self.sem, self.n = sem, 0

    def add(self, q, fn, *waits):
        q.op(fn, *waits, dma=self.sem)
        self.n += 16
        return (self.sem, self.n)


def build(nc, A, out):
    order = []
    _program(nc, A, out, order, True)
    _program(nc, A, out, order, False)


def _program(nc, A, out, order, dry):
    nosem = [0]

    def sem(name):
        if dry:
            nosem[0] += 1
            return nosem[0]
        return nc.alloc_semaphore(name)

    PE, DVE, AC, PL, SP = (Queue(n, sem("s_" + n)) for n in ("pe", "dve", "act", "pool", "sp"))

    tag = ["d" if dry else "r"]

    def at(name, shape, dt, offset):
        assert offset % 32 == 0, (name, offset)
        t = nc.alloc_sbuf_tensor_at(f"{tag[0]}_{name}", shape, dt, offset=BASE + offset)
        size = 4
        for s in shape[1:]:
            size *= s
        if dt in (BF16, U16):
            size //= 2
        ends.append((name, offset, offset + size))
        assert BASE + offset + size <= 229368, (name, offset + size)
        return t, (offset + size + 31) // 32 * 32

    ends = []
    H, p = at("H", [128, KT, NMETA + TX + TC], F32, 0)
    NW, NS = 4, 3
    Wf, p = at("Wf", [128, NW, 1024], F32, p)
    Wh, p = at("Wh", [128, NS, 1024], F32R, p)
    Wl, p = at("Wl", [128, NS, 1024], F32R, p)
    V, p = at("V", [128, NVEC], F32, p)
    CF, p = at("CF", [128, 5, 128], F32, p)
    CB, p = at("CB", [128, 2, 128], U16, p)
    SC, p = at("SC", [128, 8, 2], F32, p)
    MOD, p = at("MOD", [128, 2, 48, 2], F32, p)
    RS, p = at("RS", [128, 3, 512], F32, p)
    SM, p = at("SM", [128, 112], F32, p)
    P0 = p
    ONES, BLK, IDF, PRM, PAX = (CF[:, i, :] for i in range(5))
    IDB, MSKB = CB[:, 0, :].bitcast(BF16), CB[:, 1, :].bitcast(BF16)

    def vec(name, k=0):
        return V[:, VEC[name][0] + k:VEC[name][0] + k + 1]

    if dry:
        PS = nc_ps[0] if nc_ps else None
        if PS is None:
            PS = nc.alloc_psum_tensor("PS", [128, 8, 512], F32)
            nc_ps.append(PS)
    else:
        PS = nc_ps[0]

    bank = {"next": 0, "free": [[] for _ in range(8)], "out": [False] * 8}

    def take(n=1):
        b = bank["next"]
        if n == 2 and b % 2:
            b = (b + 1) % 8
        bank["next"] = (b + n) % 8
        w = []
        for i in range(b, b + n):
            assert not bank["out"][i], "bank in use"
            bank["out"][i] = True
            w += bank["free"][i]
        return b, w

    def give(b, toks, n=1):
        for i in range(b, b + n):
            assert bank["out"][i]
            bank["out"][i] = False
            bank["free"][i] = list(toks)

    def psb(b, n=512, p=128):
        return PS[0:p, b, 0:n]

    def psb2(b, a, z, p=128):
        return PS[:, :, :].rearrange("p b n -> p (b n)")[0:p, b * 512 + a:b * 512 + z]

    def fence():
        return [q.last() for q in (PE, DVE, AC, PL) if q.last()]

    fence_tok = [[]]

    def barrier():
        f = fence()
        fence_tok[0] = f
        for q in (PE, DVE, AC, PL):
            q.fence = f
        return f

    def F():
        return fence_tok[0]

    wsem = [DmaSem(sem(f"s_w{i}")) for i in range(NW)]
    W = {"loaded": 0, "split": 0, "used": 0, "nsplit": 0}
    u_arrived, u_ready, u_slot, wf_free, ws_free = {}, {}, {}, {}, {}

    def w_pump():
        moved = True
        while moved:
            moved = False
            i = W["loaded"]
            if i < len(order) and (i < NW or i - NW in wf_free):
                name, idx, cols, raw = order[i]
                src = A[name]
                for j in idx:
                    src = src[j]
                u_arrived[i] = wsem[i % NW].add(SP, lambda e: e.dma_start(Wf[:, i % NW, 0:cols], src),
                                                wf_free.get(i - NW))
                W["loaded"] += 1
                moved = True
            i = W["split"]
            if i < W["loaded"]:
                name, idx, cols, raw = order[i]
                f = Wf[:, i % NW, 0:cols]
                if raw:
                    u_slot[i], u_ready[i] = i % NW, u_arrived[i]
                elif W["nsplit"] < NS or W["nsplit"] - NS in ws_free:
                    n = W["nsplit"]
                    s = n % NS
                    h, l = Wh[:, s, 0:cols], Wl[:, s, 0:cols]
                    hi = AC.op(lambda e: e.activation(h, f, ACT.Copy), u_arrived[i], ws_free.get(n - NS))
                    lo = DVE.op(lambda e: e.tensor_tensor(l, f, h.bitcast(F32), ALU.subtract), hi)
                    u_slot[i], u_ready[i] = s, lo
                    wf_free[i] = lo
                    W["nsplit"] += 1
                else:
                    continue
                W["split"] += 1
                moved = True

    def w_get(name, idx, cols, raw=False):
        i = W["used"]
        W["used"] += 1
        if dry:
            order.append((name, idx, cols, raw))
            return i, 0, None
        assert order[i] == (name, idx, cols, raw)
        w_pump()
        return i, u_slot[i], u_ready[i]

    def w_done(i, tok, raw=False):
        if dry:
            return
        if raw:
            wf_free[i] = tok
        else:
            ws_free[sum(1 for u in order[:i] if not u[3])] = tok
        w_pump()

    def mm3(o, wh, wl, xh, xl, first, last, *waits, wmain=True):
        PE.op(lambda e: e.matmul(o, wh, xh, start=first, stop=False), *waits)
        PE.op(lambda e: e.matmul(o, wh, xl, start=False, stop=False))
        return PE.op(lambda e: e.matmul(o, wl, xh, start=False, stop=last))

    def lin(name, idx, kt, X, off, chunks, *waits):
        u, s, ready = w_get(name, idx, kt * 128)
        res = []
        for c0, n in chunks:
            b, bw = take()
            for k in range(kt):
                w = Wh[:, s, k * 128:k * 128 + 128], Wl[:, s, k * 128:k * 128 + 128]
                t = mm3(psb(b, n), *w, X[0][:, k, c0 - off:c0 - off + n], X[1][:, k, c0 - off:c0 - off + n],
                        k == 0, k == kt - 1, ready, bw, waits)
            res.append((b, t))
        w_done(u, t)
        return res

    def lin_tok(name, g, X, tiles, epi, *waits):
        u0, s0, r0 = w_get(name, (g, 0), 1024)
        u1, s1, r1 = w_get(name, (g, 1), 1024)
        for i, c0 in enumerate(tiles):
            b, bw = take()
            for k in range(8):
                s = (s0, s1)[k // 4]
                a = (k % 4) * 256
                o = psb(b, 256)
                xh, xl = X[0][:, k, c0:c0 + 128], X[1][:, k, c0:c0 + 128]
                wh, wl = Wh[:, s, a:a + 256], Wl[:, s, a:a + 256]
                t = mm3(o, xh, xl, wh, wl, k == 0, k == 7, r0, r1, bw, waits)
            give(b, epi(i, b, t))
        w_done(u0, t)
        w_done(u1, t)

    s_in = DmaSem(sem("s_in"))
    ld = None
    for dst, src in ((H[:, :, 0:T1], A["x0"]), (V[:, :], A["vec"]), (CF[:, :, :], A["cf"]),
                     (CB[:, :, :], A["cb"]), (H[:, :, T1:T1 + TC], A["ctx"])):
        ld = s_in.add(AC, lambda e, dst=dst, src=src: e.dma_start(dst, src))
    t_in = ld
    for q in (PE, DVE, AC, PL):
        q.fence = []
    n_load = []

    def load(dst, src, *waits):
        n_load.append(DmaSem(sem(f"s_ld{len(n_load)}")))
        return n_load[-1].add(PL, lambda e: e.dma_start(dst, src), *waits)

    c0v = VEC["c"][0]
    SCT = SM[:, 80:96]
    t = AC.op(lambda e: e.activation(SCT, V[:, c0v:c0v + 16], ACT.Silu), t_in)
    t_sc = DVE.op(lambda e: e.tensor_copy(SC[:, :, :].rearrange("p k c -> p (k c)"), SCT), t)
    mods = [(l, m) for l in range(2) for m in range(48)]
    mod_tok = [None, None]

    def mod_step(count=1):
        for _ in range(count):
            if not mods:
                return
            l, m = mods.pop(0)
            u, s, ready = w_get("wmod", (l, m), 1024, True)
            b, bw = take()
            for k in range(8):
                t = PE.op(lambda e, k=k: e.matmul(psb(b, 2), Wf[:, s, k * 128:k * 128 + 128], SC[:, k, :],
                                                  start=k == 0, stop=k == 7), ready, bw, t_sc)
            w_done(u, t, True)
            part, name = m // 8, f"bmod{l}"
            one = 1.0 if part in (1, 4) else 0.0
            t = DVE.op(lambda e: e.tensor_scalar(MOD[:, l, m, :], psb(b, 2), vec(name, m), one, ALU.add,
                                                 ALU.add), t)
            give(b, [t])
            mod_tok[l] = t

    def mod(l, part, k, c):
        return MOD[:, l, part * 8 + k, c:c + 1]

    def rsqrt(x, y, t, ready, mul=1.0, *waits):
        a = AC.op(lambda e: e.activation(y, x, ACT.Sqrt), ready, waits)
        a = DVE.op(lambda e: e.reciprocal(y, y), a)
        a = DVE.op(lambda e: e.tensor_tensor(t, y, y, ALU.mult), a)
        a = DVE.op(lambda e: e.scalar_tensor_tensor(t, t, -0.5 * mul, x, ALU.mult, ALU.mult), a)
        return DVE.op(lambda e: e.scalar_tensor_tensor(y, t, 1.5 * mul, y, ALU.add, ALU.mult), a)

    def norm(kind, c0, n, XC, SQ, scale, bias, dst, off, rs, *waits):
        hs = [H[:, k, c0:c0 + n] for k in range(8)]
        if kind == "ln":
            b, bw = take()
            for k in range(8):
                t = PE.op(lambda e, k=k: e.matmul(psb(b, n), ONES, hs[k], start=k == 0, stop=k == 7),
                          bw, waits)
            xs = [None] * 8
            for k in range(8):
                xs[k] = DVE.op(lambda e, k=k: e.tensor_tensor(XC[:, k, 0:n], hs[k], psb(b, n),
                                                              ALU.subtract), t, waits)
            give(b, [xs[7]])
            src = [XC[:, k, 0:n] for k in range(8)]
        else:
            xs, src = [None] * 8, hs
        b, bw = take()
        for k in range(8):
            t = AC.op(lambda e, k=k: e.activation(SQ[:, k, 0:n], src[k], ACT.Square), xs[k], waits)
            t = PE.op(lambda e, k=k: e.matmul(psb(b, n), ONES, SQ[:, k, 0:n], start=k == 0, stop=k == 7),
                      t, bw)
        r = RS[:, 0, 0:n]
        t = DVE.op(lambda e: e.tensor_scalar(r, psb(b, n), 1e-6, None, ALU.add), t, waits)
        give(b, [t])
        t = rsqrt(r, RS[:, 1, 0:n], RS[:, 2, 0:n], t)
        r = RS[:, 1, 0:n]
        for k in range(8):
            u = DVE.op(lambda e, k=k: e.scalar_tensor_tensor(XC[:, k, 0:n], src[k], scale(k), r, ALU.mult,
                                                             ALU.mult), t, xs[k], waits)
            if dst is None:
                u = AC.op(lambda e, k=k: e.activation(hs[k], XC[:, k, 0:n], ACT.Identity, bias=bias(k)), u)
                end = [u]
                continue
            xh, xl = dst[0][:, k, c0 - off:c0 - off + n], dst[1][:, k, c0 - off:c0 - off + n]
            if bias is None:
                u = AC.op(lambda e, k=k, xh=xh: e.activation(xh, XC[:, k, 0:n], ACT.Copy), u)
                v = DVE.op(lambda e, k=k, xh=xh, xl=xl: e.tensor_tensor(
                    xl, XC[:, k, 0:n], xh.bitcast(F32), ALU.subtract), u)
            else:
                u = AC.op(lambda e, k=k, xh=xh: e.activation(xh, XC[:, k, 0:n], ACT.Identity,
                                                             bias=bias(k)), u)
                v = DVE.op(lambda e, k=k, xh=xh, xl=xl: e.scalar_tensor_tensor(
                    xl, XC[:, k, 0:n], bias(k), xh.bitcast(F32), ALU.add, ALU.subtract), u)
            end = [v]
        return end

    def norm_all(kind, blocks, scale, bias, dst, off, tmp, *waits):
        XC, q = at(f"XC{tmp}_{nid[0]}", [128, 8, 264], F32, tmp)
        SQ, q = at(f"SQ{tmp}_{nid[0]}", [128, 8, 264], F32, q)
        nid[0] += 1
        end, toks = [], []
        for i, (c0, n, c) in enumerate(blocks):
            end = norm(kind, c0, n, XC, SQ, lambda k: scale(k, c), bias and (lambda k: bias(k, c)), dst,
                       off, i % 2, waits, end, fence())
            toks.append(end)
        return toks

    nid = [0]

    def ffn(tagw, X, off, chunks, HH, HL, TM, ready, gate, mods_per):
        free = [[], []]
        n_tm = [0]
        hw = {}
        hid_free = []
        for ci, (j0, nj) in enumerate(CH):
            hid_ready = []
            pend = []

            def finish(j, ra, rb):
                for (c0, n), (ba, ta), (bb, tb) in zip(chunks, ra, rb):
                    i = n_tm[0] % 2
                    n_tm[0] += 1
                    x = TM[:, i, 0:n]
                    t = AC.op(lambda e: e.activation(x, psb(ba, n), ACT.Silu), ta, free[i], F())
                    give(ba, [t])
                    u = DVE.op(lambda e: e.tensor_tensor(x, x, psb(bb, n), ALU.mult), t, tb)
                    give(bb, [u])
                    hh, hl = HH[:, j, c0 - off:c0 - off + n], HL[:, j, c0 - off:c0 - off + n]
                    v = AC.op(lambda e: e.activation(hh, x, ACT.Copy), u, hid_free)
                    w = PL.op(lambda e: e.tensor_tensor(hl, x, hh.bitcast(F32), ALU.subtract), v, hid_free)
                    free[i] = [w]
                    hid_ready.append(w)

            for j in range(nj):
                ra = lin(tagw + "_in", (j0 + j,), 8, X, off, chunks, ready)
                rb = lin(tagw + "_in", (NFF + j0 + j,), 8, X, off, chunks, ready)
                mod_step(mods_per)
                finish(j, ra, rb)
            hr = hid_ready[-1:]
            for m in range(8):
                r = lin(f"{tagw}_out{ci}", (m,), nj, (HH, HL), off, chunks, hr)
                for (c0, n), (b, t) in zip(chunks, r):
                    hk = H[:, m, c0:c0 + n]
                    g = gate(m, c0)
                    t2 = DVE.op(lambda e: e.scalar_tensor_tensor(hk, psb(b, n), g, hk, ALU.mult, ALU.add),
                                t, hw.get((m, c0)), ready)
                    give(b, [t2])
                    hw[m, c0] = t2
                    hid_free = [t]
        return [DVE.last()]

    def attention(units, Pb, PT, scale=None):
        st = [dict() for _ in units]
        pfree = [[], []]
        ptfree = [[], []]

        def step_a(u):
            d, s = units[u], st[u]
            i = u % 2
            if "pre" in d:
                d["pre"]()
            b, bw = take(2)
            n = d["n"]
            parts = [(0, min(n, 512))] + ([(512, n)] if n > 512 else [])
            for a, z in parts:
                extra = [x for x in d.get("add", []) if x[2] >= a and x[2] < z]
                kk = d["k"](a, z)
                t = PE.op(lambda e: e.matmul(psb2(b, a, z), d["q"], kk, start=True, stop=not extra), bw,
                          d["ready"], F())
                for x in extra:
                    rhs = x[1](x[2], x[3])
                    t = PE.op(lambda e: e.matmul(psb2(b, x[2], x[3]), x[0], rhs, start=False,
                                                 stop=x is extra[-1]), d["ready"])
            lg = psb2(b, 0, n)
            if "bias" in d:
                m = d["bias"]
                t = DVE.op(lambda e: e.tensor_tensor(psb2(b, 0, 512), psb2(b, 0, 512), m, ALU.add), t,
                           br_tok[d["bias_ready"]])
            mx = SM[:, 2 * i:2 * i + 1]
            t = DVE.op(lambda e: e.tensor_reduce(mx, lg, AX, ALU.max, negate=True), t, pfree[i])
            rs = SM[:, 4 + 2 * i:5 + 2 * i]
            t = AC.op(lambda e: e.activation(Pb[:, i, 0:n], lg, ACT.Exp, bias=mx, accum_out=rs), t,
                      pfree[i])
            give(b, [t], 2)
            rc = SM[:, 8 + 2 * (u % 4):9 + 2 * (u % 4)]
            s["rc_t"] = DVE.op(lambda e: e.reciprocal(rc, rs), t, st[u - 4]["o"] if u >= 4 else None)
            s["exp"], s["rc"] = t, rc

        def step_b(u):
            d, s = units[u], st[u]
            i = u % 2
            b, bw = take(2)
            full = [x for x in d["blocks"] if x[1] == 128]
            part = [x for x in d["blocks"] if x[1] < 128]
            for j, (c, w, v) in enumerate(full):
                t = PE.op(lambda e: e.transpose(psb2(b, j * 128, j * 128 + 128), Pb[:, i, c:c + 128], IDF),
                          s["exp"], bw)
            for j, (c, w, v) in enumerate(part):
                t = PE.op(lambda e: e.matmul(psb2(b, 512, 640, w), Pb[:, i, c:c + w], IDF, start=True,
                                             stop=True), s["exp"], bw)
            n = len(full) * 128
            q = AC if u % 2 else DVE
            cp = (lambda e, o, x: e.activation(o, x, ACT.Copy)) if q is AC else (
                lambda e, o, x: e.tensor_copy(o, x))
            t2 = q.op(lambda e: cp(e, PT[:, i, 0:n], psb2(b, 0, n)), t, ptfree[i], F())
            s["pt"] = [t2]
            if part:
                w = part[0][1]
                t2 = q.op(lambda e: cp(e, PT[0:w, i, 512:640], psb2(b, 512, 640, w)), t)
                s["pt"] = [t2]
            give(b, [t2], 2)
            pfree[i] = [t, s["rc_t"], s["exp"]]

        def step_c(u):
            d, s = units[u], st[u]
            i = u % 2
            b, bw = take(1)
            full = [x for x in d["blocks"] if x[1] == 128]
            part = [x for x in d["blocks"] if x[1] < 128]
            o = psb(b, 64)
            seq = [(PT[:, i, j * 128:j * 128 + 128], x[2]) for j, x in enumerate(full)]
            seq += [(PT[0:x[1], i, 512:640], x[2]) for x in part]
            for j, (l, r) in enumerate(seq):
                t = PE.op(lambda e: e.matmul(o, l, r, start=j == 0, stop=j == len(seq) - 1), s["pt"], bw,
                          d["vready"])
            ptfree[i] = [t]
            s["o"] = DVE.op(lambda e: e.tensor_scalar(d["out"], o, s["rc"], None, ALU.mult), t, s["rc_t"],
                            F())
            give(b, [s["o"]])

        for u in range(len(units) + 2):
            if u < len(units):
                step_a(u)
            if 1 <= u <= len(units):
                step_b(u - 1)
            if u >= 2:
                step_c(u - 2)
        return st[-1]["o"]

    def head_rms(raw, n, g, mul, ready, SQt, i, *waits):
        t = AC.op(lambda e: e.activation(SQt[:, 0:n], raw, ACT.Square), ready, waits)
        out_t = []
        for a in range(0, n, 512):
            z = min(n, a + 512)
            b, bw = take()
            t2 = PE.op(lambda e: e.matmul(psb(b, z - a), BLK, SQt[:, a:z], start=True, stop=True), t, bw)
            x, r, y = (RS[:, j, 0:z - a] for j in range(3))
            t3 = DVE.op(lambda e: e.tensor_scalar(x, psb(b, z - a), 1e-6, None, ALU.add), t2, rsfree)
            give(b, [t3])
            t4 = rsqrt(x, r, y, t3, mul)
            t5 = DVE.op(lambda e: e.scalar_tensor_tensor(raw[:, a:z], raw[:, a:z], g, r, ALU.mult,
                                                         ALU.mult), t4)
            rsfree[:] = [t5]
            out_t.append(t5)
        return out_t, t2

    rsfree = []
    br_tok = {}

    def to_features(TOKN, tiles, cols, fn, ready):
        for f in cols:
            for g0 in range(0, len(tiles), 4):
                b, bw = take()
                grp = tiles[g0:g0 + 4]
                for j, i in enumerate(grp):
                    t = PE.op(lambda e, i=i, j=j: e.transpose(psb2(b, j * 128, j * 128 + 128),
                                                              TOKN[:, i, f * 128:f * 128 + 128], IDF),
                              ready, bw)
                give(b, fn(f, g0 * 128, len(grp) * 128, b, t))

    XH, p = at("X1h", [128, 8, T1], F32R, P0)
    XL, p = at("X1l", [128, 8, T1], F32R, p)
    P1 = p
    HH, p = at("H1h", [128, 8, T1], F32R, P1)
    HL, p = at("H1l", [128, 8, T1], F32R, p)
    TM, p = at("TM1", [128, 2, 264], F32, p)
    X = (XH, XL)
    chunks = [(0, 264), (264, 264)]
    e = norm_all("rms", [(0, 264, 0), (264, 264, 0)], lambda k, c: vec("ffn1", k), None, X, 0, p, t_in)
    e = ffn("f1", X, 0, chunks, HH, HL, TM, e[1], lambda m, c0: 0.5, 2)
    e = norm_all("rms", [(0, 264, 0), (264, 264, 0)], lambda k, c: vec("mix", k), None, X, 0, p, e)
    xr = e[1]
    barrier()

    YB, p = at("YB", [128, 8, TX], F32, P1 + 8 * TX * 4)
    P2 = p
    RQ, p = at("RQ", [128, 4, TX], F32, P2)
    RK, p = at("RK", [128, 4, T1], F32, p)
    VR, p = at("VR", [128, 5, 1024], F32, p)
    P3 = p
    CS, p = at("CS", [128, 2, T1], F32, P3)
    RT, p = at("RT", [128, 2, T1], F32, p)
    tl = load(CS[:, :, :], A["rope1"], F())
    rfree = [[], []]
    idx = [0]
    rk_ready = []

    def rope(dst, c0, n, tabs, col, perm, ready, RTn):
        i = idx[0] % 2
        idx[0] += 1
        b, bw = take()
        t = PE.op(lambda e: e.matmul(psb(b, n), perm, dst, start=True, stop=True), ready, bw)
        u = DVE.op(lambda e: e.tensor_tensor(RTn[:, i, 0:n], psb(b, n), tabs[:, 1, col:col + n], ALU.mult),
                   t, rfree[i], tl)
        give(b, [u])
        v = PL.op(lambda e: e.tensor_tensor(dst, dst, tabs[:, 0, col:col + n], ALU.mult), t, tl)
        w = DVE.op(lambda e: e.tensor_tensor(dst, dst, RTn[:, i, 0:n], ALU.add), u, v)
        rfree[i] = [w]
        return w

    pend = []

    def flush():
        while pend:
            pend.pop(0)()

    for dst, nm, chs in ((RQ, "w_rq", [(16, 512)]), (RK, "w_rk", chunks)):
        for m in range(4):
            res = lin(nm, (m,), 8, X, 0, chs, xr)
            flush()
            for (c0, n), (b, t) in zip(chs, res):
                a = c0 - (16 if dst is RQ else 0)
                o = dst[:, m, a:a + n]
                t = AC.op(lambda e: e.activation(o, psb(b, n), ACT.Copy), t, F())
                give(b, [t])
                pend.append(lambda o=o, c0=c0, n=n, t=t: rk_ready.append(rope(o, c0, n, CS, c0, PRM, t, RT)))
    tiles1 = [0, 16, 144, 272, 400]

    def vcopy(dst, base, meta=False):
        def epi(i, b, t):
            rows = NMETA if i == 0 and meta else 128
            q = AC if i % 2 else DVE
            if q is AC:
                return [AC.op(lambda e: e.activation(dst[0:rows, i, base:base + 256], psb(b, 256, rows),
                                                     ACT.Copy), t, F())]
            return [DVE.op(lambda e: e.tensor_copy(dst[0:rows, i, base:base + 256], psb(b, 256, rows)), t,
                           F())]
        return epi

    for g in range(4):
        lin_tok("w_rv", g, X, tiles1, vcopy(VR, g * 256, True), xr)
        flush()
    barrier()
    DT, p = at("DT", [128, 4, T1], F32, P3)
    SS, p = at("SS", [128, 2, 5, 128], F32, p)
    YT, _ = at("YT", [128, 4, 1024], F32, P1)
    ST, p = at("ST", [128, 4, 8], F32, p)
    tl2 = load(DT[:, :, :], A["decay"], F())
    sfree = [[], []]
    units = [(h, i) for h in range(4) for i in range(4)]
    S = {}

    def ret_a(u):
        h, i = units[u]
        b, bw = take(2)
        q = RQ[:, h, i * 128:i * 128 + 128]
        for j in range(i + 1):
            k = RK[:, h, 16 + j * 128:144 + j * 128]
            t = PE.op(lambda e, j=j: e.matmul(psb2(b, j * 128, j * 128 + 128), k, q, start=True, stop=True),
                      bw, rk_ready, F())
        k = RK[:, h, 0:NMETA]
        t = PE.op(lambda e: e.matmul(psb2(b, 512, 640, NMETA), k, q, start=True, stop=True))
        s = SS[:, u % 2, :, :]
        for j in range(i + 1):
            a = (i - j) * 128
            t2 = DVE.op(lambda e, j=j, a=a: e.tensor_tensor(s[:, j, :], psb2(b, j * 128, j * 128 + 128),
                                                            DT[:, h, a:a + 128], ALU.mult), t, tl2,
                        sfree[u % 2], F())
        a = 16 + i * 128
        t2 = DVE.op(lambda e: e.tensor_tensor(s[0:NMETA, 4, :], psb2(b, 512, 640, NMETA),
                                              DT[0:NMETA, h, a:a + 128], ALU.mult), t)
        give(b, [t2], 2)
        S[u] = t2

    yt_toks = []

    def ret_b(u):
        h, i = units[u]
        b, bw = take()
        s = SS[:, u % 2, :, :]
        o = psb(b, 256)
        for j in range(i + 1):
            PE.op(lambda e, j=j: e.matmul(o, s[:, j, :], VR[:, j + 1, h * 256:h * 256 + 256], start=j == 0,
                                          stop=False), S[u], bw)
        t = PE.op(lambda e: e.matmul(o, s[0:NMETA, 4, :], VR[0:NMETA, 0, h * 256:h * 256 + 256],
                                     start=False, stop=True))
        sfree[u % 2] = [t]
        st, ag = ST[:, u % 4, 0:6], SM[:, 16 + 2 * (u % 4):18 + 2 * (u % 4)]
        v = DVE.op(lambda e: e.bn_stats(st, o), t, F())
        v = DVE.op(lambda e: e.bn_aggr(ag, st), v)
        v = DVE.op(lambda e: e.tensor_scalar(ag[:, 1:2], ag[:, 1:2], 1e-5, None, ALU.add), v)
        y = SM[:, 24 + 2 * (u % 4):25 + 2 * (u % 4)]
        v = rsqrt(ag[:, 1:2], y, SM[:, 96:97], v)
        v = DVE.op(lambda e: e.tensor_scalar(YT[:, i, h * 256:h * 256 + 256], o, ag[:, 0:1], y,
                                             ALU.subtract, ALU.mult), v)
        give(b, [v])
        yt_toks.append(v)

    for u in range(len(units) + 1):
        if u < len(units):
            ret_a(u)
        if u >= 1:
            ret_b(u - 1)

    def to_yb(f, a, n, b, t):
        return [AC.op(lambda e: e.activation(YB[:, f, a:a + n], psb(b, n), ACT.Copy), t, F())]

    to_features(YT, [0, 1, 2, 3], range(8), to_yb, yt_toks[-1])
    SG, p = at("SG", [128, 2, 512], F32, P1)
    sgf = [[], []]
    ybt = fence()
    for m in range(8):
        (b, t), = lin("w_rg", (m,), 8, X, 0, [(16, 512)], xr)
        i = m % 2
        t = AC.op(lambda e: e.activation(SG[:, i, :], psb(b), ACT.Silu), t, sgf[i], F())
        give(b, [t])
        t = DVE.op(lambda e: e.scalar_tensor_tensor(YB[:, m, :], YB[:, m, :], vec("retgn", m), SG[:, i, :],
                                                    ALU.mult, ALU.mult), t, ybt)
        sgf[i] = [t]
    barrier()

    Q, p = at("Q", [128, 8, TX], F32, P2)
    K, p = at("K", [128, 8, T1], F32, p)
    VF, p = at("VF", [128, 5, 1024], F32, p)
    SEL, p = at("SEL", [128, 16, 128], U16, p)
    CP, p = at("CP", [128, T1], BF16, p)
    P4 = p
    SQT, p = at("SQT", [128, 2, T1], F32, P1)
    LF, p = at("LF", [16, 5, T1], F32, p)
    tl = load(SEL[:, :, :], A["sel"], F())
    cz = PL.op(lambda e: e.memset(CP[:, :], 0.0), F())
    cfree = []
    res = lin("w_ff", (0,), 8, X, 0, chunks, xr)
    z, az, u_, r_, s_ = (LF[:, i, :] for i in range(5))
    for (c0, n), (b, t) in zip(chunks, res):
        t = AC.op(lambda e: e.activation(z[:, c0:c0 + n], psb(b, n, 16), ACT.Identity, bias=V[0:16,
                  VEC["bf"][0]:VEC["bf"][0] + 1]), t, F())
        give(b, [t])
    t = AC.op(lambda e: e.activation(az, z, ACT.Abs), t)
    t = AC.op(lambda e: e.activation(az, az, ACT.Exp, scale=-1.0), t)
    t = DVE.op(lambda e: e.tensor_scalar(u_, az, 1.0, None, ALU.add), t)
    tl_n = AC.op(lambda e: e.activation(r_, u_, ACT.Ln), t)
    t = DVE.op(lambda e: e.scalar_tensor_tensor(s_, u_, -1.0, az, ALU.add, ALU.subtract), t)
    t = DVE.op(lambda e: e.reciprocal(u_, u_), t, tl_n)
    t = DVE.op(lambda e: e.tensor_tensor(s_, s_, u_, ALU.mult), t)
    t = DVE.op(lambda e: e.tensor_tensor(r_, r_, s_, ALU.subtract), t)
    t = DVE.op(lambda e: e.scalar_tensor_tensor(r_, z, 0.0, r_, ALU.min, ALU.subtract), t)
    t = DVE.op(lambda e: e.tensor_scalar(r_, r_, -1.0, None, ALU.mult), t)
    t = DVE.op(lambda e: e.memset(u_, 1.0), t)
    t = DVE.op(lambda e: e.tensor_tensor_scan(s_, u_, r_, 0.0, ALU.mult, ALU.add), t)
    t = DVE.op(lambda e: e.tensor_copy(CP[0:16, :], s_), t, cz)
    t = DVE.op(lambda e: e.tensor_tensor(s_, s_, CP[0:16, :], ALU.subtract), t)
    t = DVE.op(lambda e: e.tensor_copy(CP[32:48, :], s_), t)
    t = DVE.op(lambda e: e.tensor_copy(u_, CP[32:48, :]), t)
    t = DVE.op(lambda e: e.tensor_tensor(s_, s_, u_, ALU.subtract), t)
    c_ready = DVE.op(lambda e: e.tensor_copy(CP[64:80, :], s_), t)

    qk_ready = []
    sqf = [[], []]
    nq = [0]
    for dst, nm, chs, g, mul in ((Q, "w_fq", [(16, 512)], "fq", 0.125), (K, "w_fk", chunks, "fk", 1.0)):
        for m in range(8):
            res = lin(nm, (m,), 8, X, 0, chs, xr)
            flush()
            for (c0, n), (b, t) in zip(chs, res):
                a = c0 - (16 if dst is Q else 0)
                o = dst[:, m, a:a + n]
                t = AC.op(lambda e: e.activation(o, psb(b, n), ACT.Copy), t, F())
                give(b, [t])

                def later(o=o, n=n, t=t, g=g, mul=mul):
                    i = nq[0] % 2
                    nq[0] += 1
                    r, t2 = head_rms(o, n, vec(g), mul, t, SQT[:, i, :], i, sqf[i])
                    sqf[i] = [t2]
                    qk_ready.extend(r)
                pend.append(later)
    for g in range(4):
        lin_tok("w_fv", g, X, tiles1, vcopy(VF, g * 256, True), xr)
        flush()
    barrier()
    YT, p = at("YTF", [128, 4, 1024], F32, P1)
    Pb, p = at("Pb", [128, 2, 528], F32, P4)
    PT, p = at("PT", [128, 2, 640], F32, p)
    us = []
    for h in range(16):
        r0 = 64 * (h % 2)
        for i in range(4):
            n = 144 + 128 * i
            us.append({
                "q": Q[r0:r0 + 64, h // 2, i * 128:i * 128 + 128],
                "k": lambda a, z, h=h, r0=r0: K[r0:r0 + 64, h // 2, a:z],
                "n": n,
                "add": [(IDB, lambda a, z, i=i: MSKB[:, a - 16 - 128 * i:z - 16 - 128 * i], 16 + 128 * i, n),
                        (SEL[:, h, :].bitcast(BF16), lambda a, z: CP[:, a:z], 0, n)],
                "blocks": [(16 + 128 * j, 128, VF[:, j + 1, h * 64:h * 64 + 64]) for j in range(i + 1)]
                + [(0, 16, VF[0:16, 0, h * 64:h * 64 + 64])],
                "ready": [qk_ready, c_ready, tl], "vready": [],
                "out": YT[:, i, h * 64:h * 64 + 64]})
    for d in us:
        if d["n"] > 512:
            (l1, f1, a1, z1), (l0, f0, a0, z0) = d["add"]
            d["add"] = [(l1, f1, a1, 512), (l0, f0, 0, 512), (l1, f1, 512, z1), (l0, f0, 512, z0)]
    t = attention(us, Pb, PT)
    barrier()
    YA, _ = at("YA", [128, 8, TX], F32, P2)

    def to_ya(f, a, n, b, t):
        return [AC.op(lambda e: e.activation(YA[:, f, a:a + n], psb(b, n), ACT.Copy), t, F())]

    to_features(YT, [0, 1, 2, 3], range(8), to_ya, t)
    barrier()

    def split(src, h, l, *waits):
        for k in range(8):
            t = AC.op(lambda e, k=k: e.activation(h[:, k, :], src[:, k, :], ACT.Copy), waits)
            t = DVE.op(lambda e, k=k: e.tensor_tensor(l[:, k, :], src[:, k, :], h[:, k, :].bitcast(F32),
                                                      ALU.subtract), t, waits)
        return t

    M1, _ = at("M1", [128, 8, TX], F32, P1)
    YH, p = at("YAh", [128, 8, TX], F32R, P2 + 8 * TX * 4)
    YL, p = at("YAl", [128, 8, TX], F32R, p)
    GT, p = at("GT", [128, 2, 512], F32, p)
    yr = split(YA, YH, YL, F())
    gf = [[], []]
    XX = [(16, 512)]
    for m in range(8):
        (b0, t0), = lin("w_ga", (m,), 8, X, 0, XX, xr)
        (b1, t1), = lin("w_of", (m,), 8, (YH, YL), 16, XX, yr)
        i = m % 2
        t = AC.op(lambda e: e.activation(GT[:, i, :], psb(b0), ACT.Sigmoid, bias=vec("bgate", m)), t0,
                  gf[i], F())
        give(b0, [t])
        t = DVE.op(lambda e: e.tensor_tensor(M1[:, m, :], GT[:, i, :], psb(b1), ALU.mult), t, t1, F())
        give(b1, [t])
        gf[i] = [t]
    barrier()
    YH, p2 = at("YBh", [128, 8, TX], F32R, P2)
    YL, p2 = at("YBl", [128, 8, TX], F32R, p2)
    GT, p2 = at("GT2", [128, 2, 512], F32, p2)
    MH, _ = at("MXh", [128, 8, TX], F32R, P1 + 8 * TX * 4)
    ML, _ = at("MXl", [128, 8, TX], F32R, p2)
    yr = split(YB, YH, YL, F())
    gf = [[], []]
    for m in range(8):
        (b0, t0), = lin("w_gb", (m,), 8, X, 0, XX, xr)
        (b1, t1), = lin("w_or", (m,), 8, (YH, YL), 16, XX, yr)
        i = m % 2
        t = AC.op(lambda e: e.activation(GT[:, i, :], psb(b0), ACT.Sigmoid, bias=vec("bgate", 8 + m)), t0,
                  gf[i], F())
        give(b0, [t])
        t = DVE.op(lambda e: e.tensor_tensor(GT[:, i, :], GT[:, i, :], psb(b1), ALU.mult), t, t1)
        give(b1, [t])
        t = DVE.op(lambda e: e.tensor_tensor(M1[:, m, :], M1[:, m, :], GT[:, i, :], ALU.add), t)
        gf[i] = [t]
        t2 = AC.op(lambda e: e.activation(MH[:, m, :], M1[:, m, :], ACT.Copy), t, F(), yr)
        mr = DVE.op(lambda e: e.tensor_tensor(ML[:, m, :], M1[:, m, :], MH[:, m, :].bitcast(F32),
                                              ALU.subtract), t2, F())
    for m in range(8):
        (b0, t0), = lin("w_out", (m,), 8, (MH, ML), 16, XX, mr)
        t = DVE.op(lambda e: e.tensor_tensor(H[:, m, 16:528], H[:, m, 16:528], psb(b0), ALU.add), t0)
        give(b0, [t])
    barrier()
    HH, p = at("H2h", [128, 8, T1], F32R, P1)
    HL, p = at("H2l", [128, 8, T1], F32R, p)
    TM, p = at("TM2", [128, 2, 512], F32, p)
    e = norm_all("rms", [(16, 256, 0), (272, 256, 0)], lambda k, c: vec("ffn2", k), None, X, 0, p, F())
    e = ffn("f2", X, 0, XX, HH, HL, TM, e[1], lambda m, c0: 0.5, 3)

    for l in range(2):
        mod_step(96)
        both = l == 0
        barrier()
        XH, p = at(f"X2h{l}", [128, 8, 768], F32R, P0)
        XL, p = at(f"X2l{l}", [128, 8, 768], F32R, p)
        P1 = p
        X = (XH, XL)
        mw = [F(), mod_tok[l]]
        blocks = [(16, 256, 0), (272, 256, 0), (528, 256, 1)]
        e = norm_all("ln", blocks, lambda k, c: mod(l, 1, k, c), lambda k, c: mod(l, 0, k, c), X, 16, p, mw)
        xr = e[-1]
        barrier()
        QA, p = at(f"QA{l}", [128, 3, 768], F32, P1)
        KA, p = at(f"KA{l}", [128, 3, 768], F32, p)
        QC, p = at(f"QC{l}", [128, 3, 768], F32, p)
        KC, p = at(f"KC{l}", [128, 1, 768], F32, p)
        VA, p = at(f"VA{l}", [128, 6, 512], F32, p)
        ZU, p = at(f"ZU{l}", [128, 6, 256], F32, p)
        ZV, p = at(f"ZV{l}", [128, 6, 256], F32, p)
        CS, _ = at(f"CSA{l}", [128, 2, 512], F32, p)
        GS, _ = at(f"GS{l}", [128, 256], F32, p + 4096)
        SQT, _ = at(f"SQA{l}", [128, 2, 512], F32, p + 5120)
        RT, _ = at(f"RTA{l}", [128, 1, 512], F32, p + 9216)
        PP = p
        tl = load(CS[:, :, :], A["rope2"], F())
        tlg = load(GS[:, :], A["gsgu"][l], F())
        full = [(16, 512), (528, 256)]
        lat = [(16, 512)]
        qs = full if both else lat
        sqf = [[], []]
        rfree = [[], []]
        qkr = []
        for dst, nm, nt, chs, g, mul in ((QC, "qc", 3, qs, "gq", 0.125), (KC, "kc", 1, full, "gk", 1.0),
                                         (QA, "qa", 3, qs, None, 0.125), (KA, "ka", 3, full, None, 1.0)):
            for m in range(nt):
                res = lin(f"w2_{nm}", (l, m), 8, X, 16, chs, xr)
                flush()
                for (c0, n), (b, t) in zip(chs, res):
                    o = dst[:, m, c0 - 16:c0 - 16 + n]
                    t = AC.op(lambda e: e.activation(o, psb(b, n), ACT.Copy, scale=mul if g is None else 1.0),
                              t, F())
                    give(b, [t])
                    if g is None:
                        qkr.append(t)
                        continue

                    def later(o=o, n=n, t=t, g=g, mul=mul, c0=c0):
                        i = nq[0] % 2
                        nq[0] += 1
                        r, t2 = head_rms(o, n, vec(f"{g}{l}"), mul, t, SQT[:, i, :], i, sqf[i])
                        sqf[i] = [t2]
                        qkr.extend(r)
                        if c0 == 16:
                            idx[0] = 0
                            rr = rope(o, c0, n, CS, 0, PAX, r, RT)
                            qkr.append(rr)
                    pend.append(later)
        tks = [0, 128, 256, 384, 512, 640]
        zt = tks if both else tks[:4]
        for g in range(2):
            lin_tok("w2_v", l * 2 + g, X, tks, vcopy(VA, g * 256), xr)
            flush()

        def gelu(dst):
            def epi(i, b, t):
                return [AC.op(lambda e: e.activation(dst[:, i, :], psb(b, 256), ACT.Gelu_apprx_tanh), t,
                              F())]
            return epi
        lin_tok("w2_z", l * 2, X, zt, gelu(ZU), xr)
        lin_tok("w2_z", l * 2 + 1, X, zt, gelu(ZV), xr)
        ST = SM[:, 32:80]
        for i in range(len(zt)):
            st, ag = ST[:, 8 * (i % 2):8 * (i % 2) + 6], ST[:, 16 + 2 * i:18 + 2 * i]
            zv = ZV[:, i, :]
            v = DVE.op(lambda e: e.bn_stats(st, zv), AC.last(), DVE.last())
            v = DVE.op(lambda e: e.bn_aggr(ag, st), v)
            v = DVE.op(lambda e: e.tensor_scalar(ag[:, 1:2], ag[:, 1:2], 1e-6, None, ALU.add), v)
            y = SM[:, 98 + i % 2:99 + i % 2]
            v = rsqrt(ag[:, 1:2], y, SM[:, 96:97], v)
            v = DVE.op(lambda e: e.tensor_scalar(zv, zv, ag[:, 0:1], y, ALU.subtract, ALU.mult), v)
            v = DVE.op(lambda e: e.tensor_tensor(zv, zv, GS[:, :], ALU.mult), v, tlg)
        barrier()
        OT, p = at(f"OT{l}", [128, 6, 1024], F32, P0)
        WS, p = at(f"WS{l}", [128, 4, 128], F32, p)
        BR, p = at(f"BR{l}", [128, 2, 1024], F32, p)
        Pb, p = at(f"PbA{l}", [128, 2, 768], F32, p)
        assert p <= P1
        PT, p = at(f"PTA{l}", [128, 2, 768], F32, PP)
        BM, p = at(f"BM{l}", [128, 1024], F32, p)
        SQ3, p = at(f"SQ3{l}", [128, 384], F32, p)
        tlw = load(WS[:, :, :], A["wst"][l], F())
        for i in range(len(zt)):
            for g in range(4):
                b, bw = take()
                t = PE.op(lambda e: e.matmul(psb(b, 64), WS[:, g, :], ZV[:, i, g * 64:g * 64 + 64],
                                             start=True, stop=True), bw, tlw, F())
                v = DVE.op(lambda e: e.scalar_tensor_tensor(
                    OT[:, i, 384 + g * 64:448 + g * 64], psb(b, 64), vec(f"bs{l}", g),
                    ZU[:, i, g * 64:g * 64 + 64], ALU.add, ALU.mult), t, F())
                give(b, [v])
        tlm = load(BM[:, :], A["wmask"], F())
        us = []

        def unit(Qn, Kn, h, hk, i, blocks, col, vc, k0, k1, **more):
            r0, rk = 64 * (h % 2), 64 * (hk % 2)
            assert r0 == rk
            return {"q": Qn[r0:r0 + 64, h // 2, i * 128:i * 128 + 128],
                    "k": lambda a, z: Kn[rk:rk + 64, hk // 2, k0 + a:k0 + z], "n": k1 - k0,
                    "blocks": [(c, 128, VA[:, (k0 + c) // 128, vc:vc + 64]) for c in range(0, k1 - k0, 128)],
                    "ready": [], "vready": [], "out": OT[:, i, col:col + 64], **more}

        br_load = {}

        def bias_load(h):
            br_load[h] = load(BR[:, h % 2, :], A["rpbt"][l, h], F(), DVE.last())

        def bias_add(h):
            br_tok[h] = DVE.op(lambda e: e.tensor_tensor(BR[:, h % 2, :], BR[:, h % 2, :], BM[:, :],
                                                         ALU.add), br_load[h], tlm, F())

        bias_load(0)
        bias_add(0)
        us = []
        for h in range(6):
            hs = [unit(QA, KA, h, h, i, None, h * 64, h * 64, 0, 768,
                       bias=BR[:, h % 2, (7 - 2 * i) * 64:(7 - 2 * i) * 64 + 512], bias_ready=h)
                  for i in range(4)]
            if both:
                hs += [unit(QA, KA, h, h, i, None, h * 64, h * 64, 512, 768) for i in (4, 5)]
            if h < 5:
                hs[0]["pre"] = lambda h=h: bias_load(h + 1)
                hs[3]["pre"] = lambda h=h: bias_add(h + 1)
            us += hs
        KD, p = at(f"KD{l}", [128, 2, 768], F32, p)
        f = F()
        kd = []
        for g in range(2):
            for r in range(2):
                kd.append(DVE.op(lambda e: e.tensor_copy(KD[64 * r:64 * r + 64, g, :],
                                                         KC[64 * g:64 * g + 64, 0, :]), f))
        for h in range(6):
            g = h // 3
            r0 = 64 * (h % 2)
            for i in range(6 if both else 4):
                k0 = 0 if i < 4 else 512
                us.append({"q": QC[r0:r0 + 64, h // 2, i * 128:i * 128 + 128],
                           "k": lambda a, z, r0=r0, g=g, k0=k0: KD[r0:r0 + 64, g, k0 + a:k0 + z],
                           "n": 768 - k0,
                           "blocks": [(c, 128, VA[:, (k0 + c) // 128, 384 + g * 64:448 + g * 64])
                                      for c in range(0, 768 - k0, 128)],
                           "ready": [kd], "vready": [], "out": OT[:, i, 640 + h * 64:704 + h * 64]})
        attention(us, Pb, PT)
        f = fence()
        for i in range(len(zt)):
            for g, (a, z) in enumerate(((0, 384), (384, 640), (640, 1024))):
                ss = SM[:, 32 + 3 * i + g:33 + 3 * i + g]
                ac = AC.op(lambda e: e.activation(SQ3[:, 0:z - a], OT[:, i, a:z], ACT.Square,
                                                  accum_out=ss), f, AC.last())
                v = DVE.op(lambda e: e.tensor_scalar(ss, ss, 1.0 / (z - a), 1e-6, ALU.mult, ALU.add), ac)
                y = SM[:, 98 + g % 2:99 + g % 2]
                v = rsqrt(ss, y, SM[:, 96:97], v)
                rdy = DVE.op(lambda e: e.tensor_scalar(OT[:, i, a:z], OT[:, i, a:z], y, None, ALU.mult), v)
        barrier()
        OH, p = at(f"OH{l}", [128, 8, 768], F32R, P1)
        OL, p = at(f"OL{l}", [128, 8, 768], F32R, p)

        def to_o(fi, a, n, b, t):
            g = vec(f"gout{l}", fi)
            t = AC.op(lambda e: e.activation(OH[:, fi, a:a + n], psb(b, n), ACT.Copy, scale=g), t, F())
            v = DVE.op(lambda e: e.scalar_tensor_tensor(OL[:, fi, a:a + n], psb(b, n), g,
                                                        OH[:, fi, a:a + n].bitcast(F32), ALU.mult,
                                                        ALU.subtract), t, F())
            orr.append(v)
            return [v]
        orr = []
        to_features(OT, list(range(len(zt))), range(8), to_o, F())
        nb = [(16, 256, 0), (272, 256, 0)] + ([(528, 256, 1)] if both else [])

        def prescale(ready):
            tt = None
            c1 = 784 if both else 528
            for k in range(8):
                tt = PL.op(lambda e, k=k: e.tensor_scalar(H[:, k, 16:c1], H[:, k, 16:c1], ALPHA, None,
                                                          ALU.mult), ready)
            return tt
        hp = prescale(F())
        for m in range(8):
            res = lin("w2_o", (l, m), 8, (OH, OL), 16, qs, orr[-1])
            for (c0, n), (b, t) in zip(qs, res):
                hk = H[:, m, c0:c0 + n]
                g = mod(l, 2, m, 0 if c0 == 16 else 1)
                t = DVE.op(lambda e: e.scalar_tensor_tensor(hk, psb(b, n), g, hk, ALU.mult, ALU.add), t, hp)
                give(b, [t])
        barrier()
        XH, p = at(f"X3h{l}", [128, 8, 768], F32R, P0)
        XL, p = at(f"X3l{l}", [128, 8, 768], F32R, p)
        X = (XH, XL)
        HH, p2 = at(f"H3h{l}", [128, 8, 768], F32R, p)
        HL, p2 = at(f"H3l{l}", [128, 8, 768], F32R, p2)
        TM, p2 = at(f"TM3{l}", [128, 2, 512], F32, p2)
        norm_all("ln", nb, lambda k, c: vec(f"ln1g{l}", k), lambda k, c: vec(f"ln1b{l}", k), None, 0, p, F())
        barrier()
        e = norm_all("ln", nb, lambda k, c: mod(l, 4, k, c), lambda k, c: mod(l, 3, k, c), X, 16, p, F())
        barrier()
        hp = prescale(F())
        ffn(f"g{l}", X, 16, qs, HH, HL, TM, [e[-1], hp],
            lambda m, c0: mod(l, 5, m, 0 if c0 == 16 else 1), 0)
        barrier()
        norm_all("ln", nb, lambda k, c: vec(f"ln2g{l}", k), lambda k, c: vec(f"ln2b{l}", k), None, 0, p, F())
    s_out = DmaSem(sem("s_out"))
    t = s_out.add(SP, lambda e: e.dma_start(out, H[:, :, 16:528]), fence())
    SP.op(lambda e: e.wait_ge(*t))

    if dry:
        return
    for q in (PE, DVE, AC, PL, SP):
        q.count()
    with nc.Block() as block:
        block.sync(SP.emit)
        block.gpsimd(PL.emit)
        block.scalar(AC.emit)
        block.tensor(PE.emit)
        block.vector(DVE.emit)


nc_ps = []


def _consts():
    f = np.float32
    cf = np.zeros((128, 5, 128), f)
    cf[:, 0, :] = 1.0 / 1024
    for a in (0, 64):
        cf[a:a + 64, 1, a:a + 64] = 1.0 / 64
    cf[:, 2, :] = np.eye(128)
    q = np.arange(128)
    cf[(q + 64) % 128, 3, q] = 1.0
    cf[q ^ 16, 4, q] = 1.0
    cb = np.zeros((128, 2, 128), np.uint16)
    cb[q, 0, q] = 0x3F80
    cb[:, 1, :] = np.where(q[None, :] > q[:, None], 0xF14A, 0)
    sel = np.zeros((128, 16, 128), np.uint16)
    for h in range(16):
        for a in (0, 32, 64):
            sel[a + h, h, :] = 0x3F80
    half = 64
    inv = (f(10000.0) ** (-(np.arange(half, dtype=f) / f(half)))).astype(f)
    ang = (np.arange(T1, dtype=f)[None, :] * inv[:, None]).astype(f)
    c, s = np.cos(ang.astype(np.float64)), np.sin(ang.astype(np.float64))
    rope1 = np.stack([np.concatenate([c, c]), np.concatenate([-s, s])], 1).astype(f)
    inv = (f(1.0) / (f(10000.0) ** (np.arange(16, dtype=f) / f(16)))).astype(f)
    t = np.arange(512)
    pos = np.stack([t // 64, t % 64]).astype(f)
    d = np.arange(64)
    ang = (pos[d // 32] * inv[d % 16][:, None]).astype(f).astype(np.float64)
    sg = np.where((d % 32) < 16, -1.0, 1.0)[:, None]
    rope2 = np.stack([np.tile(np.cos(ang), (2, 1)), np.tile(np.sin(ang) * sg, (2, 1))], 1).astype(f)
    lg = np.log1p(-np.exp2(-5.0 - np.arange(4)))
    df = (np.arange(T1)[None, :] - np.arange(128)[:, None]).astype(np.float64)
    decay = np.where(df[:, None, :] >= 0, np.exp(lg[None, :, None] * np.maximum(df, 0)[:, None, :]), 0.0)
    decay = (decay * 128.0 ** -0.5).astype(f)
    cc = np.arange(64)
    cs = np.clip(cc - 8, 0, 48)
    ok = (cc[None, :] >= cs[:, None]) & (cc[None, :] < cs[:, None] + 16)
    wm = np.where(ok, 0.0, -1e30).astype(f)
    wmask = np.ascontiguousarray(np.broadcast_to(np.tile(wm, (2, 1))[:, None, :], (128, 16, 64))).reshape(128, 1024)
    return {"cf": cf, "cb": cb, "sel": sel,
            "rope1": rope1, "rope2": rope2, "decay": decay, "wmask": wmask}


def _layout(i):
    def fm(w):
        k, n = w.shape
        return np.ascontiguousarray(w.reshape(k // 128, 128, n // 128, 128).transpose(2, 1, 0, 3)).reshape(
            n // 128, 128, k)

    def tm(w):
        n = w.shape[1]
        return np.ascontiguousarray(w.reshape(2, 4, 128, n // 256, 256).transpose(3, 0, 2, 1, 4)).reshape(
            n // 256, 2, 128, 1024)

    def cols(v):
        return v.reshape(-1, 128).T

    a = _consts()
    x = np.concatenate([i["meta_tokens"], i["x"][0]], 0)
    a["x0"] = np.ascontiguousarray(x.T.reshape(8, 128, T1).transpose(1, 0, 2))
    a["ctx"] = np.ascontiguousarray(i["ctx_2"][0].T.reshape(8, 128, TC).transpose(1, 0, 2))
    w = i["w_in"][0]
    at, parts = 0, {}
    for n, s in (("fq", 1024), ("fk", 1024), ("fv", 1024), ("ff", 16), ("rq", 512), ("rk", 512), ("rv", 1024),
                 ("rg", 1024), ("ga", 1024), ("gb", 1024)):
        parts[n] = w[:, at:at + s]
        at += s
    parts["ff"] = np.pad(parts["ff"], ((0, 0), (0, 112)))
    for n, v in parts.items():
        a["w_" + n] = tm(v) if n in ("fv", "rv") else fm(v)
    a["w_of"], a["w_or"], a["w_out"] = fm(i["w_o_fox"][0]), fm(i["w_o_ret"][0]), fm(i["w_out"][0])
    for t, wi, wo in (("f1", i["w_ffn1_in"][0], i["w_ffn1_out"][0]), ("f2", i["w_ffn2_in"][0], i["w_ffn2_out"][0]),
                      ("g0", i["w_ffn_in_2"][0], i["w_ffn_out_2"][0]),
                      ("g1", i["w_ffn_in_2"][1], i["w_ffn_out_2"][1])):
        a[t + "_in"] = fm(wi)
        for c, (j0, nj) in enumerate(CH):
            a[f"{t}_out{c}"] = fm(wo[j0 * 128:(j0 + nj) * 128])
    a["wmod"] = np.stack([fm(i["w_mod_2"][l]) for l in range(2)])
    names = (("qa", 384), ("ka", 384), ("va", 384), ("z", 512), ("qc", 384), ("kc", 128), ("vc", 128))
    two = {}
    for l in range(2):
        at = 0
        for n, s in names:
            two[n, l] = i["w_in_2"][l][:, at:at + s]
            at += s
    for n in ("qa", "ka", "qc", "kc"):
        a["w2_" + n] = np.stack([fm(two[n, l]) for l in range(2)])
    a["w2_v"] = np.concatenate([tm(np.concatenate([two["va", l], two["vc", l]], 1)) for l in range(2)])
    a["w2_z"] = np.concatenate([tm(two["z", l]) for l in range(2)])
    a["w2_o"] = np.stack([fm(i["w_o_2"][l]) for l in range(2)])
    a["wst"] = np.ascontiguousarray(i["w_s_2"].transpose(0, 3, 1, 2))
    a["gsgu"] = np.ascontiguousarray(np.broadcast_to(i["g_sgu_2"][:, None, :], (2, 128, 256)))
    q = np.arange(128)[:, None, None]
    j = np.arange(16)[None, :, None]
    kc = np.arange(64)[None, None, :]
    dr = np.clip(j - q // 64, 0, 14)
    dc = np.clip(kc - q % 64 + 15, 0, 30)
    a["rpbt"] = np.ascontiguousarray(i["rpb_2"][:, :, dr, dc]).reshape(2, 6, 128, 1024)
    v = np.zeros((128, NVEC), np.float32)

    def put(name, arr):
        s, n = VEC[name]
        v[:, s:s + n] = arr
    put("ffn1", cols(i["norm_ffn1"][0]))
    put("mix", cols(i["norm_mix"][0]))
    put("ffn2", cols(i["norm_ffn2"][0]))
    put("bgate", cols(i["b_gate"][0]))
    put("retgn", cols(i["ret_gn"][0]))
    put("fq", np.tile(i["fox_q_norm"][0], 2)[:, None])
    put("fk", np.tile(i["fox_k_norm"][0], 2)[:, None])
    put("bf", np.pad(i["b_forget"][0], (0, 112))[:, None])
    put("c", np.stack([cols(i["c_2"][0]), cols(i["c_ctx_2"])], 2).reshape(128, 16))
    for l in range(2):
        put(f"bmod{l}", cols(i["b_mod_2"][l]))
        put(f"gq{l}", np.tile(i["g_q_2"][l], 2)[:, None])
        put(f"gk{l}", np.tile(i["g_k_2"][l], 2)[:, None])
        put(f"gout{l}", cols(i["g_out_2"][l]))
        for n in ("ln1_g", "ln1_b", "ln2_g", "ln2_b"):
            put(n.replace("_", "") + str(l), cols(i[n + "_2"][l]))
        put(f"bs{l}", i["b_s_2"][l].T)
    a["vec"] = v
    return a


def kernel(**inputs):
    import concourse.bacc as bacc
    from concourse.bass_utils import run_bass_kernel_spmd
    arrays = {"in_" + k: np.ascontiguousarray(v)
              for k, v in _layout({k: np.asarray(v) for k, v in inputs.items()}).items()}
    nc = bacc.Bacc("TRN2", target_bir_lowering=False, num_devices=1)
    A = {k[3:]: nc.dram_tensor(k, v.shape, mybir.dt.from_np(v.dtype), kind="ExternalInput").ap()
         for k, v in arrays.items()}
    out = nc.dram_tensor("out", (128, 8, TX), F32, kind="ExternalOutput").ap()
    nc_ps.clear()
    build(nc, A, out)
    r = run_bass_kernel_spmd(nc, [arrays], core_ids=[0])
    o = r.results[0]["out"]
    return np.ascontiguousarray(o.transpose(2, 1, 0)).reshape(1, TX, D)
```

```python
import concourse.bass as bass
from concourse import mybir
import numpy as np

F32 = mybir.dt.float32
F32R = mybir.dt.float32r
BF16 = mybir.dt.bfloat16
U16 = mybir.dt.uint16
ACT = mybir.ActivationFunctionType
ALU = mybir.AluOpType
AX = mybir.AxisListType.X

D = 1024
KT = 8
NMETA = 16
TX = 512
TC = 256
T1 = NMETA + TX
NFF = 22
CH = [(0, 8), (8, 7), (15, 7)]
ALPHA = (2 * 2) ** 0.25
GAMMA = [1.0 - 2.0 ** (-5 - h) for h in range(4)]
BASE = 16512

VEC = {}
_n = 0
for _name, _w in [("ffn1", 8), ("mix", 8), ("ffn2", 8), ("bgate", 16), ("retgn", 8), ("fq", 1), ("fk", 1),
                  ("bf", 1), ("c", 16), ("bmod0", 48), ("bmod1", 48), ("gq0", 1), ("gk0", 1), ("gq1", 1),
                  ("gk1", 1), ("gout0", 8), ("gout1", 8), ("ln1g0", 8), ("ln1g1", 8), ("ln1b0", 8),
                  ("ln1b1", 8), ("ln2g0", 8), ("ln2g1", 8), ("ln2b0", 8), ("ln2b1", 8), ("bs0", 4), ("bs1", 4)]:
    VEC[_name] = (_n, _w)
    _n += _w
NVEC = _n


class Tok:

    def __init__(self, eng, idx):
        self.eng, self.idx = eng, idx


class Call:

    def matmul(self, *a, **k):
        self.make = lambda e: e.matmul(*a, **k)

    def transpose(self, *a, **k):
        self.make = lambda e: e.transpose(*a, **k)

    def activation(self, *a, **k):
        self.make = lambda e: e.activation(*a, **k)

    def tensor_tensor(self, *a, **k):
        self.make = lambda e: e.tensor_tensor(*a, **k)

    def tensor_scalar(self, *a, **k):
        self.make = lambda e: e.tensor_scalar(*a, **k)

    def scalar_tensor_tensor(self, *a, **k):
        self.make = lambda e: e.scalar_tensor_tensor(*a, **k)

    def tensor_tensor_scan(self, *a, **k):
        self.make = lambda e: e.tensor_tensor_scan(*a, **k)

    def tensor_reduce(self, *a, **k):
        self.make = lambda e: e.tensor_reduce(*a, **k)

    def tensor_copy(self, *a, **k):
        self.make = lambda e: e.tensor_copy(*a, **k)

    def reciprocal(self, *a, **k):
        self.make = lambda e: e.reciprocal(*a, **k)

    def bn_stats(self, *a, **k):
        self.make = lambda e: e.bn_stats(*a, **k)

    def bn_aggr(self, *a, **k):
        self.make = lambda e: e.bn_aggr(*a, **k)

    def memset(self, *a, **k):
        self.make = lambda e: e.memset(*a, **k)

    def dma_start(self, *a, **k):
        self.make = lambda e: e.dma_start(*a, **k)

    def wait_ge(self, *a, **k):
        self.make = lambda e: e.wait_ge(*a, **k)


class Queue:

    def __init__(self, name, sem):
        self.name, self.sem, self.items, self.marked = name, sem, [], set()

    def op(self, fn, *waits, dma=None):
        ws = []
        call = Call()
        fn(call)

        def flat(w):
            if w is None:
                return
            if isinstance(w, (list, tuple)) and not (len(w) == 2 and isinstance(w[1], int)):
                for x in w:
                    flat(x)
            else:
                ws.append(w)
        flat(list(waits))
        for w in ws:
            if isinstance(w, Tok):
                w.eng.marked.add(w.idx)
        self.items.append((ws, call.make, dma))
        return Tok(self, len(self.items) - 1)

    def last(self):
        n = len(self.items) - 1
        while n >= 0 and self.items[n][2] is not None:
            n -= 1
        return Tok(self, n) if n >= 0 else None

    def count(self):
        self.value, n = {}, 0
        for i in sorted(self.marked):
            n += 1
            self.value[i] = n

    def emit(self, e):
        seen = {}
        for i, (ws, make, dma) in enumerate(self.items):
            need = {}
            for w in ws:
                sem, v = (w.eng.sem, w.eng.value[w.idx]) if isinstance(w, Tok) else w
                k = id(sem)
                if v > seen.get(k, 0) and v > need.get(k, (None, 0))[1]:
                    need[k] = (sem, v)
            for k, (sem, v) in need.items():
                e.wait_ge(sem, v)
                seen[k] = v
            inst = make(e)
            if dma is not None:
                inst.then_inc(dma, 16)
            if i in self.marked:
                inst.then_inc(self.sem, 1)


class DmaSem:

    def __init__(self, sem):
        self.sem, self.n = sem, 0

    def add(self, q, fn, *waits):
        q.op(fn, *waits, dma=self.sem)
        self.n += 16
        return (self.sem, self.n)


def build(nc, A, out):
    order = []
    _program(nc, A, out, order, True)
    _program(nc, A, out, order, False)


def _program(nc, A, out, order, dry):
    nosem = [0]

    def sem(name):
        if dry:
            nosem[0] += 1
            return nosem[0]
        return nc.alloc_semaphore(name)

    PE, DVE, AC, PL, SP = (Queue(n, sem("s_" + n)) for n in ("pe", "dve", "act", "pool", "sp"))

    tag = ["d" if dry else "r"]

    def at(name, shape, dt, offset):
        assert offset % 32 == 0, (name, offset)
        t = nc.alloc_sbuf_tensor_at(f"{tag[0]}_{name}", shape, dt, offset=BASE + offset)
        size = 4
        for s in shape[1:]:
            size *= s
        if dt in (BF16, U16):
            size //= 2
        ends.append((name, offset, offset + size))
        assert BASE + offset + size <= 229368, (name, offset + size)
        return t, (offset + size + 31) // 32 * 32

    ends = []
    H, p = at("H", [128, KT, NMETA + TX + TC], F32, 0)
    NW, NS, AHEAD = 4, 3, 2
    Wf, p = at("Wf", [128, NW, 1024], F32, p)
    Wh, p = at("Wh", [128, NS, 1024], F32R, p)
    Wl, p = at("Wl", [128, NS, 1024], F32R, p)
    V, p = at("V", [128, NVEC], F32, p)
    CF, p = at("CF", [128, 5, 128], F32, p)
    CB, p = at("CB", [128, 2, 128], U16, p)
    SC, p = at("SC", [128, 8, 2], F32, p)
    MOD, p = at("MOD", [128, 2, 48, 2], F32, p)
    RS, p = at("RS", [128, 3, 528], F32, p)
    SM, p = at("SM", [128, 112], F32, p)
    P0 = p
    ONES, BLK, IDF, PRM, PAX = (CF[:, i, :] for i in range(5))
    IDB, MSKB = CB[:, 0, :].bitcast(BF16), CB[:, 1, :].bitcast(BF16)

    def vec(name, k=0):
        return V[:, VEC[name][0] + k:VEC[name][0] + k + 1]

    if dry:
        PS = nc_ps[0] if nc_ps else None
        if PS is None:
            PS = nc.alloc_psum_tensor("PS", [128, 8, 512], F32)
            nc_ps.append(PS)
    else:
        PS = nc_ps[0]

    bank = {"next": 0, "free": [[] for _ in range(8)], "out": [False] * 8}

    shared = {"a": [0, 2], "b": [4], "c": [6], None: [7]}
    turn = {"a": 0, "b": 0, "c": 0, None: 0}
    divided = [False]

    def take(n=1, part=None):
        if divided[0]:
            b = shared[part][turn[part] % len(shared[part])]
            turn[part] += 1
            w = []
            for i in range(b, b + n):
                assert not bank["out"][i], "bank in use"
                bank["out"][i] = True
                w += bank["free"][i]
            return b, w
        b = bank["next"]
        while (n == 2 and b % 2) or any(bank["out"][b:b + n]):
            b = (b + 1) % 8
        bank["next"] = (b + n) % 8
        w = []
        for i in range(b, b + n):
            assert not bank["out"][i], "bank in use"
            bank["out"][i] = True
            w += bank["free"][i]
        return b, w

    def give(b, toks, n=1):
        for i in range(b, b + n):
            assert bank["out"][i]
            bank["out"][i] = False
            bank["free"][i] = list(toks)

    def psb(b, n=512, p=128):
        return PS[0:p, b, 0:n]

    def psb2(b, a, z, p=128):
        return PS[:, :, :].rearrange("p b n -> p (b n)")[0:p, b * 512 + a:b * 512 + z]

    def fence():
        return [q.last() for q in (PE, DVE, AC, PL) if q.last()]

    fence_tok = [[]]

    def barrier():
        f = fence()
        fence_tok[0] = f
        for q in (PE, DVE, AC, PL):
            q.fence = f
        return f

    def F():
        return fence_tok[0]

    wsem = [DmaSem(sem(f"s_w{i}")) for i in range(NW)]
    W = {"loaded": 0, "split": 0, "used": 0, "nsplit": 0}
    u_arrived, u_ready, u_slot, wf_free, ws_free = {}, {}, {}, {}, {}

    def w_pump():
        moved = True
        while moved:
            moved = False
            i = W["loaded"]
            if i < len(order) and (i < NW or i - NW in wf_free):
                name, idx, cols, raw = order[i]
                src = A[name]
                for j in idx:
                    src = src[j]
                u_arrived[i] = wsem[i % NW].add(SP, lambda e: e.dma_start(Wf[:, i % NW, 0:cols], src),
                                                wf_free.get(i - NW))
                W["loaded"] += 1
                moved = True
            i = W["split"]
            if i < W["loaded"] and i <= W["used"] + AHEAD:
                name, idx, cols, raw = order[i]
                f = Wf[:, i % NW, 0:cols]
                if raw:
                    u_slot[i], u_ready[i] = i % NW, u_arrived[i]
                elif W["nsplit"] < NS or W["nsplit"] - NS in ws_free:
                    n = W["nsplit"]
                    s = n % NS
                    h, l = Wh[:, s, 0:cols], Wl[:, s, 0:cols]
                    hi = AC.op(lambda e: e.activation(h, f, ACT.Copy), u_arrived[i], ws_free.get(n - NS))
                    lo = DVE.op(lambda e: e.tensor_tensor(l, f, h.bitcast(F32), ALU.subtract), hi)
                    u_slot[i], u_ready[i] = s, lo
                    wf_free[i] = lo
                    W["nsplit"] += 1
                else:
                    continue
                W["split"] += 1
                moved = True

    def w_get(name, idx, cols, raw=False):
        i = W["used"]
        W["used"] += 1
        if dry:
            order.append((name, idx, cols, raw))
            return i, 0, None
        assert order[i] == (name, idx, cols, raw)
        w_pump()
        return i, u_slot[i], u_ready[i]

    def w_done(i, tok, raw=False):
        if dry:
            return
        if raw:
            wf_free[i] = tok
        else:
            ws_free[sum(1 for u in order[:i] if not u[3])] = tok
        w_pump()

    def mm3(o, wh, wl, xh, xl, first, last, *waits, wmain=True):
        PE.op(lambda e: e.matmul(o, wh, xh, start=first, stop=False), *waits)
        PE.op(lambda e: e.matmul(o, wh, xl, start=False, stop=False))
        return PE.op(lambda e: e.matmul(o, wl, xh, start=False, stop=last))

    def over(toks, c0, n, k):
        return [tk[k] for a, w, tk in toks if a < c0 + n and c0 < a + w]

    def lin(name, idx, kt, X, off, chunks, *waits, each=None, by=()):
        u, s, ready = w_get(name, idx, kt * 128)
        res = []
        for c0, n in chunks:
            b, bw = take()
            for k in range(kt):
                w = Wh[:, s, k * 128:k * 128 + 128], Wl[:, s, k * 128:k * 128 + 128]
                t = mm3(psb(b, n), *w, X[0][:, k, c0 - off:c0 - off + n], X[1][:, k, c0 - off:c0 - off + n],
                        k == 0, k == kt - 1, ready, bw, waits, over(by, c0, n, k))
            if each:
                each(c0, n, b, t)
            res.append((b, t))
        w_done(u, t)
        return res

    def lin_pair(name, idx, kt, X, off, chunks, by):
        u = [w_get(name, i, kt * 128) for i in idx]
        bs = [[take() for _ in chunks] for _ in u]
        for ks in (range(kt - 1), (kt - 1,)):
            for (un, s, ready), bb in zip(u, bs):
                for (c0, n), (b, bw) in zip(chunks, bb):
                    for k in ks:
                        w = Wh[:, s, k * 128:k * 128 + 128], Wl[:, s, k * 128:k * 128 + 128]
                        t = mm3(psb(b, n), *w, X[0][:, k, c0 - off:c0 - off + n],
                                X[1][:, k, c0 - off:c0 - off + n], k == 0, k == kt - 1, ready, bw,
                                over(by, c0, n, k))
        for un, s, ready in u:
            w_done(un, t)
        return [[(b, t) for b, bw in bb] for bb in bs]

    def lin_tok(name, g, X, tiles, epi, *waits, by=(), shift=0):
        u0, s0, r0 = w_get(name, (g, 0), 1024)
        u1, s1, r1 = w_get(name, (g, 1), 1024)
        for i, c0 in enumerate(tiles):
            b, bw = take()
            for k in range(8):
                s = (s0, s1)[k // 4]
                a = (k % 4) * 256
                o = psb(b, 256)
                xh, xl = X[0][:, k, c0:c0 + 128], X[1][:, k, c0:c0 + 128]
                wh, wl = Wh[:, s, a:a + 256], Wl[:, s, a:a + 256]
                t = mm3(o, xh, xl, wh, wl, k == 0, k == 7, r0, r1, bw, waits, over(by, c0 + shift, 128, k))
            give(b, epi(i, b, t))
        w_done(u0, t)
        w_done(u1, t)

    s_in = [DmaSem(sem(f"s_in{i}")) for i in range(4)]
    x_in = []
    for i in range(4):
        x_in.append(s_in[i].add(SP, lambda e: e.dma_start(H[:, 2 * i:2 * i + 2, 0:T1],
                                                          A["x0"][:, 2 * i:2 * i + 2, :])))
    s_con = DmaSem(sem("s_con"))
    for dst, src in ((V[:, :], A["vec"]), (CF[:, :, :], A["cf"]), (CB[:, :, :], A["cb"])):
        t_in = s_con.add(AC, lambda e, dst=dst, src=src: e.dma_start(dst, src))
    s_ctx = DmaSem(sem("s_ctx"))
    t_ctx = s_ctx.add(PL, lambda e: e.dma_start(H[:, :, T1:T1 + TC], A["ctx"]))
    for q in (PE, DVE, AC, PL):
        q.fence = []
    n_load = []

    def load(dst, src, *waits):
        n_load.append(DmaSem(sem(f"s_ld{len(n_load)}")))
        return n_load[-1].add(PL, lambda e: e.dma_start(dst, src), *waits)

    c0v = VEC["c"][0]
    SCT = SM[:, 80:96]
    t = AC.op(lambda e: e.activation(SCT, V[:, c0v:c0v + 16], ACT.Silu), t_in)
    t_sc = DVE.op(lambda e: e.tensor_copy(SC[:, :, :].rearrange("p k c -> p (k c)"), SCT), t)
    mods = [(l, m) for l in range(2) for m in range(48)]
    mod_tok = [None, None]

    def mod_until(l, part):
        while mods and mods[0] < (l, part * 8 + 8):
            mod_step()
        return mod_tok[l]

    def mod_step(count=1):
        for _ in range(count):
            if not mods:
                return
            l, m = mods.pop(0)
            u, s, ready = w_get("wmod", (l, m), 1024, True)
            b, bw = take()
            for k in range(8):
                t = PE.op(lambda e, k=k: e.matmul(psb(b, 2), Wf[:, s, k * 128:k * 128 + 128], SC[:, k, :],
                                                  start=k == 0, stop=k == 7), ready, bw, t_sc)
            w_done(u, t, True)
            part, name = m // 8, f"bmod{l}"
            one = 1.0 if part in (1, 4) else 0.0
            t = DVE.op(lambda e: e.tensor_scalar(MOD[:, l, m, :], psb(b, 2), vec(name, m), one, ALU.add,
                                                 ALU.add), t)
            give(b, [t])
            mod_tok[l] = t

    def mod(l, part, k, c):
        return MOD[:, l, part * 8 + k, c:c + 1]

    def rsqrt(x, y, t, ready, mul=1.0, *waits):
        return newton(x, y, t, AC.op(lambda e: e.activation(y, x, ACT.Sqrt), ready, waits), mul)

    def newton(x, y, t, a, mul):
        a = DVE.op(lambda e: e.reciprocal(y, y), a)
        a = DVE.op(lambda e: e.tensor_tensor(t, y, y, ALU.mult), a)
        a = DVE.op(lambda e: e.scalar_tensor_tensor(t, t, -0.5 * mul, x, ALU.mult, ALU.mult), a)
        return DVE.op(lambda e: e.scalar_tensor_tensor(y, t, 1.5 * mul, y, ALU.add, ALU.mult), a)

    def norm_all(kind, blocks, scale, bias, dst, off, tmp, ready, free=(), mods_per=0):
        XC, q = at(f"XC{tmp}_{nid[0]}", [128, 2, 8, 264], F32, tmp)
        SQ, q = at(f"SQ{tmp}_{nid[0]}", [128, 8, 264], F32, q)
        MU, q = at(f"MU{tmp}_{nid[0]}", [128, 2, 264], F32, q)
        nid[0] += 1
        S = [dict() for _ in blocks]
        sq_read = [None] * 8

        def view(i):
            c0, n, c = blocks[i]
            hs = [H[:, k, c0:c0 + n] for k in range(8)]
            xc = [XC[:, i % 2, k, 0:n] for k in range(8)]
            return c0, n, c, hs, xc, (hs if kind == "rms" else xc)

        def statistics(i):
            c0, n, c, hs, xc, src = view(i)
            before = S[i - 2]["read"] if i >= 2 else [None] * 8
            xs = [None] * 8
            if kind == "ln":
                b, bw = take()
                for k in range(8):
                    t = PE.op(lambda e, k=k: e.matmul(psb(b, n), ONES, hs[k], start=k == 0, stop=k == 7),
                              bw, over(ready, c0, n, k))
                mu = MU[:, i % 2, 0:n]
                m = AC.op(lambda e: e.activation(mu, psb(b, n), ACT.Copy), t, free, before)
                give(b, [m])
                for k in range(8):
                    q = PL if k % 3 == 2 else DVE
                    xs[k] = q.op(lambda e, k=k: e.tensor_tensor(xc[k], hs[k], mu, ALU.subtract), m,
                                 before[k], free)
            b, bw = take()
            for k in range(8):
                t = AC.op(lambda e, k=k: e.activation(SQ[:, k, 0:n], src[k], ACT.Square), xs[k], free,
                          sq_read[k], over(ready, c0, n, k))
                t = PE.op(lambda e, k=k: e.matmul(psb(b, n), ONES, SQ[:, k, 0:n], start=k == 0, stop=k == 7),
                          t, bw)
                sq_read[k] = t
            S[i].update(b=b, t=t, xs=xs)

        def root(i):
            c0, n, c, hs, xc, src = view(i)
            a = 264 * (i % 2)
            x, y, w = (RS[:, j, a:a + n] for j in range(3))
            b = S[i]["b"]
            t = DVE.op(lambda e: e.tensor_scalar(x, psb(b, n), 1e-6, None, ALU.add), S[i]["t"], free,
                       S[i - 2]["scaled"] if i >= 2 else None)
            give(b, [t])
            S[i].update(r=y, t=rsqrt(x, y, w, t))

        def apply(i):
            c0, n, c, hs, xc, src = view(i)
            r, t, read, end = S[i]["r"], S[i]["t"], [], []
            before = S[i - 2]["read"] if i >= 2 and kind == "rms" else [None] * 8
            for k in range(8):
                u = DVE.op(lambda e, k=k: e.scalar_tensor_tensor(xc[k], src[k], scale(k, c), r, ALU.mult,
                                                                 ALU.mult), t, S[i]["xs"][k], sq_read[k],
                           before[k], free)
                S[i]["scaled"] = u
                if dst is None:
                    u = AC.op(lambda e, k=k: e.activation(hs[k], xc[k], ACT.Identity, bias=bias(k, c)), u)
                    read.append([u])
                    end.append(u)
                    continue
                xh, xl = dst[0][:, k, c0 - off:c0 - off + n], dst[1][:, k, c0 - off:c0 - off + n]
                q = PL if k % 2 else DVE
                if bias is None:
                    u = AC.op(lambda e, k=k, xh=xh: e.activation(xh, xc[k], ACT.Copy), u, free)
                    v = q.op(lambda e, k=k, xh=xh, xl=xl: e.tensor_tensor(
                        xl, xc[k], xh.bitcast(F32), ALU.subtract), u, free)
                else:
                    u = AC.op(lambda e, k=k, xh=xh: e.activation(xh, xc[k], ACT.Identity,
                                                                 bias=bias(k, c)), u, free)
                    v = DVE.op(lambda e, k=k, xh=xh, xl=xl: e.scalar_tensor_tensor(
                        xl, xc[k], bias(k, c), xh.bitcast(F32), ALU.add, ALU.subtract), u, free)
                read.append([u, v])
                end.append(v)
            S[i]["read"] = read
            return c0, n, end

        out_toks = []
        statistics(0)
        mod_step(mods_per)
        for i in range(len(blocks)):
            if i + 1 < len(blocks):
                statistics(i + 1)
                mod_step(mods_per)
            root(i)
            out_toks.append(apply(i))
        return out_toks

    nid = [0]

    def ffn(tagw, X, off, chunks, HH, HL, TM, by, ready, gate, mods_per):
        free = [[], []]
        n_tm = [0]
        hw = {}
        hid_free = []
        h_end = {c0: [] for c0, n in chunks}
        for ci, (j0, nj) in enumerate(CH):
            hid = [(c0, n, []) for c0, n in chunks]

            def finish(j, ra, rb):
                for (c0, n), (ba, ta), (bb, tb), (_, _, done) in zip(chunks, ra, rb, hid):
                    i = n_tm[0] % 2
                    n_tm[0] += 1
                    x = TM[:, i, 0:n]
                    t = AC.op(lambda e: e.activation(x, psb(ba, n), ACT.Silu), ta, free[i], F())
                    give(ba, [t])
                    u = DVE.op(lambda e: e.tensor_tensor(x, x, psb(bb, n), ALU.mult), t, tb)
                    give(bb, [u])
                    hh, hl = HH[:, j, c0 - off:c0 - off + n], HL[:, j, c0 - off:c0 - off + n]
                    v = AC.op(lambda e: e.activation(hh, x, ACT.Copy), u, hid_free)
                    w = PL.op(lambda e: e.tensor_tensor(hl, x, hh.bitcast(F32), ALU.subtract), v, hid_free)
                    free[i] = [w]
                    done.append(w)

            for j in range(nj):
                ra = lin(tagw + "_in", (j0 + j,), 8, X, off, chunks, by=by)
                rb = lin(tagw + "_in", (NFF + j0 + j,), 8, X, off, chunks, by=by)
                finish(j, ra, rb)
            mod_step(mods_per)
            pair = None
            for m in range(8):
                if m == 0:
                    pair = lin_pair(f"{tagw}_out{ci}", ((0,), (1,)), nj, (HH, HL), off, chunks, hid)
                r = pair[m] if m < 2 else lin(f"{tagw}_out{ci}", (m,), nj, (HH, HL), off, chunks)
                for (c0, n), (b, t) in zip(chunks, r):
                    hk = H[:, m, c0:c0 + n]
                    g = gate(m, c0)
                    t2 = DVE.op(lambda e: e.scalar_tensor_tensor(hk, psb(b, n), g, hk, ALU.mult, ALU.add),
                                t, hw.get((m, c0)), ready)
                    give(b, [t2])
                    hw[m, c0] = t2
                    if ci == len(CH) - 1:
                        h_end[c0].append(t2)
                    hid_free = [t]
        return [(c0, n, h_end[c0]) for c0, n in chunks]

    def attention(units, Pb, PT, values, done=None):
        st = [dict() for _ in units]
        pfree = [[], [], []]
        ptfree = [[], []]

        def step_a(u):
            d, s = units[u], st[u]
            i = u % 3
            if "pre" in d:
                d["pre"]()
            b, bw = take(2, "a")
            n = d["n"]
            parts = [(0, max(256, min(n, 512)))] + ([(512, n)] if n > 512 else [])
            for a, z in parts:
                extra = [x for x in d.get("add", []) if x[2] >= a and x[2] < z]
                (q1, k1), (q2, k2) = d["qk"](a, z)
                PE.op(lambda e: e.matmul(psb2(b, a, z), q1, k1, start=True, stop=False), bw, d["ready"], F())
                t = PE.op(lambda e: e.matmul(psb2(b, a, z), q2, k2, start=False, stop=not extra))
                d["used"][:] = [t]
                for x in extra:
                    rhs = x[1](x[2], x[3])
                    t = PE.op(lambda e: e.matmul(psb2(b, x[2], x[3]), x[0], rhs, start=False,
                                                 stop=x is extra[-1]), d["ready"])
            lg = psb2(b, 0, n)
            if "bias" in d:
                m = d["bias"]
                t = DVE.op(lambda e: e.tensor_tensor(psb2(b, 0, 512), psb2(b, 0, 512), m, ALU.add), t,
                           br_tok[d["bias_ready"]])
            mx = SM[:, u % 4:u % 4 + 1]
            s["mx_t"] = DVE.op(lambda e: e.tensor_reduce(mx, lg, AX, ALU.max, negate=True), t,
                               st[u - 4]["exp"] if u >= 4 else None)
            s["a"] = (i, b, n, lg, mx)

        def step_exp(u):
            s = st[u]
            i, b, n, lg, mx = s["a"]
            rs = SM[:, 4 + u % 4:5 + u % 4]
            t = AC.op(lambda e: e.activation(Pb[:, i, 0:n], lg, ACT.Exp, bias=mx, accum_out=rs), s["mx_t"],
                      pfree[i], st[u - 4]["rc_t"] if u >= 4 else None)
            give(b, [t], 2)
            s["exp"], s["rs"] = t, rs

        def step_b(u):
            d, s = units[u], st[u]
            i, i3 = u % 2, u % 3
            b, bw = take(2, "b")
            full = [x for x in d["blocks"] if x[1] == 128]
            part = [x for x in d["blocks"] if x[1] < 128]
            for j, (c, w, v) in enumerate(full):
                t = PE.op(lambda e: e.transpose(psb2(b, j * 128, j * 128 + 128), Pb[:, i3, c:c + 128], IDF),
                          s["exp"], bw)
            for j, (c, w, v) in enumerate(part):
                t = PE.op(lambda e: e.matmul(psb2(b, 512, 640, w), Pb[:, i3, c:c + w], IDF, start=True,
                                             stop=True), s["exp"], bw)
            n = len(full) * 128
            q = AC if u % 2 or "bias" in d else DVE
            cp = (lambda e, o, x: e.activation(o, x, ACT.Copy)) if q is AC else (
                lambda e, o, x: e.tensor_copy(o, x))
            t2 = q.op(lambda e: cp(e, PT[:, i, 0:n], psb2(b, 0, n)), t, ptfree[i], F())
            s["pt"] = [t2]
            if part:
                w = part[0][1]
                t2 = q.op(lambda e: cp(e, PT[0:w, i, 512:640], psb2(b, 512, 640, w)), t)
                s["pt"] = [t2]
            give(b, [t2], 2)
            rc = SM[:, 8 + 2 * (u % 4):9 + 2 * (u % 4)]
            s["rc"] = rc
            s["rc_t"] = DVE.op(lambda e: e.reciprocal(rc, s["rs"]), s["exp"],
                               st[u - 4]["o"] if u >= 4 else None)
            pfree[i3] = [t, s["exp"]]

        def step_c(u):
            d, s = units[u], st[u]
            i = u % 2
            b, bw = take(1, "c")
            full = [x for x in d["blocks"] if x[1] == 128]
            part = [x for x in d["blocks"] if x[1] < 128]
            o = psb(b, 64)
            seq = [(PT[:, i, j * 128:j * 128 + 128], x[2]) for j, x in enumerate(full)]
            seq += [(PT[0:x[1], i, 512:640], x[2]) for x in part]
            for j, (l, r) in enumerate(seq):
                t = PE.op(lambda e: e.matmul(o, l, r, start=j == 0, stop=j == len(seq) - 1), s["pt"],
                          bw,
                          d["vready"])
            ptfree[i] = [t]
            s["o"] = DVE.op(lambda e: e.tensor_scalar(d["out"], o, s["rc"], None, ALU.mult), t, s["rc_t"],
                            F())
            if done:
                done[0] = s["o"]
            give(b, [s["o"]])

        divided[0] = True
        shared["c"] = values
        for u in range(len(units) + 3):
            if u < len(units):
                step_a(u)
            if 2 <= u <= len(units) + 1:
                step_b(u - 2)
            if u < len(units):
                step_exp(u)
            if u >= 3:
                step_c(u - 3)
        divided[0] = False
        return st[-1]["o"]

    def stack_q(q, r0, dst, *waits):
        o = 64 - r0
        hi = dst[r0:r0 + 64]
        t = AC.op(lambda e: e.activation(hi, q, ACT.Copy), waits, PL.last())
        return [t, PL.op(lambda e: e.tensor_tensor(dst[o:o + 64], q, hi.bitcast(F32), ALU.subtract), t)]

    def stack_k(k, r0, dst, lo, twice, *waits):
        o = 64 - r0
        hi = dst[r0:r0 + 64]
        t = AC.op(lambda e: e.activation(hi, k, ACT.Copy), waits)
        u = [AC.op(lambda e: e.activation(dst[o:o + 64], k, ACT.Copy), waits),
             PL.op(lambda e: e.tensor_tensor(lo[r0:r0 + 64], k, hi.bitcast(F32), ALU.subtract), t, waits)]
        if twice:
            u.append(PL.op(lambda e: e.tensor_tensor(lo[o:o + 64], k, hi.bitcast(F32), ALU.subtract), t,
                           waits))
        return u

    def head_rms(raw, n, g, mul, ready, SQt, wfree):
        t = AC.op(lambda e: e.activation(SQt[:, 0:n], raw, ACT.Square), ready, list(wfree))
        b, bw = take()
        t2 = PE.op(lambda e: e.matmul(psb(b, n), BLK, SQt[:, 0:n], start=True, stop=True), t, bw)
        wfree[:] = [t2]
        x, r, y = (RS[:, j, 0:n] for j in range(3))
        t3 = DVE.op(lambda e: e.tensor_scalar(x, psb(b, n), 1e-6, None, ALU.add), t2, rsfree)
        give(b, [t3])
        t3 = AC.op(lambda e: e.activation(r, x, ACT.Sqrt), t3)

        def second():
            t4 = newton(x, r, y, t3, mul)
            t5 = DVE.op(lambda e: e.scalar_tensor_tensor(raw, raw, g, r, ALU.mult, ALU.mult), t4)
            rsfree[:] = [t5]
            return t5
        return second

    rsfree = []
    br_tok = {}

    def to_features(TOKN, tiles, cols, fn, ready):
        for f in cols:
            for g0 in range(0, len(tiles), 4):
                b, bw = take()
                grp = tiles[g0:g0 + 4]
                for j, i in enumerate(grp):
                    t = PE.op(lambda e, i=i, j=j: e.transpose(psb2(b, j * 128, j * 128 + 128),
                                                              TOKN[:, i, f * 128:f * 128 + 128], IDF),
                              ready, bw)
                give(b, fn(f, g0 * 128, len(grp) * 128, b, t))

    XH, p = at("X1h", [128, 8, T1], F32R, P0)
    XL, p = at("X1l", [128, 8, T1], F32R, p)
    P1 = p
    HH, p = at("H1h", [128, 8, T1], F32R, P1)
    HL, p = at("H1l", [128, 8, T1], F32R, p)
    TM, p = at("TM1", [128, 2, 264], F32, p)
    X = (XH, XL)
    chunks = [(0, 264), (264, 264)]
    nb1 = [(0, 264, 0), (264, 264, 0)]
    by = norm_all("rms", nb1, lambda k, c: vec("ffn1", k), None, X, 0, p, 
                  [(0, T1, [[x_in[k // 2], t_in] for k in range(8)])], (), 2)
    e = ffn("f1", X, 0, chunks, HH, HL, TM, by, [], lambda m, c0: 0.5, 3)
    by = norm_all("rms", nb1, lambda k, c: vec("mix", k), None, X, 0, p, e, PE.last(), 3)
    barrier()

    YB, p = at("YB", [128, 8, TX], F32, P1 + 8 * TX * 4)
    P2 = p
    RQ, p = at("RQ", [128, 4, TX], F32, P2)
    RK, p = at("RK", [128, 4, T1], F32, p)
    VR, p = at("VR", [128, 5, 1024], F32, p)
    P3 = p
    CS, p = at("CS", [128, 2, T1], F32, P3)
    RT, p = at("RT", [128, 2, T1], F32, p)
    tl = load(CS[:, :, :], A["rope1"], F())
    rfree = [[], []]
    idx = [0]
    rk_ready = []

    def rope(dst, c0, n, tabs, col, perm, ready, RTn, nrt=2):
        i = idx[0] % nrt
        idx[0] += 1
        b, bw = take()
        t = PE.op(lambda e: e.matmul(psb(b, n), perm, dst, start=True, stop=True), ready, bw)
        u = DVE.op(lambda e: e.tensor_tensor(RTn[:, i, 0:n], psb(b, n), tabs[:, 1, col:col + n], ALU.mult),
                   t, rfree[i], tl)
        give(b, [u])
        v = PL.op(lambda e: e.tensor_tensor(dst, dst, tabs[:, 0, col:col + n], ALU.mult), t, tl)

        def second():
            w = DVE.op(lambda e: e.tensor_tensor(dst, dst, RTn[:, i, 0:n], ALU.add), u, v)
            rfree[i] = [w]
            return w
        return second

    jobs = []

    def tick():
        for f in jobs.pop(0) if jobs else []:
            f()

    def flush():
        while jobs:
            tick()

    def at_tick(n, f):
        while len(jobs) <= n:
            jobs.append([])
        jobs[n].append(f)

    for dst, nm, chs in ((RQ, "w_rq", [(16, 512)]), (RK, "w_rk", chunks)):
        for m in range(4):
            res = lin(nm, (m,), 8, X, 0, chs, by=by)
            tick()
            for j, ((c0, n), (b, t)) in enumerate(zip(chs, res)):
                a = c0 - (16 if dst is RQ else 0)
                o = dst[:, m, a:a + n]
                t = AC.op(lambda e: e.activation(o, psb(b, n), ACT.Copy), t, F())
                give(b, [t])
                hold = []
                at_tick(0, lambda o=o, c0=c0, n=n, t=t, hold=hold: hold.append(
                    rope(o, c0, n, CS, c0, PRM, t, RT)))
                at_tick(1, lambda hold=hold: rk_ready.append(hold[0]()))
    tiles1 = [0, 16, 144, 272, 400]

    def vcopy(dst, base, meta=False):
        def epi(i, b, t):
            rows = NMETA if i == 0 and meta else 128
            q = AC if i % 2 else DVE
            if q is AC:
                return [AC.op(lambda e: e.activation(dst[0:rows, i, base:base + 256], psb(b, 256, rows),
                                                     ACT.Copy), t, F())]
            return [DVE.op(lambda e: e.tensor_copy(dst[0:rows, i, base:base + 256], psb(b, 256, rows)), t,
                           F())]
        return epi

    for g in range(4):
        lin_tok("w_rv", g, X, tiles1, vcopy(VR, g * 256, True), by=by)
        tick()
    flush()
    barrier()
    DT, p = at("DT", [128, 4, T1], F32, P3)
    SS, p = at("SS", [128, 2, 5, 128], F32, p)
    YT, _ = at("YT", [128, 4, 1024], F32, P1)
    ST, p = at("ST", [128, 4, 8], F32, p)
    AG, p = at("AG", [128, 4, 4, 2], F32, p)
    AY, p = at("AY", [128, 2, 4, 4], F32, p)
    tl2 = load(DT[:, :, :], A["decay"], F())
    sfree = [[], []]
    units = [(h, i) for h in range(4) for i in range(4)]
    S = {}

    def ret_a(u):
        h, i = units[u]
        b, bw = take(2)
        q = RQ[:, h, i * 128:i * 128 + 128]
        for j in range(i + 1):
            k = RK[:, h, 16 + j * 128:144 + j * 128]
            t = PE.op(lambda e, j=j: e.matmul(psb2(b, j * 128, j * 128 + 128), k, q, start=True, stop=True),
                      bw, rk_ready, F())
        k = RK[:, h, 0:NMETA]
        t = PE.op(lambda e: e.matmul(psb2(b, 512, 640, NMETA), k, q, start=True, stop=True))
        s = SS[:, u % 2, :, :]
        for j in range(i + 1):
            a = (i - j) * 128
            t2 = DVE.op(lambda e, j=j, a=a: e.tensor_tensor(s[:, j, :], psb2(b, j * 128, j * 128 + 128),
                                                            DT[:, h, a:a + 128], ALU.mult), t, tl2,
                        sfree[u % 2], F())
        a = 16 + i * 128
        t2 = DVE.op(lambda e: e.tensor_tensor(s[0:NMETA, 4, :], psb2(b, 512, 640, NMETA),
                                              DT[0:NMETA, h, a:a + 128], ALU.mult), t)
        give(b, [t2], 2)
        S[u] = t2

    yt_toks = []

    def ret_b(u):
        h, i = units[u]
        b, bw = take()
        s = SS[:, u % 2, :, :]
        o = psb(b, 256)
        for j in range(i + 1):
            PE.op(lambda e, j=j: e.matmul(o, s[:, j, :], VR[:, j + 1, h * 256:h * 256 + 256], start=j == 0,
                                          stop=False), S[u], bw)
        t = PE.op(lambda e: e.matmul(o, s[0:NMETA, 4, :], VR[0:NMETA, 0, h * 256:h * 256 + 256],
                                     start=False, stop=True))
        sfree[u % 2] = [t]
        st, ag = ST[:, u % 4, 0:6], AG[:, h, i, :]
        v = DVE.op(lambda e: e.bn_stats(st, o), t, F())
        c = AC.op(lambda e: e.activation(YT[:, i, h * 256:h * 256 + 256], o, ACT.Copy), t, F(), v)
        give(b, [c])
        gn.append(DVE.op(lambda e: e.bn_aggr(ag, st), v))
        if i < 3:
            return
        var, y, w = AG[:, h, :, 1], AY[:, 0, h, :], AY[:, 1, h, :]
        v = DVE.op(lambda e: e.tensor_scalar(var, var, 1e-5, None, ALU.add), gn[-1])
        v = rsqrt(var, y, w, v)
        for j in range(4):
            yt = YT[:, j, h * 256:h * 256 + 256]
            yt_toks.append(DVE.op(lambda e: e.tensor_scalar(yt, yt, AG[:, h, j, 0:1], y[:, j:j + 1],
                                                            ALU.subtract, ALU.mult), v, c))

    gn = []
    for u in range(len(units) + 1):
        if u < len(units):
            ret_a(u)
        if u >= 1:
            ret_b(u - 1)

    def to_yb(f, a, n, b, t):
        return [AC.op(lambda e: e.activation(YB[:, f, a:a + n], psb(b, n), ACT.Copy), t, F())]

    to_features(YT, [0, 1, 2, 3], range(8), to_yb, yt_toks[-1])
    SG, p = at("SG", [128, 2, 512], F32, P1)
    sgf = [[], []]
    ybt = fence()
    for m in range(8):
        (b, t), = lin("w_rg", (m,), 8, X, 0, [(16, 512)], by=by)
        i = m % 2
        t = AC.op(lambda e: e.activation(SG[:, i, :], psb(b), ACT.Silu), t, sgf[i], F())
        give(b, [t])
        t = DVE.op(lambda e: e.scalar_tensor_tensor(YB[:, m, :], YB[:, m, :], vec("retgn", m), SG[:, i, :],
                                                    ALU.mult, ALU.mult), t, ybt)
        sgf[i] = [t]
    barrier()

    Q, p = at("Q", [128, 2, TX], F32, P2)
    K, p = at("K", [128, 2, T1], F32, p)
    VF, p = at("VF", [128, 5, 1024], F32, p)
    SEL, p = at("SEL", [128, 16, 128], U16, p)
    CP, p = at("CP", [128, T1], BF16, p)
    SQT, p = at("SQT", [128, 2, T1], F32, p)
    Pb, p = at("Pb", [128, 3, 528], F32, p)
    PT, p = at("PT", [128, 2, 640], F32, p)
    QS, p = at("QS", [128, 2, TX], F32R, p)
    KS, p = at("KS", [128, 2, T1], F32R, p)
    KL, p = at("KL", [128, T1], F32R, p)
    YT, _ = at("YTF", [128, 4, 1024], F32, P1)
    LF, _ = at("LF", [16, 5, T1], F32, P1)
    tl = load(SEL[:, :, :], A["sel"], F())
    cz = PL.op(lambda e: e.memset(CP[:, :], 0.0), F())
    cfree = []
    res = lin("w_ff", (0,), 8, X, 0, chunks, by=by)
    z, az, u_, r_, s_ = (LF[:, i, :] for i in range(5))
    for (c0, n), (b, t) in zip(chunks, res):
        t = AC.op(lambda e: e.activation(z[:, c0:c0 + n], psb(b, n, 16), ACT.Identity, bias=V[0:16,
                  VEC["bf"][0]:VEC["bf"][0] + 1]), t, F())
        give(b, [t])
    t = AC.op(lambda e: e.activation(az, z, ACT.Abs), t)
    t = AC.op(lambda e: e.activation(az, az, ACT.Exp, scale=-1.0), t)
    t = DVE.op(lambda e: e.tensor_scalar(u_, az, 1.0, None, ALU.add), t)
    tl_n = AC.op(lambda e: e.activation(r_, u_, ACT.Ln), t)
    t = DVE.op(lambda e: e.scalar_tensor_tensor(s_, u_, -1.0, az, ALU.add, ALU.subtract), t)
    t = DVE.op(lambda e: e.reciprocal(u_, u_), t, tl_n)
    t = DVE.op(lambda e: e.tensor_tensor(s_, s_, u_, ALU.mult), t)
    t = DVE.op(lambda e: e.tensor_tensor(r_, r_, s_, ALU.subtract), t)
    t = DVE.op(lambda e: e.scalar_tensor_tensor(r_, z, 0.0, r_, ALU.min, ALU.subtract), t)
    t = DVE.op(lambda e: e.tensor_scalar(r_, r_, -1.0, None, ALU.mult), t)
    t = DVE.op(lambda e: e.memset(u_, 1.0), t)
    t = DVE.op(lambda e: e.tensor_tensor_scan(s_, u_, r_, 0.0, ALU.mult, ALU.add), t)
    t = DVE.op(lambda e: e.tensor_copy(CP[0:16, :], s_), t, cz)
    t = DVE.op(lambda e: e.tensor_tensor(s_, s_, CP[0:16, :], ALU.subtract), t)
    t = DVE.op(lambda e: e.tensor_copy(CP[32:48, :], s_), t)
    t = DVE.op(lambda e: e.tensor_copy(u_, CP[32:48, :]), t)
    t = DVE.op(lambda e: e.tensor_tensor(s_, s_, u_, ALU.subtract), t)
    c_ready = DVE.op(lambda e: e.tensor_copy(CP[64:80, :], s_), t)

    for g in range(4):
        lin_tok("w_fv", g, X, tiles1, vcopy(VF, g * 256, True), by=by)

    sqf = [[], []]
    nq = [0]
    raw_t = {}
    half = [None]
    stacked = {h: [] for h in range(16)}
    used = [[], []]

    def project(which, m, part=None):
        dst, nm, chs = (Q, "w_fq", [(16, 512)]) if which == "q" else (K, "w_fk", chunks)
        raw_t.setdefault((which, m), [])

        def each(c0, n, b, t):
            a = c0 - (16 if dst is Q else 0)
            o = dst[:, m % 2, a:a + n]
            t = AC.op(lambda e: e.activation(o, psb(b, n), ACT.Copy), t, F(),
                      stacked[2 * m - 3] if m >= 2 else None)
            give(b, [t])
            raw_t[which, m].append((o, n, t))

        u, s, ready = half[0] if part == 1 else w_get(nm, (m,), 1024)
        half[0] = u, s, ready
        for c0, n in chs if part is None else chs[part:part + 1]:
            b, bw = take()
            for k in range(8):
                w = Wh[:, s, k * 128:k * 128 + 128], Wl[:, s, k * 128:k * 128 + 128]
                t = mm3(psb(b, n), *w, XH[:, k, c0:c0 + n], XL[:, k, c0:c0 + n], k == 0, k == 7, ready, bw)
            each(c0, n, b, t)
        if part != 0:
            w_done(u, t)

    def normalise(which, m, i):
        g, mul = ("fq", 0.125) if which == "q" else ("fk", 1.0)
        r = raw_t[which, m]
        o, n, t = r[i]
        s = nq[0] % 2
        nq[0] += 1
        r[i] = head_rms(o, n, vec(g), mul, t, SQT[:, s, :], sqf[s])

    def normalised(which, m, i):
        raw_t[which, m][i] = raw_t[which, m][i]()

    def stack(h):
        m, r0, s = h // 2, 64 * (h % 2), h % 2
        w = [raw_t["q", m], raw_t["k", m], list(used[s])]
        stacked[h] += stack_q(Q[r0:r0 + 64, m % 2, :], r0, QS[:, s, :], w)
        stacked[h] += stack_k(K[r0:r0 + 64, m % 2, :], r0, KS[:, s, :], KL, False, w)

    project("q", 0)
    project("k", 0)
    for w, i in (("q", 0), ("k", 0), ("k", 1)):
        normalise(w, 0, i)
        normalised(w, 0, i)
    stack(0)
    barrier()
    us = []
    for h in range(16):
        r0 = 64 * (h % 2)
        for i in range(4):
            n = 144 + 128 * i
            m, j, hs = h // 2, 4 * (h % 2) + i, h % 2
            pre = []
            if j == 0:
                pre.append(lambda h=h: stack(h + 1))
            if m < 7:
                pre += [lambda f=f, a=a, m=m: f(a[0], m + 1, *a[1:])
                        for f, a, at_j in ((project, "q", 0), (normalise, ("q", 0), 1),
                                           (project, ("k", 0), 2), (normalised, ("q", 0), 2),
                                           (project, ("k", 1), 3), (normalise, ("k", 0), 4),
                                           (normalised, ("k", 0), 5), (normalise, ("k", 1), 5),
                                           (normalised, ("k", 1), 6)) if at_j == j]
                if j == 7:
                    pre.append(lambda h=h: stack(h + 1))
            us.append({
                "pre": lambda pre=pre: [f() for f in pre],
                "qk": lambda a, z, i=i, r0=r0, s=hs: (
                    (QS[:, s, i * 128:i * 128 + 128], KS[:, s, a:z]),
                    (QS[r0:r0 + 64, s, i * 128:i * 128 + 128], KL[r0:r0 + 64, a:z])),
                "n": n,
                "used": used[hs],
                "add": [(IDB, lambda a, z, i=i: MSKB[:, a - 16 - 128 * i:z - 16 - 128 * i], 16 + 128 * i, n),
                        (SEL[:, h, :].bitcast(BF16), lambda a, z: CP[:, a:z], 0, max(n, 256))],
                "blocks": [(16 + 128 * j, 128, VF[:, j + 1, h * 64:h * 64 + 64]) for j in range(i + 1)]
                + [(0, 16, VF[0:16, 0, h * 64:h * 64 + 64])],
                "ready": [stacked[h], c_ready, tl], "vready": [],
                "out": YT[:, i, h * 64:h * 64 + 64]})
    for d in us:
        if d["n"] > 512:
            (l1, f1, a1, z1), (l0, f0, a0, z0) = d["add"]
            d["add"] = [(l1, f1, a1, 512), (l0, f0, 0, 512), (l1, f1, 512, z1), (l0, f0, 512, z0)]
    t = attention(us, Pb, PT, [6])
    barrier()
    YA, _ = at("YA", [128, 8, TX], F32, P2)

    def to_ya(f, a, n, b, t):
        return [AC.op(lambda e: e.activation(YA[:, f, a:a + n], psb(b, n), ACT.Copy), t, F())]

    to_features(YT, [0, 1, 2, 3], range(8), to_ya, t)
    barrier()

    def split(src, h, l, *waits):
        for k in range(8):
            t = AC.op(lambda e, k=k: e.activation(h[:, k, :], src[:, k, :], ACT.Copy), waits)
            t = DVE.op(lambda e, k=k: e.tensor_tensor(l[:, k, :], src[:, k, :], h[:, k, :].bitcast(F32),
                                                      ALU.subtract), t, waits)
        return t

    M1, _ = at("M1", [128, 8, TX], F32, P1)
    YH, p = at("YAh", [128, 8, TX], F32R, P2 + 8 * TX * 4)
    YL, p = at("YAl", [128, 8, TX], F32R, p)
    GT, p = at("GT", [128, 2, 512], F32, p)
    yr = split(YA, YH, YL, F())
    gf = [[], []]
    XX = [(16, 512)]
    for m in range(8):
        (b0, t0), = lin("w_ga", (m,), 8, X, 0, XX, by=by)
        (b1, t1), = lin("w_of", (m,), 8, (YH, YL), 16, XX, yr)
        i = m % 2
        t = AC.op(lambda e: e.activation(GT[:, i, :], psb(b0), ACT.Sigmoid, bias=vec("bgate", m)), t0,
                  gf[i], F())
        give(b0, [t])
        t = DVE.op(lambda e: e.tensor_tensor(M1[:, m, :], GT[:, i, :], psb(b1), ALU.mult), t, t1, F())
        give(b1, [t])
        gf[i] = [t]
    barrier()
    YH, p2 = at("YBh", [128, 8, TX], F32R, P2)
    YL, p2 = at("YBl", [128, 8, TX], F32R, p2)
    GT, p2 = at("GT2", [128, 2, 512], F32, p2)
    MH, _ = at("MXh", [128, 8, TX], F32R, P1 + 8 * TX * 4)
    ML, _ = at("MXl", [128, 8, TX], F32R, p2)
    yr = split(YB, YH, YL, F())
    gf = [[], []]
    for m in range(8):
        (b0, t0), = lin("w_gb", (m,), 8, X, 0, XX, by=by)
        (b1, t1), = lin("w_or", (m,), 8, (YH, YL), 16, XX, yr)
        i = m % 2
        t = AC.op(lambda e: e.activation(GT[:, i, :], psb(b0), ACT.Sigmoid, bias=vec("bgate", 8 + m)), t0,
                  gf[i], F())
        give(b0, [t])
        t = DVE.op(lambda e: e.tensor_tensor(GT[:, i, :], GT[:, i, :], psb(b1), ALU.mult), t, t1)
        give(b1, [t])
        t = DVE.op(lambda e: e.tensor_tensor(M1[:, m, :], M1[:, m, :], GT[:, i, :], ALU.add), t)
        gf[i] = [t]
        t2 = AC.op(lambda e: e.activation(MH[:, m, :], M1[:, m, :], ACT.Copy), t, F(), yr)
        mr = DVE.op(lambda e: e.tensor_tensor(ML[:, m, :], M1[:, m, :], MH[:, m, :].bitcast(F32),
                                              ALU.subtract), t2, F())
    hmix = [(16, 512, [])]
    for m in range(8):
        (b0, t0), = lin("w_out", (m,), 8, (MH, ML), 16, XX, mr)
        t = DVE.op(lambda e: e.tensor_tensor(H[:, m, 16:528], H[:, m, 16:528], psb(b0), ALU.add), t0)
        give(b0, [t])
        hmix[0][2].append(t)
    barrier()
    HH, p = at("H2h", [128, 8, T1], F32R, P1)
    HL, p = at("H2l", [128, 8, T1], F32R, p)
    TM, p = at("TM2", [128, 2, 512], F32, p)
    nb2 = [(16, 256, 0), (272, 256, 0)]
    by = norm_all("rms", nb2, lambda k, c: vec("ffn2", k), None, X, 0, p, hmix, F(), 3)
    e = ffn("f2", X, 0, XX, HH, HL, TM, by, [], lambda m, c0: 0.5, 3)

    h_ready = e + [(528, TC, [t_ctx] * 8)]
    for l in range(2):
        both = l == 0
        barrier()
        XH, p = at(f"X2h{l}", [128, 8, 768], F32R, P0)
        XL, p = at(f"X2l{l}", [128, 8, 768], F32R, p)
        P1 = p
        X = (XH, XL)
        mt = mod_until(l, 1)
        blocks = [(16, 256, 0), (272, 256, 0), (528, 256, 1)]
        by = norm_all("ln", blocks, lambda k, c: mod(l, 1, k, c), lambda k, c: mod(l, 0, k, c), X, 16, p,
                      h_ready, [F(), mt], 3)
        barrier()

        def prescale():
            c1 = 784 if both else 528
            for k in range(8):
                tt = PL.op(lambda e, k=k: e.tensor_scalar(H[:, k, 16:c1], H[:, k, 16:c1], ALPHA, None,
                                                          ALU.mult), F())
            return tt
        hp = prescale()
        QA, p = at(f"QA{l}", [128, 3, 768], F32, P1)
        KA, p = at(f"KA{l}", [128, 3, 768], F32, p)
        QC, p = at(f"QC{l}", [128, 3, 768], F32, p)
        KC, p = at(f"KC{l}", [128, 1, 768], F32, p)
        VA, p = at(f"VA{l}", [128, 6, 512], F32, p)
        ZU, p = at(f"ZU{l}", [128, 6, 256], F32, p)
        ZV, p = at(f"ZV{l}", [128, 6, 256], F32, p)
        GS, p = at(f"GS{l}", [128, 256], F32, p)
        WS, p = at(f"WS{l}", [128, 4, 128], F32, p)
        BM, p = at(f"BM{l}", [128, 1024], F32, p)
        CS, _ = at(f"CSA{l}", [128, 2, 512], F32, p)
        SQT, _ = at(f"SQA{l}", [128, 2, 512], F32, p + 4096)
        RT, _ = at(f"RTA{l}", [128, 1, 512], F32, p + 8192)
        PP = p
        tl = load(CS[:, :, :], A["rope2"], F())
        tlg = load(GS[:, :], A["gsgu"][l], F())
        tlw = load(WS[:, :, :], A["wst"][l], F())
        tlm = load(BM[:, :], A["wmask"], F())
        full = [(16, 512), (528, 256)]
        lat = [(16, 512)]
        qs = full if both else lat
        sqf = [[], []]
        rfree = [[], []]
        qkr = []
        def proj(dst, nm, m, chs, g, mul):
            res = lin(f"w2_{nm}", (l, m), 8, X, 16, chs, by=by)
            tick()
            base = len(jobs) - 1 if jobs else 0
            for (c0, n), (b, t) in zip(chs, res):
                o = dst[:, m, c0 - 16:c0 - 16 + n]
                t = AC.op(lambda e: e.activation(o, psb(b, n), ACT.Copy, scale=mul if g is None else 1.0),
                          t, F())
                give(b, [t])
                if g is None:
                    continue
                hold = []

                def one(o=o, n=n, t=t, hold=hold):
                    i = nq[0] % 2
                    nq[0] += 1
                    hold.append(head_rms(o, n, vec(f"{g}{l}"), mul, t, SQT[:, i, :], sqf[i]))

                def two(hold=hold):
                    hold.append(hold[0]())
                    qkr.append(hold[1])

                def three(o=o, n=n, c0=c0, hold=hold):
                    hold.append(rope(o, c0, n, CS, 0, PAX, hold[1], RT, 1))
                j = base if c0 == 16 else base + 1
                at_tick(j, one)
                at_tick(j + 1, two)
                if c0 == 16:
                    at_tick(j + 2, three)
                    at_tick(j + 3, lambda hold=hold: qkr.append(hold[2]()))

        for dst, nm, m, chs, g, mul in (
                (QC, "qc", 0, qs, "gq", 0.125), (QA, "qa", 0, qs, None, 0.125), (QA, "qa", 1, qs, None, 0.125),
                (QC, "qc", 1, qs, "gq", 0.125), (QA, "qa", 2, qs, None, 0.125), (KA, "ka", 0, full, None, 1.0),
                (QC, "qc", 2, qs, "gq", 0.125), (KA, "ka", 1, full, None, 1.0), (KA, "ka", 2, full, None, 1.0),
                (KC, "kc", 0, full, "gk", 1.0)):
            proj(dst, nm, m, chs, g, mul)
        tks = [0, 128, 256, 384, 512, 640]
        zt = tks if both else tks[:4]
        for g in range(2):
            lin_tok("w2_v", l * 2 + g, X, tks, vcopy(VA, g * 256), by=by, shift=16)
            tick()

        def gelu(dst):
            def epi(i, b, t):
                return [AC.op(lambda e: e.activation(dst[:, i, :], psb(b, 256), ACT.Gelu_apprx_tanh), t,
                              F())]
            return epi
        for g, dst in ((0, ZU), (1, ZV)):
            lin_tok("w2_z", l * 2 + g, X, zt, gelu(dst), by=by, shift=16)
            tick()
        flush()
        barrier()
        OT, p = at(f"OT{l}", [128, 6, 1024], F32, P0)
        BR, p = at(f"BR{l}", [128, 2, 1024], F32, p)
        Pb, p = at(f"PbA{l}", [128, 3, 768], F32, p)
        QS, p = at(f"QSA{l}", [128, 2, 768], F32R, p)
        assert p <= P1
        assert p <= P1
        PT, p = at(f"PTA{l}", [128, 2, 768], F32, PP)
        SQ3, p = at(f"SQ3{l}", [128, 384], F32, p)
        KS, p = at(f"KSA{l}", [128, 2, 768], F32R, p)
        KL, p = at(f"KLA{l}", [128, 2, 768], F32R, p)
        AG, ay, aw = SM[:, 48:60], SM[:, 60:66], SM[:, 66:72]
        nz = len(zt)
        zr = {}

        def gate_norm():
            vs = []
            for i in range(nz):
                st = SM[:, 32 + 6 * (i % 2):38 + 6 * (i % 2)]
                v = DVE.op(lambda e: e.bn_stats(st, ZV[:, i, :]), F(), vs[i - 2] if i >= 2 else None)
                vs.append(DVE.op(lambda e: e.bn_aggr(AG[:, 2 * i:2 * i + 2], st), v))
            var = AG.rearrange("p (i c) -> p i c", c=2)[:, 0:nz, 1]
            v = DVE.op(lambda e: e.tensor_scalar(var, var, 1e-6, None, ALU.add), vs[-1])
            zr["v"] = rsqrt(var, ay[:, 0:nz], aw[:, 0:nz], v)

        def gating(i):
            zv = ZV[:, i, :]
            v = DVE.op(lambda e: e.tensor_scalar(zv, zv, AG[:, 2 * i:2 * i + 1], ay[:, i:i + 1],
                                                 ALU.subtract, ALU.mult), zr["v"])
            v = PL.op(lambda e: e.tensor_tensor(zv, zv, GS[:, :], ALU.mult), v, tlg, PL.last())
            b, bw = take()
            for g in range(4):
                t = PE.op(lambda e: e.matmul(psb2(b, g * 64, g * 64 + 64), WS[:, g, :],
                                             ZV[:, i, g * 64:g * 64 + 64], start=True, stop=True), v, bw, tlw)
            for g in range(4):
                v = DVE.op(lambda e: e.scalar_tensor_tensor(
                    OT[:, i, 384 + g * 64:448 + g * 64], psb2(b, g * 64, g * 64 + 64), vec(f"bs{l}", g),
                    ZU[:, i, g * 64:g * 64 + 64], ALU.add, ALU.mult), t, F())
            give(b, [v])
            zr[i] = v

        nqc = 768 if both else 512
        stacked = {h: [] for h in range(12)}
        used = [[], []]

        def kslot(h):
            return h % 2 if h < 6 else h // 3 % 2

        def stack(h):
            w = [F(), list(used[h % 2])]
            hh, r0 = h % 6, 64 * (h % 2)
            stacked[h] += stack_q((QA if h < 6 else QC)[r0:r0 + 64, hh // 2, 0:nqc], r0, QS[:, h % 2, 0:nqc],
                                  w)
            s = kslot(h)
            if h == 0:
                w.append(list(used[1]))
            if h < 6:
                stacked[h] += stack_k(KA[r0:r0 + 64, hh // 2, :], r0, KS[:, s, :], KL[:, s, :], False, w)
            elif hh % 3 == 0:
                g = hh // 3
                r = 64 * g
                stacked[h] += stack_k(KC[r:r + 64, 0, :], r, KS[:, s, :], KL[:, s, :], True, w, used[0],
                                      used[1])
            else:
                stacked[h] += stacked[h - 1][2:]

        def unit(h, i, vc, k0, k1, col, **more):
            r0, s, ks = 64 * (h % 2), h % 2, kslot(h)
            return {"qk": lambda a, z: (
                        (QS[:, s, i * 128:i * 128 + 128], KS[:, ks, k0 + a:k0 + z]),
                        (QS[r0:r0 + 64, s, i * 128:i * 128 + 128], KL[r0:r0 + 64, ks, k0 + a:k0 + z])),
                    "n": k1 - k0, "used": used[s],
                    "blocks": [(c, 128, VA[:, (k0 + c) // 128, vc:vc + 64]) for c in range(0, k1 - k0, 128)],
                    "ready": [stacked[h]], "vready": [], "out": OT[:, i, col:col + 64], **more}

        br_load = {}

        def bias_load(h):
            br_load[h] = load(BR[:, h % 2, :], A["rpbt"][l, h], F(), DVE.last())

        def bias_add(h):
            br_tok[h] = DVE.op(lambda e: e.tensor_tensor(BR[:, h % 2, :], BR[:, h % 2, :], BM[:, :],
                                                         ALU.add), br_load[h], tlm, F())

        seq = [6, 7, 8, 9, 10, 11, 0, 1, 2, 3, 4, 5]
        us = []
        for n, h in enumerate(seq):
            hooks = {}
            if n < 11:
                hooks[1] = [lambda h2=seq[n + 1]: stack(h2)]
            if h < 6:
                hs = [unit(h, i, h * 64, 0, 768, h * 64,
                           bias=BR[:, h % 2, (7 - 2 * i) * 64:(7 - 2 * i) * 64 + 512], bias_ready=h)
                      for i in range(4)]
                if both:
                    hs += [unit(h, i, h * 64, 512, 768, h * 64) for i in (4, 5)]
                if h < 5:
                    hooks[0] = [lambda h=h: bias_load(h + 1)]
                    hooks[3] = [lambda h=h: bias_add(h + 1)]
                if 1 <= h <= 4:
                    for i in range(4):
                        j = 4 * (h - 1) + i
                        if j < 2 * nz:
                            hooks.setdefault(i, []).append(lambda j=j: squares(j // 2, 1 + j % 2))
            else:
                g = (h - 6) // 3
                hs = [unit(h, i, 384 + g * 64, 0 if i < 4 else 512, 768, 640 + (h - 6) * 64)
                      for i in range(nz)]
                if h == 6:
                    hooks[2] = [gate_norm]
                if h in (7, 8):
                    for i in range(nz // 2):
                        hooks.setdefault(i, []).append(lambda i=i, h=h: gating((h - 7) * (nz // 2) + i))
                if h == 11:
                    hooks[3] = [lambda: bias_add(0)]
            for i, fs in hooks.items():
                hs[i]["pre"] = lambda fs=fs: [f() for f in fs]
            us += hs
        GR = ((0, 384), (384, 640), (640, 1024))
        last_sq = [None]

        def squares(i, g):
            a, z = GR[g]
            last_sq[0] = AC.op(lambda e: e.activation(SQ3[:, 0:z - a], OT[:, i, a:z], ACT.Square,
                                                      accum_out=SM[:, 32 + 6 * g + i:33 + 6 * g + i]),
                               F(), last_sq[0], ot_done[0], zr.get(i))

        ot_done = [None]
        stack(6)
        bias_load(0)
        attention(us, Pb, PT, [6], ot_done)
        for i in range(nz):
            squares(i, 0)
        ss, sw, sy = SM[:, 32:50], SM[:, 50:68], SM[:, 72:90]
        v = last_sq[0]
        for g, (a, z) in enumerate(GR):
            x = ss[:, 6 * g:6 * g + nz]
            v = DVE.op(lambda e: e.tensor_scalar(x, x, 1.0 / (z - a), 1e-6, ALU.mult, ALU.add), v)
        v = rsqrt(ss, sy, sw, v)
        rdy = []
        for i in range(nz):
            r = []
            for g, (a, z) in enumerate(GR):
                y = sy[:, 6 * g + i:6 * g + i + 1]
                o = OT[:, i, a:z]
                if g == 1:
                    r.append(PL.op(lambda e: e.tensor_scalar(o, o, y, None, ALU.mult), v))
                elif g == 0:
                    r.append(DVE.op(lambda e: e.tensor_scalar(o, o, y, None, ALU.mult), v))
                else:
                    r.append(AC.op(lambda e: e.activation(o, o, ACT.Copy, scale=y), v))
            rdy.append(r)
        barrier()
        OH, p = at(f"OH{l}", [128, 8, 768], F32R, P1)
        OL, p = at(f"OL{l}", [128, 8, 768], F32R, p)

        def to_o(fi, a, n, b, t):
            g = vec(f"gout{l}", fi)
            t = AC.op(lambda e: e.activation(OH[:, fi, a:a + n], psb(b, n), ACT.Copy, scale=g), t, F())
            v = DVE.op(lambda e: e.scalar_tensor_tensor(OL[:, fi, a:a + n], psb(b, n), g,
                                                        OH[:, fi, a:a + n].bitcast(F32), ALU.mult,
                                                        ALU.subtract), t, F())
            orr.append(v)
            return [v]
        orr = []
        to_features(OT, list(range(nz)), range(8), to_o, rdy)
        nb = [(16, 256, 0), (272, 256, 0)] + ([(528, 256, 1)] if both else [])

        mt = mod_until(l, 2)
        hr = [(c0, n, []) for c0, n in qs]
        for m in range(8):
            res = lin("w2_o", (l, m), 8, (OH, OL), 16, qs, orr[-1])
            for (c0, n), (b, t), (_, _, done) in zip(qs, res, hr):
                hk = H[:, m, c0:c0 + n]
                g = mod(l, 2, m, 0 if c0 == 16 else 1)
                t = DVE.op(lambda e: e.scalar_tensor_tensor(hk, psb(b, n), g, hk, ALU.mult, ALU.add), t, hp,
                           mt)
                give(b, [t])
                done.append(t)
        barrier()
        XH, p = at(f"X3h{l}", [128, 8, 768], F32R, P0)
        XL, p = at(f"X3l{l}", [128, 8, 768], F32R, p)
        X = (XH, XL)
        HH, p2 = at(f"H3h{l}", [128, 8, 768], F32R, p)
        HL, p2 = at(f"H3l{l}", [128, 8, 768], F32R, p2)
        TM, p2 = at(f"TM3{l}", [128, 2, 512], F32, p2)
        hr = norm_all("ln", nb, lambda k, c: vec(f"ln1g{l}", k), lambda k, c: vec(f"ln1b{l}", k), None, 0,
                      p2, hr, F(), 3)
        mt = mod_until(l, 4)
        by = norm_all("ln", nb, lambda k, c: mod(l, 4, k, c), lambda k, c: mod(l, 3, k, c), X, 16, p, hr,
                      [F(), mt], 3)
        barrier()
        hp = prescale()
        mt = mod_until(l, 5)
        e = ffn(f"g{l}", X, 16, qs, HH, HL, TM, by, [hp, mt],
                lambda m, c0: mod(l, 5, m, 0 if c0 == 16 else 1), 3)
        barrier()
        h_ready = norm_all("ln", nb, lambda k, c: vec(f"ln2g{l}", k), lambda k, c: vec(f"ln2b{l}", k), None,
                           0, p, e, F(), 2)
    s_out = DmaSem(sem("s_out"))
    for c0, n, _ in h_ready:
        for k in range(0, 8, 2):
            t = s_out.add(SP, lambda e: e.dma_start(out[:, k:k + 2, c0 - 16:c0 - 16 + n],
                                                    H[:, k:k + 2, c0:c0 + n]), over(h_ready, c0, n, k + 1))
    SP.op(lambda e: e.wait_ge(*t))

    if dry:
        return
    for q in (PE, DVE, AC, PL, SP):
        q.count()
    with nc.Block() as block:
        block.sync(SP.emit)
        block.gpsimd(PL.emit)
        block.scalar(AC.emit)
        block.tensor(PE.emit)
        block.vector(DVE.emit)


nc_ps = []


def _consts():
    f = np.float32
    cf = np.zeros((128, 5, 128), f)
    cf[:, 0, :] = 1.0 / 1024
    for a in (0, 64):
        cf[a:a + 64, 1, a:a + 64] = 1.0 / 64
    cf[:, 2, :] = np.eye(128)
    q = np.arange(128)
    cf[(q + 64) % 128, 3, q] = 1.0
    cf[q ^ 16, 4, q] = 1.0
    cb = np.zeros((128, 2, 128), np.uint16)
    cb[q, 0, q] = 0x3F80
    cb[:, 1, :] = np.where(q[None, :] > q[:, None], 0xF14A, 0)
    sel = np.zeros((128, 16, 128), np.uint16)
    for h in range(16):
        for a in (0, 32, 64):
            sel[a + h, h, :] = 0x3F80
    half = 64
    inv = (f(10000.0) ** (-(np.arange(half, dtype=f) / f(half)))).astype(f)
    ang = (np.arange(T1, dtype=f)[None, :] * inv[:, None]).astype(f)
    c, s = np.cos(ang.astype(np.float64)), np.sin(ang.astype(np.float64))
    rope1 = np.stack([np.concatenate([c, c]), np.concatenate([-s, s])], 1).astype(f)
    inv = (f(1.0) / (f(10000.0) ** (np.arange(16, dtype=f) / f(16)))).astype(f)
    t = np.arange(512)
    pos = np.stack([t // 64, t % 64]).astype(f)
    d = np.arange(64)
    ang = (pos[d // 32] * inv[d % 16][:, None]).astype(f).astype(np.float64)
    sg = np.where((d % 32) < 16, -1.0, 1.0)[:, None]
    rope2 = np.stack([np.tile(np.cos(ang), (2, 1)), np.tile(np.sin(ang) * sg, (2, 1))], 1).astype(f)
    lg = np.log1p(-np.exp2(-5.0 - np.arange(4)))
    df = (np.arange(T1)[None, :] - np.arange(128)[:, None]).astype(np.float64)
    decay = np.where(df[:, None, :] >= 0, np.exp(lg[None, :, None] * np.maximum(df, 0)[:, None, :]), 0.0)
    decay = (decay * 128.0 ** -0.5).astype(f)
    cc = np.arange(64)
    cs = np.clip(cc - 8, 0, 48)
    ok = (cc[None, :] >= cs[:, None]) & (cc[None, :] < cs[:, None] + 16)
    wm = np.where(ok, 0.0, -1e30).astype(f)
    wmask = np.ascontiguousarray(np.broadcast_to(np.tile(wm, (2, 1))[:, None, :], (128, 16, 64))).reshape(128, 1024)
    return {"cf": cf, "cb": cb, "sel": sel,
            "rope1": rope1, "rope2": rope2, "decay": decay, "wmask": wmask}


def _layout(i):
    def fm(w):
        k, n = w.shape
        return np.ascontiguousarray(w.reshape(k // 128, 128, n // 128, 128).transpose(2, 1, 0, 3)).reshape(
            n // 128, 128, k)

    def tm(w):
        n = w.shape[1]
        return np.ascontiguousarray(w.reshape(2, 4, 128, n // 256, 256).transpose(3, 0, 2, 1, 4)).reshape(
            n // 256, 2, 128, 1024)

    def cols(v):
        return v.reshape(-1, 128).T

    a = _consts()
    x = np.concatenate([i["meta_tokens"], i["x"][0]], 0)
    a["x0"] = np.ascontiguousarray(x.T.reshape(8, 128, T1).transpose(1, 0, 2))
    a["ctx"] = np.ascontiguousarray(i["ctx_2"][0].T.reshape(8, 128, TC).transpose(1, 0, 2))
    w = i["w_in"][0]
    at, parts = 0, {}
    for n, s in (("fq", 1024), ("fk", 1024), ("fv", 1024), ("ff", 16), ("rq", 512), ("rk", 512), ("rv", 1024),
                 ("rg", 1024), ("ga", 1024), ("gb", 1024)):
        parts[n] = w[:, at:at + s]
        at += s
    parts["ff"] = np.pad(parts["ff"], ((0, 0), (0, 112)))
    for n, v in parts.items():
        a["w_" + n] = tm(v) if n in ("fv", "rv") else fm(v)
    a["w_of"], a["w_or"], a["w_out"] = fm(i["w_o_fox"][0]), fm(i["w_o_ret"][0]), fm(i["w_out"][0])
    for t, wi, wo in (("f1", i["w_ffn1_in"][0], i["w_ffn1_out"][0]), ("f2", i["w_ffn2_in"][0], i["w_ffn2_out"][0]),
                      ("g0", i["w_ffn_in_2"][0], i["w_ffn_out_2"][0]),
                      ("g1", i["w_ffn_in_2"][1], i["w_ffn_out_2"][1])):
        a[t + "_in"] = fm(wi)
        for c, (j0, nj) in enumerate(CH):
            a[f"{t}_out{c}"] = fm(wo[j0 * 128:(j0 + nj) * 128])
    a["wmod"] = np.stack([fm(i["w_mod_2"][l]) for l in range(2)])
    names = (("qa", 384), ("ka", 384), ("va", 384), ("z", 512), ("qc", 384), ("kc", 128), ("vc", 128))
    two = {}
    for l in range(2):
        at = 0
        for n, s in names:
            two[n, l] = i["w_in_2"][l][:, at:at + s]
            at += s
    for n in ("qa", "ka", "qc", "kc"):
        a["w2_" + n] = np.stack([fm(two[n, l]) for l in range(2)])
    a["w2_v"] = np.concatenate([tm(np.concatenate([two["va", l], two["vc", l]], 1)) for l in range(2)])
    a["w2_z"] = np.concatenate([tm(two["z", l]) for l in range(2)])
    a["w2_o"] = np.stack([fm(i["w_o_2"][l]) for l in range(2)])
    a["wst"] = np.ascontiguousarray(i["w_s_2"].transpose(0, 3, 1, 2))
    a["gsgu"] = np.ascontiguousarray(np.broadcast_to(i["g_sgu_2"][:, None, :], (2, 128, 256)))
    q = np.arange(128)[:, None, None]
    j = np.arange(16)[None, :, None]
    kc = np.arange(64)[None, None, :]
    dr = np.clip(j - q // 64, 0, 14)
    dc = np.clip(kc - q % 64 + 15, 0, 30)
    a["rpbt"] = np.ascontiguousarray(i["rpb_2"][:, :, dr, dc]).reshape(2, 6, 128, 1024)
    v = np.zeros((128, NVEC), np.float32)

    def put(name, arr):
        s, n = VEC[name]
        v[:, s:s + n] = arr
    put("ffn1", cols(i["norm_ffn1"][0]))
    put("mix", cols(i["norm_mix"][0]))
    put("ffn2", cols(i["norm_ffn2"][0]))
    put("bgate", cols(i["b_gate"][0]))
    put("retgn", cols(i["ret_gn"][0]))
    put("fq", np.tile(i["fox_q_norm"][0], 2)[:, None])
    put("fk", np.tile(i["fox_k_norm"][0], 2)[:, None])
    put("bf", np.pad(i["b_forget"][0], (0, 112))[:, None])
    put("c", np.stack([cols(i["c_2"][0]), cols(i["c_ctx_2"])], 2).reshape(128, 16))
    for l in range(2):
        put(f"bmod{l}", cols(i["b_mod_2"][l]))
        put(f"gq{l}", np.tile(i["g_q_2"][l], 2)[:, None])
        put(f"gk{l}", np.tile(i["g_k_2"][l], 2)[:, None])
        put(f"gout{l}", cols(i["g_out_2"][l]))
        for n in ("ln1_g", "ln1_b", "ln2_g", "ln2_b"):
            put(n.replace("_", "") + str(l), cols(i[n + "_2"][l]))
        put(f"bs{l}", i["b_s_2"][l].T)
    a["vec"] = v
    return a


def kernel(**inputs):
    import concourse.bacc as bacc
    from concourse.bass_utils import run_bass_kernel_spmd
    arrays = {"in_" + k: np.ascontiguousarray(v)
              for k, v in _layout({k: np.asarray(v) for k, v in inputs.items()}).items()}
    nc = bacc.Bacc("TRN2", target_bir_lowering=False, num_devices=1)
    A = {k[3:]: nc.dram_tensor(k, v.shape, mybir.dt.from_np(v.dtype), kind="ExternalInput").ap()
         for k, v in arrays.items()}
    out = nc.dram_tensor("out", (128, 8, TX), F32, kind="ExternalOutput").ap()
    nc_ps.clear()
    build(nc, A, out)
    r = run_bass_kernel_spmd(nc, [arrays], core_ids=[0])
    o = r.results[0]["out"]
    return np.ascontiguousarray(o.transpose(2, 1, 0)).reshape(1, TX, D)
```

```python
import concourse.bass as bass
from concourse import mybir
import numpy as np

F32 = mybir.dt.float32
F32R = mybir.dt.float32r
BF16 = mybir.dt.bfloat16
U16 = mybir.dt.uint16
ACT = mybir.ActivationFunctionType
ALU = mybir.AluOpType
AX = mybir.AxisListType.X

D = 1024
KT = 8
NMETA = 16
TX = 512
TC = 256
T1 = NMETA + TX
NFF = 22
CH = [(0, 8), (8, 7), (15, 7)]
ALPHA = (2 * 2) ** 0.25
GAMMA = [1.0 - 2.0 ** (-5 - h) for h in range(4)]
BASE = 16512

VEC = {}
_n = 0
for _name, _w in [("ffn1", 8), ("mix", 8), ("ffn2", 8), ("bgate", 16), ("retgn", 8), ("fq", 1), ("fk", 1),
                  ("bf", 1), ("c", 16), ("bmod0", 48), ("bmod1", 48), ("gq0", 1), ("gk0", 1), ("gq1", 1),
                  ("gk1", 1), ("gout0", 8), ("gout1", 8), ("ln1g0", 8), ("ln1g1", 8), ("ln1b0", 8),
                  ("ln1b1", 8), ("ln2g0", 8), ("ln2g1", 8), ("ln2b0", 8), ("ln2b1", 8), ("bs0", 4), ("bs1", 4)]:
    VEC[_name] = (_n, _w)
    _n += _w
NVEC = _n


class Tok:

    def __init__(self, eng, idx):
        self.eng, self.idx = eng, idx


class Call:

    def matmul(self, *a, **k):
        self.make = lambda e: e.matmul(*a, **k)

    def transpose(self, *a, **k):
        self.make = lambda e: e.transpose(*a, **k)

    def activation(self, *a, **k):
        self.make = lambda e: e.activation(*a, **k)

    def tensor_tensor(self, *a, **k):
        self.make = lambda e: e.tensor_tensor(*a, **k)

    def tensor_scalar(self, *a, **k):
        self.make = lambda e: e.tensor_scalar(*a, **k)

    def scalar_tensor_tensor(self, *a, **k):
        self.make = lambda e: e.scalar_tensor_tensor(*a, **k)

    def tensor_tensor_scan(self, *a, **k):
        self.make = lambda e: e.tensor_tensor_scan(*a, **k)

    def tensor_reduce(self, *a, **k):
        self.make = lambda e: e.tensor_reduce(*a, **k)

    def tensor_copy(self, *a, **k):
        self.make = lambda e: e.tensor_copy(*a, **k)

    def reciprocal(self, *a, **k):
        self.make = lambda e: e.reciprocal(*a, **k)

    def bn_stats(self, *a, **k):
        self.make = lambda e: e.bn_stats(*a, **k)

    def bn_aggr(self, *a, **k):
        self.make = lambda e: e.bn_aggr(*a, **k)

    def memset(self, *a, **k):
        self.make = lambda e: e.memset(*a, **k)

    def dma_start(self, *a, **k):
        self.make = lambda e: e.dma_start(*a, **k)

    def wait_ge(self, *a, **k):
        self.make = lambda e: e.wait_ge(*a, **k)


class Queue:

    def __init__(self, name, sem):
        self.name, self.sem, self.items, self.marked = name, sem, [], set()

    def op(self, fn, *waits, dma=None):
        ws = []
        call = Call()
        fn(call)

        def flat(w):
            if w is None:
                return
            if isinstance(w, (list, tuple)) and not (len(w) == 2 and isinstance(w[1], int)):
                for x in w:
                    flat(x)
            else:
                ws.append(w)
        flat(list(waits))
        for w in ws:
            if isinstance(w, Tok):
                w.eng.marked.add(w.idx)
        self.items.append((ws, call.make, dma))
        return Tok(self, len(self.items) - 1)

    def last(self):
        n = len(self.items) - 1
        while n >= 0 and self.items[n][2] is not None:
            n -= 1
        return Tok(self, n) if n >= 0 else None

    def count(self):
        self.value, n = {}, 0
        for i in sorted(self.marked):
            n += 1
            self.value[i] = n

    def emit(self, e):
        seen = {}
        for i, (ws, make, dma) in enumerate(self.items):
            need = {}
            for w in ws:
                sem, v = (w.eng.sem, w.eng.value[w.idx]) if isinstance(w, Tok) else w
                k = id(sem)
                if v > seen.get(k, 0) and v > need.get(k, (None, 0))[1]:
                    need[k] = (sem, v)
            for k, (sem, v) in need.items():
                e.wait_ge(sem, v)
                seen[k] = v
            inst = make(e)
            if dma is not None:
                inst.then_inc(dma, 16)
            if i in self.marked:
                inst.then_inc(self.sem, 1)


class DmaSem:

    def __init__(self, sem):
        self.sem, self.n = sem, 0

    def add(self, q, fn, *waits):
        q.op(fn, *waits, dma=self.sem)
        self.n += 16
        return (self.sem, self.n)


def build(nc, A, out):
    order = []
    _program(nc, A, out, order, True)
    _program(nc, A, out, order, False)


def _program(nc, A, out, order, dry):
    nosem = [0]

    def sem(name):
        if dry:
            nosem[0] += 1
            return nosem[0]
        return nc.alloc_semaphore(name)

    PE, DVE, AC, PL, SP = (Queue(n, sem("s_" + n)) for n in ("pe", "dve", "act", "pool", "sp"))

    tag = ["d" if dry else "r"]

    def at(name, shape, dt, offset):
        assert offset % 32 == 0, (name, offset)
        t = nc.alloc_sbuf_tensor_at(f"{tag[0]}_{name}", shape, dt, offset=BASE + offset)
        size = 4
        for s in shape[1:]:
            size *= s
        if dt in (BF16, U16):
            size //= 2
        ends.append((name, offset, offset + size))
        assert BASE + offset + size <= 229368, (name, offset + size)
        return t, (offset + size + 31) // 32 * 32

    ends = []
    H, p = at("H", [128, KT, NMETA + TX + TC], F32, 0)
    NW, NS, AHEAD = 4, 3, 1
    Wf, p = at("Wf", [128, NW, 1024], F32, p)
    Wh, p = at("Wh", [128, NS, 1024], F32R, p)
    Wl, p = at("Wl", [128, NS, 1024], F32R, p)
    V, p = at("V", [128, NVEC], F32, p)
    CF, p = at("CF", [128, 5, 128], F32, p)
    CB, p = at("CB", [128, 2, 128], U16, p)
    SC, p = at("SC", [128, 8, 2], F32, p)
    MOD, p = at("MOD", [128, 2, 48, 2], F32, p)
    RS, p = at("RS", [128, 3, 528], F32, p)
    SM, p = at("SM", [128, 112], F32, p)
    P0 = p
    ONES, BLK, IDF, PRM, PAX = (CF[:, i, :] for i in range(5))
    IDB, MSKB = CB[:, 0, :].bitcast(BF16), CB[:, 1, :].bitcast(BF16)

    def vec(name, k=0):
        return V[:, VEC[name][0] + k:VEC[name][0] + k + 1]

    if dry:
        PS = nc_ps[0] if nc_ps else None
        if PS is None:
            PS = nc.alloc_psum_tensor("PS", [128, 8, 512], F32)
            nc_ps.append(PS)
    else:
        PS = nc_ps[0]

    bank = {"next": 0, "free": [[] for _ in range(8)], "out": [False] * 8}

    shared = {"a": [0, 2], "b": [4], "c": [6], None: [7]}
    turn = {"a": 0, "b": 0, "c": 0, None: 0}
    divided = [False]

    def take(n=1, part=None):
        if divided[0]:
            b = shared[part][turn[part] % len(shared[part])]
            turn[part] += 1
            w = []
            for i in range(b, b + n):
                assert not bank["out"][i], "bank in use"
                bank["out"][i] = True
                w += bank["free"][i]
            return b, w
        b = bank["next"]
        while (n == 2 and b % 2) or any(bank["out"][b:b + n]):
            b = (b + 1) % 8
        bank["next"] = (b + n) % 8
        w = []
        for i in range(b, b + n):
            assert not bank["out"][i], "bank in use"
            bank["out"][i] = True
            w += bank["free"][i]
        return b, w

    def give(b, toks, n=1):
        for i in range(b, b + n):
            assert bank["out"][i]
            bank["out"][i] = False
            bank["free"][i] = list(toks)

    def psb(b, n=512, p=128):
        return PS[0:p, b, 0:n]

    def psb2(b, a, z, p=128):
        return PS[:, :, :].rearrange("p b n -> p (b n)")[0:p, b * 512 + a:b * 512 + z]

    def fence():
        return [q.last() for q in (PE, DVE, AC, PL) if q.last()]

    fence_tok = [[]]

    def barrier():
        f = fence()
        fence_tok[0] = f
        for q in (PE, DVE, AC, PL):
            q.fence = f
        return f

    def F():
        return fence_tok[0]

    wsem = [DmaSem(sem(f"s_w{i}")) for i in range(NW)]
    W = {"loaded": 0, "split": 0, "used": 0, "nsplit": 0}
    u_arrived, u_ready, u_slot, wf_free, ws_free = {}, {}, {}, {}, {}

    def w_pump():
        moved = True
        while moved:
            moved = False
            i = W["loaded"]
            if i < len(order) and (i < NW or i - NW in wf_free):
                name, idx, cols, raw = order[i]
                src = A[name]
                for j in idx:
                    src = src[j]
                u_arrived[i] = wsem[i % NW].add(SP, lambda e: e.dma_start(Wf[:, i % NW, 0:cols], src),
                                                wf_free.get(i - NW))
                W["loaded"] += 1
                moved = True
            i = W["split"]
            if i < W["loaded"] and i <= W["used"] + AHEAD:
                name, idx, cols, raw = order[i]
                f = Wf[:, i % NW, 0:cols]
                if raw:
                    u_slot[i], u_ready[i] = i % NW, u_arrived[i]
                elif W["nsplit"] < NS or W["nsplit"] - NS in ws_free:
                    n = W["nsplit"]
                    s = n % NS
                    h, l = Wh[:, s, 0:cols], Wl[:, s, 0:cols]
                    hi = AC.op(lambda e: e.activation(h, f, ACT.Copy), u_arrived[i], ws_free.get(n - NS))
                    lo = DVE.op(lambda e: e.tensor_tensor(l, f, h.bitcast(F32), ALU.subtract), hi)
                    u_slot[i], u_ready[i] = s, lo
                    wf_free[i] = lo
                    W["nsplit"] += 1
                else:
                    continue
                W["split"] += 1
                moved = True

    def w_get(name, idx, cols, raw=False):
        i = W["used"]
        W["used"] += 1
        if dry:
            order.append((name, idx, cols, raw))
            return i, 0, None
        assert order[i] == (name, idx, cols, raw)
        w_pump()
        return i, u_slot[i], u_ready[i]

    def w_done(i, tok, raw=False):
        if dry:
            return
        if raw:
            wf_free[i] = tok
        else:
            ws_free[sum(1 for u in order[:i] if not u[3])] = tok
        w_pump()

    def mm3(o, wh, wl, xh, xl, first, last, *waits, wmain=True):
        PE.op(lambda e: e.matmul(o, wh, xh, start=first, stop=False), *waits)
        PE.op(lambda e: e.matmul(o, wh, xl, start=False, stop=False))
        return PE.op(lambda e: e.matmul(o, wl, xh, start=False, stop=last))

    def over(toks, c0, n, k):
        return [tk[k] for a, w, tk in toks if a < c0 + n and c0 < a + w]

    def lin(name, idx, kt, X, off, chunks, *waits, each=None, by=(), first=0):
        u, s, ready = w_get(name, idx, kt * 128)
        res = []
        for c0, n in chunks:
            b, bw = take()
            ks = [(first + k) % kt for k in range(kt)]
            for k in ks:
                w = Wh[:, s, k * 128:k * 128 + 128], Wl[:, s, k * 128:k * 128 + 128]
                t = mm3(psb(b, n), *w, X[0][:, k, c0 - off:c0 - off + n], X[1][:, k, c0 - off:c0 - off + n],
                        k == ks[0], k == ks[-1], ready, bw, waits, over(by, c0, n, k))
            if each:
                each(c0, n, b, t)
            res.append((b, t))
        w_done(u, t)
        return res

    def lin_pair(name, idx, kt, X, off, chunks, by):
        u = [w_get(name, i, kt * 128) for i in idx]
        bs = [[take() for _ in chunks] for _ in u]
        for ks in (range(kt - 1), (kt - 1,)):
            for (un, s, ready), bb in zip(u, bs):
                for (c0, n), (b, bw) in zip(chunks, bb):
                    for k in ks:
                        w = Wh[:, s, k * 128:k * 128 + 128], Wl[:, s, k * 128:k * 128 + 128]
                        t = mm3(psb(b, n), *w, X[0][:, k, c0 - off:c0 - off + n],
                                X[1][:, k, c0 - off:c0 - off + n], k == 0, k == kt - 1, ready, bw,
                                over(by, c0, n, k))
        for un, s, ready in u:
            w_done(un, t)
        return [[(b, t) for b, bw in bb] for bb in bs]

    def lin_tok(name, g, X, tiles, epi, *waits, by=(), shift=0):
        u0, s0, r0 = w_get(name, (g, 0), 1024)
        u1, s1, r1 = w_get(name, (g, 1), 1024)
        for i, c0 in enumerate(tiles):
            b, bw = take()
            for k in range(8):
                s = (s0, s1)[k // 4]
                a = (k % 4) * 256
                o = psb(b, 256)
                xh, xl = X[0][:, k, c0:c0 + 128], X[1][:, k, c0:c0 + 128]
                wh, wl = Wh[:, s, a:a + 256], Wl[:, s, a:a + 256]
                t = mm3(o, xh, xl, wh, wl, k == 0, k == 7, (r0, r1)[k // 4], bw, waits,
                        over(by, c0 + shift, 128, k))
                if k == 3:
                    t_half = t
            give(b, epi(i, b, t))
        w_done(u0, t_half)
        w_done(u1, t)

    s_in = [DmaSem(sem(f"s_in{i}")) for i in range(4)]
    x_in = []
    for i in range(4):
        x_in.append(s_in[i].add(SP, lambda e: e.dma_start(H[:, 2 * i:2 * i + 2, 0:T1],
                                                          A["x0"][:, 2 * i:2 * i + 2, :])))
    s_con = DmaSem(sem("s_con"))
    for dst, src in ((V[:, :], A["vec"]), (CF[:, :, :], A["cf"]), (CB[:, :, :], A["cb"])):
        t_in = s_con.add(AC, lambda e, dst=dst, src=src: e.dma_start(dst, src))
    s_ctx = DmaSem(sem("s_ctx"))
    t_ctx = s_ctx.add(PL, lambda e: e.dma_start(H[:, :, T1:T1 + TC], A["ctx"]))
    for q in (PE, DVE, AC, PL):
        q.fence = []
    n_load = []

    def load(dst, src, *waits):
        n_load.append(DmaSem(sem(f"s_ld{len(n_load)}")))
        return n_load[-1].add(PL, lambda e: e.dma_start(dst, src), *waits)

    c0v = VEC["c"][0]
    SCT = SM[:, 80:96]
    t = AC.op(lambda e: e.activation(SCT, V[:, c0v:c0v + 16], ACT.Silu), t_in)
    t_sc = DVE.op(lambda e: e.tensor_copy(SC[:, :, :].rearrange("p k c -> p (k c)"), SCT), t)
    mods = [(l, m) for l in range(2) for m in range(48)]
    mod_tok = [None, None]

    def mod_until(l, part):
        while mods and mods[0] < (l, part * 8 + 8):
            mod_step()
        return mod_tok[l]

    def mod_step(count=1):
        count = min(count, len(mods))
        if not count:
            return
        b, bw = take()
        done = []
        for j in range(count):
            l, m = mods.pop(0)
            u, s, ready = w_get("wmod", (l, m), 1024, True)
            o = psb2(b, 2 * j, 2 * j + 2)
            for k in range(8):
                t = PE.op(lambda e, k=k: e.matmul(o, Wf[:, s, k * 128:k * 128 + 128], SC[:, k, :],
                                                  start=k == 0, stop=k == 7), ready, bw, t_sc)
            w_done(u, t, True)
            done.append((l, m, o))
        for l, m, o in done:
            part, name = m // 8, f"bmod{l}"
            one = 1.0 if part in (1, 4) else 0.0
            mod_tok[l] = DVE.op(lambda e: e.tensor_scalar(MOD[:, l, m, :], o, vec(name, m), one, ALU.add,
                                                          ALU.add), t)
        give(b, [mod_tok[l]])

    def mod(l, part, k, c):
        return MOD[:, l, part * 8 + k, c:c + 1]

    def rsqrt(x, y, t, ready, mul=1.0, *waits):
        return newton(x, y, t, AC.op(lambda e: e.activation(y, x, ACT.Sqrt), ready, waits), mul)

    def newton(x, y, t, a, mul):
        a = DVE.op(lambda e: e.reciprocal(y, y), a)
        a = DVE.op(lambda e: e.tensor_tensor(t, y, y, ALU.mult), a)
        a = DVE.op(lambda e: e.scalar_tensor_tensor(t, t, -0.5 * mul, x, ALU.mult, ALU.mult), a)
        return DVE.op(lambda e: e.scalar_tensor_tensor(y, t, 1.5 * mul, y, ALU.add, ALU.mult), a)

    def norm_all(*a):
        begin, finish, toks = norm_plan(*a[:9])
        begin()
        finish(n_mods=a[9] if len(a) > 9 else 0)
        return toks

    def norm_plan(kind, blocks, scale, bias, dst, off, tmp, ready, free=()):
        XC, q = at(f"XC{tmp}_{nid[0]}", [128, 2, 8, 264], F32, tmp)
        SQ, q = at(f"SQ{tmp}_{nid[0]}", [128, 8, 264], F32, q)
        MU, q = at(f"MU{tmp}_{nid[0]}", [128, 2, 264], F32, q)
        nid[0] += 1
        S = [dict() for _ in blocks]
        sq_read = [None] * 8

        def view(i):
            c0, n, c = blocks[i]
            hs = [H[:, k, c0:c0 + n] for k in range(8)]
            xc = [XC[:, i % 2, k, 0:n] for k in range(8)]
            return c0, n, c, hs, xc, (hs if kind == "rms" else xc)

        def statistics(i):
            c0, n, c, hs, xc, src = view(i)
            before = S[i - 2]["read"] if i >= 2 else [None] * 8
            xs = [None] * 8
            if kind == "ln":
                b, bw = take()
                for k in range(8):
                    t = PE.op(lambda e, k=k: e.matmul(psb(b, n), ONES, hs[k], start=k == 0, stop=k == 7),
                              bw, over(ready, c0, n, k))
                mu = MU[:, i % 2, 0:n]
                m = AC.op(lambda e: e.activation(mu, psb(b, n), ACT.Copy), t, free, before)
                give(b, [m])
                for k in range(8):
                    q = PL if k % 3 == 2 else DVE
                    xs[k] = q.op(lambda e, k=k: e.tensor_tensor(xc[k], hs[k], mu, ALU.subtract), m,
                                 before[k], free)
            S[i]["xs"] = xs

        def squares(i):
            c0, n, c, hs, xc, src = view(i)
            xs = S[i]["xs"]
            b, bw = take()
            for k in range(8):
                w = xs[k], free, sq_read[k], over(ready, c0, n, k)
                if kind == "rms" and k % 3 == 2:
                    t = PL.op(lambda e, k=k: e.tensor_tensor(SQ[:, k, 0:n], src[k], src[k], ALU.mult), w)
                else:
                    t = AC.op(lambda e, k=k: e.activation(SQ[:, k, 0:n], src[k], ACT.Square), w)
                t = PE.op(lambda e, k=k: e.matmul(psb(b, n), ONES, SQ[:, k, 0:n], start=k == 0, stop=k == 7),
                          t, bw)
                sq_read[k] = t
            S[i].update(b=b, t=t)

        def root(i):
            c0, n, c, hs, xc, src = view(i)
            a = 264 * (i % 2)
            x, y, w = (RS[:, j, a:a + n] for j in range(3))
            b = S[i]["b"]
            t = DVE.op(lambda e: e.tensor_scalar(x, psb(b, n), 1e-6, None, ALU.add), S[i]["t"], free,
                       rs_last[i % 2])
            give(b, [t])
            t = AC.op(lambda e: e.activation(y, x, ACT.Sqrt), t)
            S[i].update(r=y, root=(x, y, w, t))

        def apply(i):
            c0, n, c, hs, xc, src = view(i)
            r, t, read, end = S[i]["r"], newton(*S[i]["root"], 1.0), [], []
            before = S[i - 2]["read"] if i >= 2 and kind == "rms" else [None] * 8
            late = []
            for k in range(8):
                u = DVE.op(lambda e, k=k: e.scalar_tensor_tensor(xc[k], src[k], scale(k, c), r, ALU.mult,
                                                                 ALU.mult), t, S[i]["xs"][k], sq_read[k],
                           before[k], free)
                rs_last[i % 2] = u
                if dst is None:
                    u = AC.op(lambda e, k=k: e.activation(hs[k], xc[k], ACT.Identity, bias=bias(k, c)), u)
                    read.append([u])
                    end.append(u)
                    continue
                xh, xl = dst[0][:, k, c0 - off:c0 - off + n], dst[1][:, k, c0 - off:c0 - off + n]
                q = PL if k % 2 else DVE
                if bias is None:
                    u = AC.op(lambda e, k=k, xh=xh: e.activation(xh, xc[k], ACT.Copy), u, free)
                    late.append((q, u, lambda e, k=k, xh=xh, xl=xl: e.tensor_tensor(
                        xl, xc[k], xh.bitcast(F32), ALU.subtract)))
                else:
                    u = AC.op(lambda e, k=k, xh=xh: e.activation(xh, xc[k], ACT.Identity,
                                                                 bias=bias(k, c)), u, free)
                    late.append((DVE, u, lambda e, k=k, xh=xh, xl=xl: e.scalar_tensor_tensor(
                        xl, xc[k], bias(k, c), xh.bitcast(F32), ALU.add, ALU.subtract)))
                for q, u, fn in (late[-3:-2] if k < 7 else late[-3:]):
                    v = q.op(fn, u, free)
                    read.append([u, v])
                    end.append(v)
            S[i]["read"] = read
            return c0, n, end

        out_toks = []

        def begin():
            statistics(0)
            squares(0)

        def finish(n_mods=0, lead=None):
            for i in range(len(blocks)):
                if i + 1 < len(blocks):
                    statistics(i + 1)
                    squares(i + 1)
                elif lead:
                    lead()
                root(i)
                out_toks.append(apply(i))
            mod_step(n_mods)
        return begin, finish, out_toks

    nid = [0]
    rs_last = [None, None]

    def ffn(tagw, X, off, chunks, HH, HL, TM, by, ready, gate, mods_per):
        free = [[], []]
        n_tm = [0]
        hw = {}
        hid_free = []
        h_end = {c0: [] for c0, n in chunks}
        for ci, (j0, nj) in enumerate(CH):
            hid = [(c0, n, []) for c0, n in chunks]

            def finish(j, ra, rb):
                for (c0, n), (ba, ta), (bb, tb), (_, _, done) in zip(chunks, ra, rb, hid):
                    i = n_tm[0] % 2
                    n_tm[0] += 1
                    x = TM[:, i, 0:n]
                    t = AC.op(lambda e: e.activation(x, psb(ba, n), ACT.Silu), ta, free[i], F())
                    give(ba, [t])
                    u = DVE.op(lambda e: e.tensor_tensor(x, x, psb(bb, n), ALU.mult), t, tb)
                    give(bb, [u])
                    hh, hl = HH[:, j, c0 - off:c0 - off + n], HL[:, j, c0 - off:c0 - off + n]
                    v = AC.op(lambda e: e.activation(hh, x, ACT.Copy), u, hid_free)
                    w = PL.op(lambda e: e.tensor_tensor(hl, x, hh.bitcast(F32), ALU.subtract), v, hid_free)
                    free[i] = [w]
                    done.append(w)

            for j in range(nj):
                ra = lin(tagw + "_in", (j0 + j,), 8, X, off, chunks, by=by)
                rb = lin(tagw + "_in", (NFF + j0 + j,), 8, X, off, chunks, by=by)
                finish(j, ra, rb)
            mod_step(mods_per)
            pair = None
            for m in range(8):
                if m == 0:
                    pair = lin_pair(f"{tagw}_out{ci}", ((0,), (1,)), nj, (HH, HL), off, chunks, hid)
                r = pair[m] if m < 2 else lin(f"{tagw}_out{ci}", (m,), nj, (HH, HL), off, chunks)
                for (c0, n), (b, t) in zip(chunks, r):
                    hk = H[:, m, c0:c0 + n]
                    g = gate(m, c0)
                    t2 = DVE.op(lambda e: e.scalar_tensor_tensor(hk, psb(b, n), g, hk, ALU.mult, ALU.add),
                                t, hw.get((m, c0)), ready)
                    give(b, [t2])
                    hw[m, c0] = t2
                    if ci == len(CH) - 1:
                        h_end[c0].append(t2)
                    hid_free = [t]
        return [(c0, n, h_end[c0]) for c0, n in chunks]

    def attention(units, Pb, PT, values, done=None):
        st = [dict() for _ in units]
        pfree = [[], [], []]
        ptfree = [[], []]

        def step_a(u):
            d, s = units[u], st[u]
            i = u % 3
            if "pre" in d:
                d["pre"]()
            b, bw = take(2, "a")
            n = d["n"]
            parts = [(0, max(256, min(n, 512)))] + ([(512, n)] if n > 512 else [])
            for a, z in parts:
                extra = [x for x in d.get("add", []) if x[2] >= a and x[2] < z]
                (q1, k1), (q2, k2) = d["qk"](a, z)
                PE.op(lambda e: e.matmul(psb2(b, a, z), q1, k1, start=True, stop=False), bw, d["ready"], F())
                t = PE.op(lambda e: e.matmul(psb2(b, a, z), q2, k2, start=False, stop=not extra))
                d["used"][:] = [t]
                for x in extra:
                    rhs = x[1](x[2], x[3])
                    t = PE.op(lambda e: e.matmul(psb2(b, x[2], x[3]), x[0], rhs, start=False,
                                                 stop=x is extra[-1]), d["ready"])
            lg = psb2(b, 0, n)
            if "bias" in d:
                m = d["bias"]
                t = DVE.op(lambda e: e.tensor_tensor(psb2(b, 0, 512), psb2(b, 0, 512), m, ALU.add), t,
                           br_tok[d["bias_ready"]])
            mx = SM[:, u % 4:u % 4 + 1]
            s["mx_t"] = DVE.op(lambda e: e.tensor_reduce(mx, lg, AX, ALU.max, negate=True), t,
                               st[u - 4]["exp"] if u >= 4 else None)
            s["a"] = (i, b, n, lg, mx)

        def step_exp(u):
            s = st[u]
            i, b, n, lg, mx = s["a"]
            rs = SM[:, 4 + u % 4:5 + u % 4]
            t = AC.op(lambda e: e.activation(Pb[:, i, 0:n], lg, ACT.Exp, bias=mx, accum_out=rs), s["mx_t"],
                      pfree[i], st[u - 4]["rc_t"] if u >= 4 else None)
            give(b, [t], 2)
            s["exp"], s["rs"] = t, rs

        def step_b(u):
            d, s = units[u], st[u]
            i, i3 = u % 2, u % 3
            b, bw = take(2, "b")
            full = [x for x in d["blocks"] if x[1] == 128]
            part = [x for x in d["blocks"] if x[1] < 128]
            for j, (c, w, v) in enumerate(full):
                t = PE.op(lambda e: e.transpose(psb2(b, j * 128, j * 128 + 128), Pb[:, i3, c:c + 128], IDF),
                          s["exp"], bw)
            for j, (c, w, v) in enumerate(part):
                t = PE.op(lambda e: e.matmul(psb2(b, 512, 640, w), Pb[:, i3, c:c + w], IDF, start=True,
                                             stop=True), s["exp"], bw)
            n = len(full) * 128
            q = AC
            cp = (lambda e, o, x: e.activation(o, x, ACT.Copy)) if q is AC else (
                lambda e, o, x: e.tensor_copy(o, x))
            t2 = q.op(lambda e: cp(e, PT[:, i, 0:n], psb2(b, 0, n)), t, ptfree[i], F())
            s["pt"] = [t2]
            if part:
                w = part[0][1]
                t2 = q.op(lambda e: cp(e, PT[0:w, i, 512:640], psb2(b, 512, 640, w)), t)
                s["pt"] = [t2]
            give(b, [t2], 2)
            rc = SM[:, 8 + 2 * (u % 4):9 + 2 * (u % 4)]
            s["rc"] = rc
            s["rc_t"] = DVE.op(lambda e: e.reciprocal(rc, s["rs"]), s["exp"],
                               st[u - 4]["o"] if u >= 4 else None)
            pfree[i3] = [t, s["exp"]]

        def step_c(u):
            d, s = units[u], st[u]
            i = u % 2
            b, bw = take(1, "c")
            full = [x for x in d["blocks"] if x[1] == 128]
            part = [x for x in d["blocks"] if x[1] < 128]
            o = psb(b, 128)
            seq = [(PT[:, i, j * 128:j * 128 + 128], x[2]) for j, x in enumerate(full)]
            seq += [(PT[0:x[1], i, 512:640], x[2]) for x in part]
            for j, (l, r) in enumerate(seq):
                t = PE.op(lambda e: e.matmul(o, l, r, start=j == 0, stop=j == len(seq) - 1), s["pt"],
                          bw,
                          d["vready"])
            ptfree[i] = [t]
            o = psb2(b, 64 * d["half"], 64 * d["half"] + 64)
            s["o"] = DVE.op(lambda e: e.tensor_scalar(d["out"], o, s["rc"], None, ALU.mult), t, s["rc_t"],
                            F())
            if done:
                done[0] = s["o"]
            give(b, [s["o"]])

        divided[0] = True
        shared["c"] = values
        for u in range(len(units) + 3):
            if u < len(units):
                step_a(u)
            if 2 <= u <= len(units) + 1:
                step_b(u - 2)
            if u < len(units):
                step_exp(u)
            if u >= 3:
                step_c(u - 3)
        divided[0] = False
        return st[-1]["o"]

    def stack_q(q, r0, dst, *waits, eng=None):
        o = 64 - r0
        hi = dst[r0:r0 + 64]
        t = AC.op(lambda e: e.activation(hi, q, ACT.Copy), waits, PL.last())
        return [t, (eng or PL).op(lambda e: e.tensor_tensor(dst[o:o + 64], q, hi.bitcast(F32),
                                                            ALU.subtract), t)]

    def stack_k(k, r0, dst, lo, twice, *waits):
        o = 64 - r0
        hi = dst[r0:r0 + 64]
        t = AC.op(lambda e: e.activation(hi, k, ACT.Copy), waits)
        u = [AC.op(lambda e: e.activation(dst[o:o + 64], k, ACT.Copy), waits),
             PL.op(lambda e: e.tensor_tensor(lo[r0:r0 + 64], k, hi.bitcast(F32), ALU.subtract), t, waits)]
        if twice:
            u.append(DVE.op(lambda e: e.tensor_tensor(lo[o:o + 64], k, hi.bitcast(F32), ALU.subtract), t,
                           waits))
        return u

    def head_rms(raw, n, g, mul, ready, SQt, wfree):
        t = AC.op(lambda e: e.activation(SQt[:, 0:n], raw, ACT.Square), ready, list(wfree))
        b, bw = take()
        t2 = PE.op(lambda e: e.matmul(psb(b, n), BLK, SQt[:, 0:n], start=True, stop=True), t, bw)
        wfree[:] = [t2]
        x, r, y = (RS[:, j, 0:n] for j in range(3))
        t3 = DVE.op(lambda e: e.tensor_scalar(x, psb(b, n), 1e-6, None, ALU.add), t2, rsfree)
        give(b, [t3])
        t3 = AC.op(lambda e: e.activation(r, x, ACT.Sqrt), t3)

        def second():
            t4 = newton(x, r, y, t3, mul)
            t5 = DVE.op(lambda e: e.scalar_tensor_tensor(raw, raw, g, r, ALU.mult, ALU.mult), t4)
            rsfree[:] = [t5]
            return t5
        return second

    rsfree = []
    br_tok = {}

    def to_features(TOKN, tiles, cols, fn, ready):
        for f in cols:
            for g0 in range(0, len(tiles), 4):
                b, bw = take()
                grp = tiles[g0:g0 + 4]
                for j, i in enumerate(grp):
                    t = PE.op(lambda e, i=i, j=j: e.transpose(psb2(b, j * 128, j * 128 + 128),
                                                              TOKN[:, i, f * 128:f * 128 + 128], IDF),
                              ready, bw)
                give(b, fn(f, tiles[g0] * 128, len(grp) * 128, b, t))

    XH, p = at("X1h", [128, 8, T1], F32R, P0)
    XL, p = at("X1l", [128, 8, T1], F32R, p)
    P1 = p
    HH, p = at("H1h", [128, 8, T1], F32R, P1)
    HL, p = at("H1l", [128, 8, T1], F32R, p)
    TM, p = at("TM1", [128, 2, 264], F32, p)
    X = (XH, XL)
    chunks = [(0, 264), (264, 264)]
    nb1 = [(0, 264, 0), (264, 264, 0)]
    by = norm_all("rms", nb1, lambda k, c: vec("ffn1", k), None, X, 0, p, 
                  [(0, T1, [[x_in[k // 2], t_in] for k in range(8)])], (), 4)
    e = ffn("f1", X, 0, chunks, HH, HL, TM, by, [], lambda m, c0: 0.5, 3)
    by = norm_all("rms", nb1, lambda k, c: vec("mix", k), None, X, 0, p, e, PE.last(), 6)
    barrier()

    YB, p = at("YB", [128, 8, TX], F32, P1 + 8 * TX * 4)
    P2 = p
    RQ, p = at("RQ", [128, 4, TX], F32, P2)
    RK, p = at("RK", [128, 4, T1], F32, p)
    VR, p = at("VR", [128, 5, 1024], F32, p)
    P3 = p
    CS, p = at("CS", [128, 2, T1], F32, P3)
    RT, p = at("RT", [128, 2, T1], F32, p)
    tl = load(CS[:, :, :], A["rope1"], F())
    rfree = [[], []]
    idx = [0]
    rk_ready = []

    def rope(dst, c0, n, tabs, col, perm, ready, RTn, nrt=2):
        i = idx[0] % nrt
        idx[0] += 1
        b, bw = take()
        t = PE.op(lambda e: e.matmul(psb(b, n), perm, dst, start=True, stop=True), ready, bw)
        u = DVE.op(lambda e: e.tensor_tensor(RTn[:, i, 0:n], psb(b, n), tabs[:, 1, col:col + n], ALU.mult),
                   t, rfree[i], tl)
        give(b, [u])
        v = PL.op(lambda e: e.tensor_tensor(dst, dst, tabs[:, 0, col:col + n], ALU.mult), t, tl)

        def second():
            w = DVE.op(lambda e: e.tensor_tensor(dst, dst, RTn[:, i, 0:n], ALU.add), u, v)
            rfree[i] = [w]
            return w
        return second

    jobs = []

    def tick():
        for f in jobs.pop(0) if jobs else []:
            f()

    def flush():
        while jobs:
            tick()

    def at_tick(n, f):
        while len(jobs) <= n:
            jobs.append([])
        jobs[n].append(f)

    for dst, nm, chs in ((RK, "w_rk", chunks), (RQ, "w_rq", [(16, 512)])):
        for m in range(4):
            res = lin(nm, (m,), 8, X, 0, chs, by=by)
            tick()
            for j, ((c0, n), (b, t)) in enumerate(zip(chs, res)):
                a = c0 - (16 if dst is RQ else 0)
                o = dst[:, m, a:a + n]
                t = AC.op(lambda e: e.activation(o, psb(b, n), ACT.Copy), t, F())
                give(b, [t])
                hold = []
                at_tick(0, lambda o=o, c0=c0, n=n, t=t, hold=hold: hold.append(
                    rope(o, c0, n, CS, c0, PRM, t, RT)))
                at_tick(1, lambda hold=hold: rk_ready.append(hold[0]()))
    tiles1 = [0, 16, 144, 272, 400]

    def vcopy(dst, base, meta=False):
        def epi(i, b, t):
            rows = NMETA if i == 0 and meta else 128
            q = AC if i % 2 else DVE
            if q is AC:
                return [AC.op(lambda e: e.activation(dst[0:rows, i, base:base + 256], psb(b, 256, rows),
                                                     ACT.Copy), t, F())]
            return [DVE.op(lambda e: e.tensor_copy(dst[0:rows, i, base:base + 256], psb(b, 256, rows)), t,
                           F())]
        return epi

    for g in range(4):
        lin_tok("w_rv", g, X, tiles1, vcopy(VR, g * 256, True), by=by)
        tick()
    flush()
    barrier()
    DT, p = at("DT", [128, 4, T1], F32, P3)
    SS, p = at("SS", [128, 2, 5, 128], F32, p)
    YT, _ = at("YT", [128, 4, 1024], F32, P1)
    ST, p = at("ST", [128, 4, 8], F32, p)
    AG, p = at("AG", [128, 4, 4, 2], F32, p)
    AY, p = at("AY", [128, 2, 4, 4], F32, p)
    tl2 = load(DT[:, :, :], A["decay"], F())
    sfree = [[], []]
    units = [(h, i) for h in range(4) for i in range(4)]
    S = {}

    def ret_a(u):
        h, i = units[u]
        b, bw = take(2)
        q = RQ[:, h, i * 128:i * 128 + 128]
        for j in range(i + 1):
            k = RK[:, h, 16 + j * 128:144 + j * 128]
            t = PE.op(lambda e, j=j: e.matmul(psb2(b, j * 128, j * 128 + 128), k, q, start=True, stop=True),
                      bw, rk_ready, F())
        k = RK[:, h, 0:NMETA]
        t = PE.op(lambda e: e.matmul(psb2(b, 512, 640, NMETA), k, q, start=True, stop=True))
        s = SS[:, u % 2, :, :]
        for j in range(i + 1):
            a = (i - j) * 128
            t2 = DVE.op(lambda e, j=j, a=a: e.tensor_tensor(s[:, j, :], psb2(b, j * 128, j * 128 + 128),
                                                            DT[:, h, a:a + 128], ALU.mult), t, tl2,
                        sfree[u % 2], F())
        a = 16 + i * 128
        t2 = DVE.op(lambda e: e.tensor_tensor(s[0:NMETA, 4, :], psb2(b, 512, 640, NMETA),
                                              DT[0:NMETA, h, a:a + 128], ALU.mult), t)
        give(b, [t2], 2)
        S[u] = t2

    yt_toks = []

    def ret_b(u):
        h, i = units[u]
        b, bw = take()
        s = SS[:, u % 2, :, :]
        o = psb(b, 256)
        for j in range(i + 1):
            PE.op(lambda e, j=j: e.matmul(o, s[:, j, :], VR[:, j + 1, h * 256:h * 256 + 256], start=j == 0,
                                          stop=False), S[u], bw)
        t = PE.op(lambda e: e.matmul(o, s[0:NMETA, 4, :], VR[0:NMETA, 0, h * 256:h * 256 + 256],
                                     start=False, stop=True))
        sfree[u % 2] = [t]
        st, ag = ST[:, u % 4, 0:6], AG[:, h, i, :]
        v = DVE.op(lambda e: e.bn_stats(st, o), t, F())
        c = AC.op(lambda e: e.activation(YT[:, i, h * 256:h * 256 + 256], o, ACT.Copy), t, F(), v)
        give(b, [c])
        gn.append(DVE.op(lambda e: e.bn_aggr(ag, st), v))
        if i < 3:
            return
        var, y, w = AG[:, h, :, 1], AY[:, 0, h, :], AY[:, 1, h, :]
        v = DVE.op(lambda e: e.tensor_scalar(var, var, 1e-5, None, ALU.add), gn[-1])
        v = rsqrt(var, y, w, v)
        for j in range(4):
            yt = YT[:, j, h * 256:h * 256 + 256]
            yt_toks.append(DVE.op(lambda e: e.tensor_scalar(yt, yt, AG[:, h, j, 0:1], y[:, j:j + 1],
                                                            ALU.subtract, ALU.mult), v, c))

    gn = []
    SG, p = at("SG", [128, 8, 512], F32, p)
    sg_tok = []
    for u in range(len(units) + 1):
        if u < len(units):
            ret_a(u)
            if u % 2 == 0:
                m = u // 2
                (b, t), = lin("w_rg", (m,), 8, X, 0, [(16, 512)], by=by)
                t = AC.op(lambda e: e.activation(SG[:, m, :], psb(b), ACT.Silu), t, F())
                give(b, [t])
                sg_tok.append(t)
        if u >= 1:
            ret_b(u - 1)

    def to_yb(f, a, n, b, t):
        return [DVE.op(lambda e: e.scalar_tensor_tensor(YB[:, f, a:a + n], psb(b, n), vec("retgn", f),
                                                        SG[:, f, a:a + n], ALU.mult, ALU.mult), t,
                       sg_tok[f], F())]

    for f in range(8):
        to_features(YT, [0, 1, 2, 3], [f], to_yb, yt_toks[4 * (f // 2) + 3])
    barrier()

    Q, p = at("Q", [128, 2, TX], F32, P2)
    K, p = at("K", [128, 2, T1], F32, p)
    VF, p = at("VF", [128, 5, 1024], F32, p)
    SEL, p = at("SEL", [128, 16, 128], U16, p)
    CP, p = at("CP", [128, T1], BF16, p)
    SQT, p = at("SQT", [128, 2, T1], F32, p)
    Pb, p = at("Pb", [128, 3, 528], F32, p)
    PT, p = at("PT", [128, 2, 640], F32, p)
    QS, p = at("QS", [128, 2, TX], F32R, p)
    KS, p = at("KS", [128, 2, T1], F32R, p)
    KL, p = at("KL", [128, T1], F32R, p)
    RS2, p = at("RS2", [128, 3, 528], F32, p)
    YT, _ = at("YTF", [128, 4, 1024], F32, P1)
    LF, _ = at("LF", [16, 5, T1], F32, P1)
    tl = load(SEL[:, :, :], A["sel"], F())
    cz = PL.op(lambda e: e.memset(CP[:, :], 0.0), F())
    cfree = []
    res = lin("w_ff", (0,), 8, X, 0, chunks, by=by)
    z, az, u_, r_, s_ = (LF[:, i, :] for i in range(5))
    for (c0, n), (b, t) in zip(chunks, res):
        t = AC.op(lambda e: e.activation(z[:, c0:c0 + n], psb(b, n, 16), ACT.Identity, bias=V[0:16,
                  VEC["bf"][0]:VEC["bf"][0] + 1]), t, F())
        give(b, [t])
    t = AC.op(lambda e: e.activation(az, z, ACT.Abs), t)
    t = AC.op(lambda e: e.activation(az, az, ACT.Exp, scale=-1.0), t)
    t = DVE.op(lambda e: e.tensor_scalar(u_, az, 1.0, None, ALU.add), t)
    tl_n = AC.op(lambda e: e.activation(r_, u_, ACT.Ln), t)
    t = DVE.op(lambda e: e.scalar_tensor_tensor(s_, u_, -1.0, az, ALU.add, ALU.subtract), t)
    t = DVE.op(lambda e: e.reciprocal(u_, u_), t, tl_n)
    t = DVE.op(lambda e: e.tensor_tensor(s_, s_, u_, ALU.mult), t)
    t = DVE.op(lambda e: e.tensor_tensor(r_, r_, s_, ALU.subtract), t)
    t = DVE.op(lambda e: e.scalar_tensor_tensor(r_, z, 0.0, r_, ALU.min, ALU.subtract), t)
    t = DVE.op(lambda e: e.tensor_scalar(r_, r_, -1.0, None, ALU.mult), t)
    t = DVE.op(lambda e: e.memset(u_, 1.0), t)
    t = DVE.op(lambda e: e.tensor_tensor_scan(s_, u_, r_, 0.0, ALU.mult, ALU.add), t)
    t = DVE.op(lambda e: e.tensor_copy(CP[0:16, :], s_), t, cz)
    t = DVE.op(lambda e: e.tensor_tensor(s_, s_, CP[0:16, :], ALU.subtract), t)
    t = DVE.op(lambda e: e.tensor_copy(CP[32:48, :], s_), t)
    t = DVE.op(lambda e: e.tensor_copy(u_, CP[32:48, :]), t)
    t = DVE.op(lambda e: e.tensor_tensor(s_, s_, u_, ALU.subtract), t)
    c_ready = DVE.op(lambda e: e.tensor_copy(CP[64:80, :], s_), t)

    sqf = [[], []]
    nq = [0]
    raw_t = {}
    half = []
    stacked = {h: [] for h in range(16)}
    used = [[], []]

    def project(which, m, i, k0=0, k1=8):
        dst, nm, chs = (Q, "w_fq", [(16, 512)]) if which == "q" else (K, "w_fk", chunks)
        c0, n = chs[i]
        if i == 0 and k0 == 0:
            half[:] = w_get(nm, (m,), 1024)
            raw_t[which, m] = []
        u, s, ready = half[0:3]
        if k0 == 0:
            half[3:] = take()
        b, bw = half[3:]
        for k in range(k0, k1):
            w = Wh[:, s, k * 128:k * 128 + 128], Wl[:, s, k * 128:k * 128 + 128]
            t = mm3(psb(b, n), *w, XH[:, k, c0:c0 + n], XL[:, k, c0:c0 + n], k == 0, k == 7, ready, bw)
        if k1 == 8:
            a = c0 - (16 if dst is Q else 0)
            o = dst[:, m % 2, a:a + n]
            v = AC.op(lambda e: e.activation(o, psb(b, n), ACT.Copy), t, F(),
                      stacked[2 * m - 3] if m >= 2 else None)
            give(b, [v])
            j = nq[0] % 2
            nq[0] += 1
            v = AC.op(lambda e: e.activation(SQT[:, j, 0:n], o, ACT.Square), v, list(sqf[j]))
            raw_t[which, m].append((o, n, v, j))
            if i == len(chs) - 1:
                w_done(u, t)

    def root(which, m, i):
        o, n, t, j = raw_t[which, m][i]
        b, bw = take()
        t = PE.op(lambda e: e.matmul(psb(b, n), BLK, SQT[:, j, 0:n], start=True, stop=True), t, bw)
        sqf[j] = [t]
        x, r, y = (R2[j][:, c, 0:n] for c in range(3))
        t = DVE.op(lambda e: e.tensor_scalar(x, psb(b, n), 1e-6, None, ALU.add), t, r2free[j])
        give(b, [t])
        t = AC.op(lambda e: e.activation(r, x, ACT.Sqrt), t)
        raw_t[which, m][i] = o, n, t, j

    def refine(which, m, i):
        mul = 0.125 if which == "q" else 1.0
        o, n, t, j = raw_t[which, m][i]
        x, r, y = (R2[j][:, c, 0:n] for c in range(3))
        t = DVE.op(lambda e: e.reciprocal(r, r), t)
        t = PL.op(lambda e: e.tensor_tensor(y, r, r, ALU.mult), t, PL.last())
        t = PL.op(lambda e: e.tensor_tensor(y, y, x, ALU.mult), t)
        t = PL.op(lambda e: e.tensor_scalar(y, y, -0.5 * mul, 1.5 * mul, ALU.mult, ALU.add), t)
        t = PL.op(lambda e: e.tensor_tensor(r, r, y, ALU.mult), t)
        raw_t[which, m][i] = o, n, t, j

    def scale(which, m, i):
        o, n, t, j = raw_t[which, m][i]
        g, r = vec("fq" if which == "q" else "fk"), R2[j][:, 1, 0:n]
        t = DVE.op(lambda e: e.scalar_tensor_tensor(o, o, g, r, ALU.mult, ALU.mult), t)
        r2free[j] = [t]
        raw_t[which, m][i] = t

    R2 = [RS, RS2]
    r2free = [[], []]

    def stack(h):
        m, r0, s = h // 2, 64 * (h % 2), h % 2
        w = [raw_t["q", m], raw_t["k", m], list(used[s])]
        stacked[h] += stack_q(Q[r0:r0 + 64, m % 2, :], r0, QS[:, s, :], w)
        stacked[h] += stack_k(K[r0:r0 + 64, m % 2, :], r0, KS[:, s, :], KL, False, w)

    plan = [(0, project, "q", 0, 0, 3), (1, project, "q", 0, 3, 6), (2, project, "q", 0, 6, 8),
            (3, root, "q", 0), (3, project, "k", 0, 0, 4), (4, refine, "q", 0),
            (4, project, "k", 0, 4, 8), (5, root, "k", 0), (5, project, "k", 1, 0, 4),
            (6, scale, "q", 0), (6, refine, "k", 0), (6, project, "k", 1, 4, 8), (7, root, "k", 1),
            (8, scale, "k", 0), (8, refine, "k", 1), (10, scale, "k", 1), (10, stack, 0), (14, stack, 1)]
    steps = {}
    for m in range(8):
        for at_u, f, *a in plan:
            g = (lambda a=a, m=m: stack(2 * m + a[0])) if f is stack else (
                lambda f=f, a=a, m=m: f(a[0], m, *a[1:]))
            steps.setdefault(8 * m - 12 + at_u, []).append((m, g))
    project("q", 0, 0)
    project("k", 0, 0)
    root("q", 0, 0)
    project("k", 0, 1)
    after = [[(refine, "q", 0), (root, "k", 0)], [(scale, "q", 0), (refine, "k", 0)],
             [(root, "k", 1), (scale, "k", 0)], [(refine, "k", 1), (scale, "k", 1)]]
    for g in range(4):
        lin_tok("w_fv", g, X, tiles1, vcopy(VF, g * 256, True), by=by)
        for f, w, i in after[g]:
            f(w, 0, i)
    stack(0)
    divided[0] = True
    for n in sorted(n for n in steps if n < 0):
        for m, g in steps[n]:
            if m > 0:
                g()
    barrier()
    us = []
    for h in range(16):
        r0 = 64 * (h % 2)
        for i in range(4):
            n = 144 + 128 * i
            hs = h % 2
            pre = [g for m, g in steps.get(4 * h + i, [])]
            us.append({
                "pre": lambda pre=pre: [f() for f in pre],
                "qk": lambda a, z, i=i, r0=r0, s=hs: (
                    (QS[:, s, i * 128:i * 128 + 128], KS[:, s, a:z]),
                    (QS[r0:r0 + 64, s, i * 128:i * 128 + 128], KL[r0:r0 + 64, a:z])),
                "n": n,
                "used": used[hs],
                "add": [(IDB, lambda a, z, i=i: MSKB[:, a - 16 - 128 * i:z - 16 - 128 * i], 16 + 128 * i, n),
                        (SEL[:, h, :].bitcast(BF16), lambda a, z: CP[:, a:z], 0, max(n, 256))],
                "half": h % 2,
                "blocks": [(16 + 128 * j, 128, VF[:, j + 1, h // 2 * 128:h // 2 * 128 + 128])
                           for j in range(i + 1)] + [(0, 16, VF[0:16, 0, h // 2 * 128:h // 2 * 128 + 128])],
                "ready": [stacked[h], c_ready, tl], "vready": [],
                "out": YT[:, i, h * 64:h * 64 + 64]})
    for d in us:
        if d["n"] > 512:
            (l1, f1, a1, z1), (l0, f0, a0, z0) = d["add"]
            d["add"] = [(l1, f1, a1, 512), (l0, f0, 0, 512), (l1, f1, 512, z1), (l0, f0, 512, z0)]
    t = attention(us, Pb, PT, [6])
    barrier()
    YA, _ = at("YA", [128, 8, TX], F32, P2)

    def to_ya(f, a, n, b, t):
        return [AC.op(lambda e: e.activation(YA[:, f, a:a + n], psb(b, n), ACT.Copy), t, F())]

    to_features(YT, [0, 1, 2, 3], range(8), to_ya, t)
    barrier()

    def split(src, h, l, *waits):
        for k in range(8):
            t = AC.op(lambda e, k=k: e.activation(h[:, k, :], src[:, k, :], ACT.Copy), waits)
            t = DVE.op(lambda e, k=k: e.tensor_tensor(l[:, k, :], src[:, k, :], h[:, k, :].bitcast(F32),
                                                      ALU.subtract), t, waits)
        return t

    M1, _ = at("M1", [128, 8, TX], F32, P1)
    YH, p = at("YAh", [128, 8, TX], F32R, P2 + 8 * TX * 4)
    YL, p = at("YAl", [128, 8, TX], F32R, p)
    GT, p = at("GT", [128, 2, 512], F32, p)
    yr = split(YA, YH, YL, F())
    gf = [[], []]
    XX = [(16, 512)]
    for m in range(8):
        (b0, t0), = lin("w_ga", (m,), 8, X, 0, XX, by=by)
        (b1, t1), = lin("w_of", (m,), 8, (YH, YL), 16, XX, yr)
        i = m % 2
        t = AC.op(lambda e: e.activation(GT[:, i, :], psb(b0), ACT.Sigmoid, bias=vec("bgate", m)), t0,
                  gf[i], F())
        give(b0, [t])
        t = DVE.op(lambda e: e.tensor_tensor(M1[:, m, :], GT[:, i, :], psb(b1), ALU.mult), t, t1, F())
        give(b1, [t])
        gf[i] = [t]
    barrier()
    YH, p2 = at("YBh", [128, 8, TX], F32R, P2)
    YL, p2 = at("YBl", [128, 8, TX], F32R, p2)
    GT, p2 = at("GT2", [128, 2, 512], F32, p2)
    MH, _ = at("MXh", [128, 8, TX], F32R, P1 + 8 * TX * 4)
    ML, _ = at("MXl", [128, 8, TX], F32R, p2)
    yr = split(YB, YH, YL, F())
    gf = [[], []]
    for m in range(8):
        (b0, t0), = lin("w_gb", (m,), 8, X, 0, XX, by=by)
        (b1, t1), = lin("w_or", (m,), 8, (YH, YL), 16, XX, yr)
        i = m % 2
        t = AC.op(lambda e: e.activation(GT[:, i, :], psb(b0), ACT.Sigmoid, bias=vec("bgate", 8 + m)), t0,
                  gf[i], F())
        give(b0, [t])
        t = DVE.op(lambda e: e.tensor_tensor(GT[:, i, :], GT[:, i, :], psb(b1), ALU.mult), t, t1)
        give(b1, [t])
        t = DVE.op(lambda e: e.tensor_tensor(M1[:, m, :], M1[:, m, :], GT[:, i, :], ALU.add), t)
        gf[i] = [t]
        t2 = AC.op(lambda e: e.activation(MH[:, m, :], M1[:, m, :], ACT.Copy), t, F(), yr)
        mr = DVE.op(lambda e: e.tensor_tensor(ML[:, m, :], M1[:, m, :], MH[:, m, :].bitcast(F32),
                                              ALU.subtract), t2, F())
    hmix = [(16, 512, [])]
    for m in range(8):
        (b0, t0), = lin("w_out", (m,), 8, (MH, ML), 16, XX, mr)
        t = DVE.op(lambda e: e.tensor_tensor(H[:, m, 16:528], H[:, m, 16:528], psb(b0), ALU.add), t0)
        give(b0, [t])
        hmix[0][2].append(t)
    barrier()
    HH, p = at("H2h", [128, 8, T1], F32R, P1)
    HL, p = at("H2l", [128, 8, T1], F32R, p)
    TM, p = at("TM2", [128, 2, 512], F32, p)
    nb2 = [(16, 256, 0), (272, 256, 0)]
    by = norm_all("rms", nb2, lambda k, c: vec("ffn2", k), None, X, 0, p, hmix, F(), 6)
    e = ffn("f2", X, 0, XX, HH, HL, TM, by, [], lambda m, c0: 0.5, 3)

    h_ready = e + [(528, TC, [t_ctx] * 8)]
    for l in range(2):
        both = l == 0
        if l == 0:
            barrier()
        XH, p = at(f"X2h{l}", [128, 8, 768], F32R, P0)
        XL, p = at(f"X2l{l}", [128, 8, 768], F32R, p)
        P1 = p
        X = (XH, XL)
        mt = mod_until(l, 1)
        blocks = [(16, 256, 0), (272, 256, 0), (528, 256, 1)]
        begin, finish, by = norm_plan("ln", blocks, lambda k, c, l=l: mod(l, 1, k, c),
                                      lambda k, c, l=l: mod(l, 0, k, c), X, 16, p, h_ready, [F(), mt])
        if l == 0:
            begin()
        else:
            before(lead=begin)
        finish(8)
        barrier()

        def prescale():
            c1 = 784 if both else 528
            for k in range(8):
                tt = PL.op(lambda e, k=k: e.tensor_scalar(H[:, k, 16:c1], H[:, k, 16:c1], ALPHA, None,
                                                          ALU.mult), F())
            return tt
        hp = prescale()
        QA, p = at(f"QA{l}", [128, 3, 768], F32, P1)
        KA, p = at(f"KA{l}", [128, 3, 768], F32, p)
        QC, p = at(f"QC{l}", [128, 3, 768], F32, p)
        KC, p = at(f"KC{l}", [128, 1, 768], F32, p)
        VA, p = at(f"VA{l}", [128, 6, 512], F32, p)
        ZU, p = at(f"ZU{l}", [128, 6, 256], F32, p)
        ZV, p = at(f"ZV{l}", [128, 6, 256], F32, p)
        GS, p = at(f"GS{l}", [128, 256], F32, p)
        WS, p = at(f"WS{l}", [128, 4, 128], F32, p)
        BM, p = at(f"BM{l}", [128, 1024], F32, p)
        CS, _ = at(f"CSA{l}", [128, 2, 512], F32, p)
        SQT, _ = at(f"SQA{l}", [128, 2, 512], F32, p + 4096)
        RT, _ = at(f"RTA{l}", [128, 1, 512], F32, p + 8192)
        PP = p
        tl = load(CS[:, :, :], A["rope2"], F())
        tlg = load(GS[:, :], A["gsgu"][l], F())
        tlw = load(WS[:, :, :], A["wst"][l], F())
        tlm = load(BM[:, :], A["wmask"], F())
        full = [(16, 512), (528, 256)]
        lat = [(16, 512)]
        qs = full if both else lat
        sqf = [[], []]
        rfree = [[], []]
        qkr = []
        def proj(dst, nm, m, chs, g, mul):
            res = lin(f"w2_{nm}", (l, m), 8, X, 16, chs, by=by)
            tick()
            base = max(len(jobs) - 2, 0)
            for (c0, n), (b, t) in zip(chs, res):
                o = dst[:, m, c0 - 16:c0 - 16 + n]
                t = AC.op(lambda e: e.activation(o, psb(b, n), ACT.Copy, scale=mul if g is None else 1.0),
                          t, F())
                give(b, [t])
                if g is None:
                    continue
                hold = []

                def one(o=o, n=n, t=t, hold=hold):
                    i = nq[0] % 2
                    nq[0] += 1
                    hold.append(head_rms(o, n, vec(f"{g}{l}"), mul, t, SQT[:, i, :], sqf[i]))

                def two(hold=hold):
                    hold.append(hold[0]())
                    qkr.append(hold[1])

                def three(o=o, n=n, c0=c0, hold=hold):
                    hold.append(rope(o, c0, n, CS, 0, PAX, hold[1], RT, 1))
                j = base if c0 == 16 else base + 1
                at_tick(j, one)
                at_tick(j + 1, two)
                if c0 == 16:
                    at_tick(j + 2, three)
                    at_tick(j + 3, lambda hold=hold: qkr.append(hold[2]()))

        for dst, nm, m, chs, g, mul in (
                (QC, "qc", 0, qs, "gq", 0.125), (QA, "qa", 0, qs, None, 0.125), (KC, "kc", 0, full, "gk", 1.0),
                (QA, "qa", 1, qs, None, 0.125), (QC, "qc", 1, qs, "gq", 0.125), (QA, "qa", 2, qs, None, 0.125),
                (KA, "ka", 0, full, None, 1.0), (QC, "qc", 2, qs, "gq", 0.125), (KA, "ka", 1, full, None, 1.0),
                (KA, "ka", 2, full, None, 1.0)):
            proj(dst, nm, m, chs, g, mul)
        tks = [0, 128, 256, 384, 512, 640]
        zt = tks if both else tks[:4]
        for g in range(2):
            lin_tok("w2_v", l * 2 + g, X, tks, vcopy(VA, g * 256), by=by, shift=16)
            tick()

        def gelu(dst):
            def epi(i, b, t):
                return [AC.op(lambda e: e.activation(dst[:, i, :], psb(b, 256), ACT.Gelu_apprx_tanh), t,
                              F())]
            return epi
        for g, dst in ((0, ZU), (1, ZV)):
            lin_tok("w2_z", l * 2 + g, X, zt, gelu(dst), by=by, shift=16)
            tick()
        flush()
        barrier()
        OT, p = at(f"OT{l}", [128, 6, 1024], F32, P0)
        BR, p = at(f"BR{l}", [128, 2, 1024], F32, p)
        Pb, p = at(f"PbA{l}", [128, 3, 768], F32, p)
        QS, p = at(f"QSA{l}", [128, 2, 768], F32R, p)
        assert p <= P1
        assert p <= P1
        PT, p = at(f"PTA{l}", [128, 2, 768], F32, PP)
        SQ3, p = at(f"SQ3{l}", [128, 384], F32, p)
        KS, p = at(f"KSA{l}", [128, 2, 768], F32R, p)
        KL, p = at(f"KLA{l}", [128, 2, 768], F32R, p)
        AG, ay, aw = SM[:, 48:60], SM[:, 60:66], SM[:, 66:72]
        nz = len(zt)
        zr = {}

        def gate_norm():
            vs = []
            for i in range(nz):
                st = SM[:, 32 + 6 * (i % 2):38 + 6 * (i % 2)]
                v = DVE.op(lambda e: e.bn_stats(st, ZV[:, i, :]), F(), vs[i - 2] if i >= 2 else None)
                vs.append(DVE.op(lambda e: e.bn_aggr(AG[:, 2 * i:2 * i + 2], st), v))
            var = AG.rearrange("p (i c) -> p i c", c=2)[:, 0:nz, 1]
            v = DVE.op(lambda e: e.tensor_scalar(var, var, 1e-6, None, ALU.add), vs[-1])
            zr["v"] = rsqrt(var, ay[:, 0:nz], aw[:, 0:nz], v)

        def gate_scale(i):
            zv = ZV[:, i, :]
            v = DVE.op(lambda e: e.tensor_scalar(zv, zv, AG[:, 2 * i:2 * i + 1], ay[:, i:i + 1],
                                                 ALU.subtract, ALU.mult), zr["v"])
            zr["z", i] = PL.op(lambda e: e.tensor_tensor(zv, zv, GS[:, :], ALU.mult), v, tlg, PL.last())

        def gating(i):
            v = zr["z", i]
            b, bw = take()
            for g in range(4):
                t = PE.op(lambda e: e.matmul(psb2(b, g * 64, g * 64 + 64), WS[:, g, :],
                                             ZV[:, i, g * 64:g * 64 + 64], start=True, stop=True), v, bw, tlw)
            for g in range(4):
                v = DVE.op(lambda e: e.scalar_tensor_tensor(
                    OT[:, i, 384 + g * 64:448 + g * 64], psb2(b, g * 64, g * 64 + 64), vec(f"bs{l}", g),
                    ZU[:, i, g * 64:g * 64 + 64], ALU.add, ALU.mult), t, F())
            give(b, [v])
            zr[i] = v

        nqc = 768 if both else 512
        stacked = {h: [] for h in range(12)}
        used = [[], []]

        def kslot(h):
            return h % 2 if h < 6 else h // 3 % 2

        def stack(h):
            w = [F(), list(used[h % 2])]
            hh, r0 = h % 6, 64 * (h % 2)
            stacked[h] += stack_q((QA if h < 6 else QC)[r0:r0 + 64, hh // 2, 0:nqc], r0, QS[:, h % 2, 0:nqc],
                                  w, eng=DVE if h == 6 else None)
            s = kslot(h)
            if h == 0:
                w.append(list(used[1]))
            if h < 6:
                stacked[h] += stack_k(KA[r0:r0 + 64, hh // 2, :], r0, KS[:, s, :], KL[:, s, :], False, w)
            elif hh % 3 == 0:
                g = hh // 3
                r = 64 * g
                stacked[h] += stack_k(KC[r:r + 64, 0, :], r, KS[:, s, :], KL[:, s, :], True, w, used[0],
                                      used[1])
            else:
                stacked[h] += stacked[h - 1][2:]

        def unit(h, i, vc, k0, k1, col, **more):
            r0, s, ks = 64 * (h % 2), h % 2, kslot(h)
            return {"qk": lambda a, z: (
                        (QS[:, s, i * 128:i * 128 + 128], KS[:, ks, k0 + a:k0 + z]),
                        (QS[r0:r0 + 64, s, i * 128:i * 128 + 128], KL[r0:r0 + 64, ks, k0 + a:k0 + z])),
                    "n": k1 - k0, "used": used[s],
                    "half": vc // 64 % 2,
                    "blocks": [(c, 128, VA[:, (k0 + c) // 128, vc // 128 * 128:vc // 128 * 128 + 128])
                               for c in range(0, k1 - k0, 128)],
                    "ready": [stacked[h]], "vready": [], "out": OT[:, i, col:col + 64], **more}

        br_load = {}

        def bias_load(h):
            br_load[h] = load(BR[:, h % 2, :], A["rpbt"][l, h], F(), DVE.last())

        def bias_add(h):
            br_tok[h] = PL.op(lambda e: e.tensor_tensor(BR[:, h % 2, :], BR[:, h % 2, :], BM[:, :],
                                                        ALU.add), br_load[h], tlm, F(), PL.last())

        seq = [6, 7, 8, 9, 10, 11, 0, 1, 2, 3, 4, 5]
        us = []
        for n, h in enumerate(seq):
            hooks = {}
            if n < 11:
                hooks[1] = [lambda h2=seq[n + 1]: stack(h2)]
            if h < 6:
                hs = [unit(h, i, h * 64, 0, 768, h * 64,
                           bias=BR[:, h % 2, (7 - 2 * i) * 64:(7 - 2 * i) * 64 + 512], bias_ready=h)
                      for i in range(4)]
                if both:
                    hs += [unit(h, i, h * 64, 512, 768, h * 64) for i in (4, 5)]
                if h < 5:
                    hooks[0] = [lambda h=h: bias_load(h + 1)]
                    hooks[3] = [lambda h=h: bias_add(h + 1)]
                if 1 <= h <= 4:
                    for i in range(4):
                        j = 4 * (h - 1) + i
                        if j < 2 * nz:
                            hooks.setdefault(i, []).append(lambda j=j: squares(j // 2, 1 + j % 2))
            else:
                g = (h - 6) // 3
                hs = [unit(h, i, 384 + g * 64, 0 if i < 4 else 512, 768, 640 + (h - 6) * 64)
                      for i in range(nz)]
                if h == 6:
                    hooks[2] = [gate_norm]
                if h in (7, 8):
                    for i in range(nz // 2):
                        j = (h - 7) * (nz // 2) + i
                        hooks.setdefault(i, []).append(lambda j=j: gate_scale(j))
                        hooks.setdefault(i + 1, []).append(lambda j=j: gating(j))
                if h == 11:
                    hooks[3] = [lambda: bias_add(0)]
            if h == 5:
                hooks.setdefault(0, []).append(lambda: group_root(6, 18, last_sq[0]))
                for i in (1, 2, 3):
                    hooks.setdefault(i, []).append(lambda i=i: [
                        group_scale(j, g) for j in range(nz)[2 * i - 2:2 * i] for g in (1, 2)])
            if both and h < 9:
                for i in (4, 5):
                    hooks.setdefault(i, []).append(lambda: mod_step(1))
            for i, fs in hooks.items():
                hs[i]["pre"] = lambda fs=fs: [f() for f in fs]
            us += hs
        GR = ((0, 384), (384, 640), (640, 1024))
        last_sq = [None]

        def squares(i, g):
            a, z = GR[g]
            last_sq[0] = AC.op(lambda e: e.activation(SQ3[:, 0:z - a], OT[:, i, a:z], ACT.Square,
                                                      accum_out=SM[:, 32 + 6 * g + i:33 + 6 * g + i]),
                               F(), last_sq[0], ot_done[0], zr.get(i))

        ss, sw, sy = SM[:, 32:50], SM[:, 50:68], SM[:, 72:90]
        root_t = {}
        scaled = {0: [], 1: [], 2: []}

        def group_root(a, z, v):
            for g in range(a // 6, z // 6):
                x = ss[:, 6 * g:6 * g + nz]
                w = 1.0 / (GR[g][1] - GR[g][0])
                v = DVE.op(lambda e: e.tensor_scalar(x, x, w, 1e-6, ALU.mult, ALU.add), v)
            v = rsqrt(ss[:, a:z], sy[:, a:z], sw[:, a:z], v)
            for g in range(a // 6, z // 6):
                root_t[g] = v

        def group_scale(i, g):
            y, o = sy[:, 6 * g + i:6 * g + i + 1], OT[:, i, GR[g][0]:GR[g][1]]
            if g == 1:
                v = PL.op(lambda e: e.tensor_scalar(o, o, y, None, ALU.mult), root_t[g], PL.last(), zr[i])
            elif g == 0:
                v = DVE.op(lambda e: e.tensor_scalar(o, o, y, None, ALU.mult), root_t[g])
            else:
                v = AC.op(lambda e: e.activation(o, o, ACT.Copy, scale=y), root_t[g])
            scaled[g].append(v)

        ot_done = [None]
        stack(6)
        bias_load(0)
        attention(us, Pb, PT, [6], ot_done)
        barrier()
        for i in range(nz):
            squares(i, 0)
        group_root(0, 6, last_sq[0])
        for i in range(nz):
            group_scale(i, 0)
        OH, p = at(f"OH{l}", [128, 8, 768], F32R, P1)
        OL, p = at(f"OL{l}", [128, 8, 768], F32R, p)

        def to_o(fi, a, n, b, t):
            g = vec(f"gout{l}", fi)
            t = AC.op(lambda e: e.activation(OH[:, fi, a:a + n], psb(b, n), ACT.Copy, scale=g), t, F())
            v = DVE.op(lambda e: e.scalar_tensor_tensor(OL[:, fi, a:a + n], psb(b, n), g,
                                                        OH[:, fi, a:a + n].bitcast(F32), ALU.mult,
                                                        ALU.subtract), t, F())
            orr[-1][2][fi] = v
            return [v]
        orr = []
        for c0, n in qs:
            orr.append((c0, n, [None] * 8))
            for fi in (3, 4, 5, 6, 7, 0, 1, 2):
                to_features(OT, [0, 1, 2, 3] if c0 == 16 else [4, 5], [fi], to_o,
                            scaled[(0, 0, 0, 1, 1, 2, 2, 2)[fi]])
        nb = [(16, 256, 0), (272, 256, 0)] + ([(528, 256, 1)] if both else [])

        mt = mod_until(l, 2)
        hr = [(c0, n, []) for c0, n in qs]
        for m in range(8):
            res = lin("w2_o", (l, m), 8, (OH, OL), 16, qs, by=orr, first=3)
            for (c0, n), (b, t), (_, _, done) in zip(qs, res, hr):
                hk = H[:, m, c0:c0 + n]
                g = mod(l, 2, m, 0 if c0 == 16 else 1)
                t = DVE.op(lambda e: e.scalar_tensor_tensor(hk, psb(b, n), g, hk, ALU.mult, ALU.add), t, hp,
                           mt)
                give(b, [t])
                done.append(t)
        barrier()
        XH, p = at(f"X3h{l}", [128, 8, 768], F32R, P0)
        XL, p = at(f"X3l{l}", [128, 8, 768], F32R, p)
        X = (XH, XL)
        HH, p2 = at(f"H3h{l}", [128, 8, 768], F32R, p)
        HL, p2 = at(f"H3l{l}", [128, 8, 768], F32R, p2)
        TM, p2 = at(f"TM3{l}", [128, 2, 512], F32, p2)
        mt = mod_until(l, 4)
        begin1, finish1, hr = norm_plan("ln", nb, lambda k, c: vec(f"ln1g{l}", k),
                                        lambda k, c: vec(f"ln1b{l}", k), None, 0, p2, hr, F())
        begin2, finish2, by = norm_plan("ln", nb, lambda k, c: mod(l, 4, k, c),
                                        lambda k, c: mod(l, 3, k, c), X, 16, p, hr, [F(), mt])
        begin1()
        finish1(lead=begin2)
        finish2(10)
        barrier()
        hp = prescale()
        mt = mod_until(l, 5)
        e = ffn(f"g{l}", X, 16, qs, HH, HL, TM, by, [hp, mt],
                lambda m, c0: mod(l, 5, m, 0 if c0 == 16 else 1), 3)
        barrier()
        begin, before, h_ready = norm_plan("ln", nb, lambda k, c, l=l: vec(f"ln2g{l}", k),
                                           lambda k, c, l=l: vec(f"ln2b{l}", k), None, 0, p2, e, F())
        begin()
    before()
    s_out = DmaSem(sem("s_out"))
    for c0, n, _ in h_ready:
        for k in range(0, 8, 2):
            t = s_out.add(SP, lambda e: e.dma_start(out[:, k:k + 2, c0 - 16:c0 - 16 + n],
                                                    H[:, k:k + 2, c0:c0 + n]), over(h_ready, c0, n, k + 1))
    SP.op(lambda e: e.wait_ge(*t))

    if dry:
        return
    for q in (PE, DVE, AC, PL, SP):
        q.count()
    with nc.Block() as block:
        block.sync(SP.emit)
        block.gpsimd(PL.emit)
        block.scalar(AC.emit)
        block.tensor(PE.emit)
        block.vector(DVE.emit)


nc_ps = []


def _consts():
    f = np.float32
    cf = np.zeros((128, 5, 128), f)
    cf[:, 0, :] = 1.0 / 1024
    for a in (0, 64):
        cf[a:a + 64, 1, a:a + 64] = 1.0 / 64
    cf[:, 2, :] = np.eye(128)
    q = np.arange(128)
    cf[(q + 64) % 128, 3, q] = 1.0
    cf[q ^ 16, 4, q] = 1.0
    cb = np.zeros((128, 2, 128), np.uint16)
    cb[q, 0, q] = 0x3F80
    cb[:, 1, :] = np.where(q[None, :] > q[:, None], 0xF14A, 0)
    sel = np.zeros((128, 16, 128), np.uint16)
    for h in range(16):
        for a in (0, 32, 64):
            sel[a + h, h, :] = 0x3F80
    half = 64
    inv = (f(10000.0) ** (-(np.arange(half, dtype=f) / f(half)))).astype(f)
    ang = (np.arange(T1, dtype=f)[None, :] * inv[:, None]).astype(f)
    c, s = np.cos(ang.astype(np.float64)), np.sin(ang.astype(np.float64))
    rope1 = np.stack([np.concatenate([c, c]), np.concatenate([-s, s])], 1).astype(f)
    inv = (f(1.0) / (f(10000.0) ** (np.arange(16, dtype=f) / f(16)))).astype(f)
    t = np.arange(512)
    pos = np.stack([t // 64, t % 64]).astype(f)
    d = np.arange(64)
    ang = (pos[d // 32] * inv[d % 16][:, None]).astype(f).astype(np.float64)
    sg = np.where((d % 32) < 16, -1.0, 1.0)[:, None]
    rope2 = np.stack([np.tile(np.cos(ang), (2, 1)), np.tile(np.sin(ang) * sg, (2, 1))], 1).astype(f)
    lg = np.log1p(-np.exp2(-5.0 - np.arange(4)))
    df = (np.arange(T1)[None, :] - np.arange(128)[:, None]).astype(np.float64)
    decay = np.where(df[:, None, :] >= 0, np.exp(lg[None, :, None] * np.maximum(df, 0)[:, None, :]), 0.0)
    decay = (decay * 128.0 ** -0.5).astype(f)
    cc = np.arange(64)
    cs = np.clip(cc - 8, 0, 48)
    ok = (cc[None, :] >= cs[:, None]) & (cc[None, :] < cs[:, None] + 16)
    wm = np.where(ok, 0.0, -1e30).astype(f)
    wmask = np.ascontiguousarray(np.broadcast_to(np.tile(wm, (2, 1))[:, None, :], (128, 16, 64))).reshape(128, 1024)
    return {"cf": cf, "cb": cb, "sel": sel,
            "rope1": rope1, "rope2": rope2, "decay": decay, "wmask": wmask}


def _layout(i):
    def fm(w):
        k, n = w.shape
        return np.ascontiguousarray(w.reshape(k // 128, 128, n // 128, 128).transpose(2, 1, 0, 3)).reshape(
            n // 128, 128, k)

    def tm(w):
        n = w.shape[1]
        return np.ascontiguousarray(w.reshape(2, 4, 128, n // 256, 256).transpose(3, 0, 2, 1, 4)).reshape(
            n // 256, 2, 128, 1024)

    def cols(v):
        return v.reshape(-1, 128).T

    a = _consts()
    x = np.concatenate([i["meta_tokens"], i["x"][0]], 0)
    a["x0"] = np.ascontiguousarray(x.T.reshape(8, 128, T1).transpose(1, 0, 2))
    a["ctx"] = np.ascontiguousarray(i["ctx_2"][0].T.reshape(8, 128, TC).transpose(1, 0, 2))
    w = i["w_in"][0]
    at, parts = 0, {}
    for n, s in (("fq", 1024), ("fk", 1024), ("fv", 1024), ("ff", 16), ("rq", 512), ("rk", 512), ("rv", 1024),
                 ("rg", 1024), ("ga", 1024), ("gb", 1024)):
        parts[n] = w[:, at:at + s]
        at += s
    parts["ff"] = np.pad(parts["ff"], ((0, 0), (0, 112)))
    for n, v in parts.items():
        a["w_" + n] = tm(v) if n in ("fv", "rv") else fm(v)
    a["w_of"], a["w_or"], a["w_out"] = fm(i["w_o_fox"][0]), fm(i["w_o_ret"][0]), fm(i["w_out"][0])
    for t, wi, wo in (("f1", i["w_ffn1_in"][0], i["w_ffn1_out"][0]), ("f2", i["w_ffn2_in"][0], i["w_ffn2_out"][0]),
                      ("g0", i["w_ffn_in_2"][0], i["w_ffn_out_2"][0]),
                      ("g1", i["w_ffn_in_2"][1], i["w_ffn_out_2"][1])):
        a[t + "_in"] = fm(wi)
        for c, (j0, nj) in enumerate(CH):
            a[f"{t}_out{c}"] = fm(wo[j0 * 128:(j0 + nj) * 128])
    a["wmod"] = np.stack([fm(i["w_mod_2"][l]) for l in range(2)])
    names = (("qa", 384), ("ka", 384), ("va", 384), ("z", 512), ("qc", 384), ("kc", 128), ("vc", 128))
    two = {}
    for l in range(2):
        at = 0
        for n, s in names:
            two[n, l] = i["w_in_2"][l][:, at:at + s]
            at += s
    for n in ("qa", "ka", "qc", "kc"):
        a["w2_" + n] = np.stack([fm(two[n, l]) for l in range(2)])
    a["w2_v"] = np.concatenate([tm(np.concatenate([two["va", l], two["vc", l]], 1)) for l in range(2)])
    a["w2_z"] = np.concatenate([tm(two["z", l]) for l in range(2)])
    a["w2_o"] = np.stack([fm(i["w_o_2"][l]) for l in range(2)])
    a["wst"] = np.ascontiguousarray(i["w_s_2"].transpose(0, 3, 1, 2))
    a["gsgu"] = np.ascontiguousarray(np.broadcast_to(i["g_sgu_2"][:, None, :], (2, 128, 256)))
    q = np.arange(128)[:, None, None]
    j = np.arange(16)[None, :, None]
    kc = np.arange(64)[None, None, :]
    dr = np.clip(j - q // 64, 0, 14)
    dc = np.clip(kc - q % 64 + 15, 0, 30)
    a["rpbt"] = np.ascontiguousarray(i["rpb_2"][:, :, dr, dc]).reshape(2, 6, 128, 1024)
    v = np.zeros((128, NVEC), np.float32)

    def put(name, arr):
        s, n = VEC[name]
        v[:, s:s + n] = arr
    put("ffn1", cols(i["norm_ffn1"][0]))
    put("mix", cols(i["norm_mix"][0]))
    put("ffn2", cols(i["norm_ffn2"][0]))
    put("bgate", cols(i["b_gate"][0]))
    put("retgn", cols(i["ret_gn"][0]))
    put("fq", np.tile(i["fox_q_norm"][0], 2)[:, None])
    put("fk", np.tile(i["fox_k_norm"][0], 2)[:, None])
    put("bf", np.pad(i["b_forget"][0], (0, 112))[:, None])
    put("c", np.stack([cols(i["c_2"][0]), cols(i["c_ctx_2"])], 2).reshape(128, 16))
    for l in range(2):
        put(f"bmod{l}", cols(i["b_mod_2"][l]))
        put(f"gq{l}", np.tile(i["g_q_2"][l], 2)[:, None])
        put(f"gk{l}", np.tile(i["g_k_2"][l], 2)[:, None])
        put(f"gout{l}", cols(i["g_out_2"][l]))
        for n in ("ln1_g", "ln1_b", "ln2_g", "ln2_b"):
            put(n.replace("_", "") + str(l), cols(i[n + "_2"][l]))
        put(f"bs{l}", i["b_s_2"][l].T)
    a["vec"] = v
    return a


def kernel(**inputs):
    import concourse.bacc as bacc
    from concourse.bass_utils import run_bass_kernel_spmd
    arrays = {"in_" + k: np.ascontiguousarray(v)
              for k, v in _layout({k: np.asarray(v) for k, v in inputs.items()}).items()}
    nc = bacc.Bacc("TRN2", target_bir_lowering=False, num_devices=1)
    A = {k[3:]: nc.dram_tensor(k, v.shape, mybir.dt.from_np(v.dtype), kind="ExternalInput").ap()
         for k, v in arrays.items()}
    out = nc.dram_tensor("out", (128, 8, TX), F32, kind="ExternalOutput").ap()
    nc_ps.clear()
    build(nc, A, out)
    r = run_bass_kernel_spmd(nc, [arrays], core_ids=[0])
    o = r.results[0]["out"]
    return np.ascontiguousarray(o.transpose(2, 1, 0)).reshape(1, TX, D)
```
